# Optimizing a Trainium2 kernel written in Bass

```python
import jax, jax.numpy as jnp
from jax import lax
import numpy as np

D_MODEL = 1024
BATCH = 1
SEQ = 512
DEPTH = 1

CHUNK = 64
EPS = 1e-6

A_HEADS = 8
A_HEAD_DIM = 64
A_WIDTH = A_HEADS * A_HEAD_DIM
A_LEFT_CHUNKS = 8
A_MAX_REL = 128

B_HEADS = 8
B_KEY_DIM = 64
B_VAL_DIM = 64
B_KWIDTH = B_HEADS * B_KEY_DIM
B_VWIDTH = B_HEADS * B_VAL_DIM

C_HEADS = 8
C_Q_RANK = 256
C_KV_RANK = 128
C_NOPE = 64
C_ROPE = 32
C_V = 64
C_WIDTH = C_HEADS * C_V
C_QBLOCK = 128
ROPE_BASE = 10000.0

N_BRANCH = 3
BRANCH_WIDTH = 512
D_FF = 4 * D_MODEL

IN_SPLIT_SIZES = (A_WIDTH, A_WIDTH, A_WIDTH,
                  B_KWIDTH, B_KWIDTH, B_VWIDTH, B_VWIDTH,
                  C_Q_RANK, C_KV_RANK, C_ROPE,
                  N_BRANCH * D_MODEL)
IN_COLS = sum(IN_SPLIT_SIZES)


def rmsnorm(x, g):
    x32 = x.astype(jnp.float32)
    y = x32 * lax.rsqrt(jnp.mean(jnp.square(x32), axis=-1, keepdims=True) + EPS)
    return (y * g.astype(jnp.float32)).astype(x.dtype)

def rope(x, cos, sin):
    x1, x2 = jnp.split(x.astype(jnp.float32), 2, axis=-1)
    return jnp.concatenate([x1 * cos - x2 * sin, x2 * cos + x1 * sin], axis=-1).astype(x.dtype)

def chunked_relpos_attention(q, k, v, rel_table):
    bsz, seq, heads, dh = q.shape
    n_chunks = seq // CHUNK
    pad = A_LEFT_CHUNKS * CHUNK
    band = pad + CHUNK
    k_pad = jnp.pad(k, ((0, 0), (pad, 0), (0, 0), (0, 0)))
    v_pad = jnp.pad(v, ((0, 0), (pad, 0), (0, 0), (0, 0)))
    qi = jnp.arange(CHUNK)[:, None]
    kj = jnp.arange(band)[None, :]
    rel = jnp.clip(qi + pad - kj, -A_MAX_REL, A_MAX_REL) + A_MAX_REL
    bias = rel_table.astype(jnp.float32)[:, rel]
    q_chunks = q.reshape(bsz, n_chunks, CHUNK, heads, dh).transpose(1, 0, 2, 3, 4)
    scale = dh ** -0.5

    def one_chunk(args):
        c, q_blk = args
        k_band = lax.dynamic_slice_in_dim(k_pad, c * CHUNK, band, axis=1)
        v_band = lax.dynamic_slice_in_dim(v_pad, c * CHUNK, band, axis=1)
        s = jnp.einsum('bqhd,bkhd->bhqk', q_blk, k_band).astype(jnp.float32) * scale + bias
        valid = kj >= pad - c * CHUNK
        s = jnp.where(valid[None, None], s, -jnp.inf)
        p = jax.nn.softmax(s, axis=-1).astype(v.dtype)
        return jnp.einsum('bhqk,bkhd->bqhd', p, v_band)

    out = lax.map(one_chunk, (jnp.arange(n_chunks), q_chunks))
    return out.transpose(1, 0, 2, 3, 4).reshape(bsz, seq, heads * dh)

def hgrn2_recurrence(q, f_logit, i_val, g, lower_bound, norm_g):
    bsz, seq, _ = q.shape
    n_chunks = seq // CHUNK
    f32 = jnp.float32

    def to_chunks(t, d):
        return t.astype(f32).reshape(bsz, n_chunks, CHUNK, B_HEADS, d).transpose(1, 0, 3, 2, 4)

    z = to_chunks(f_logit, B_KEY_DIM)
    lb = lower_bound.reshape(1, B_HEADS, 1, B_KEY_DIM)
    log_f = jnp.logaddexp(jnp.log(lb), jnp.log1p(-lb) + jax.nn.log_sigmoid(z))
    k = (1.0 - lb) * jax.nn.sigmoid(-z)
    qc = jax.nn.silu(to_chunks(q, B_KEY_DIM))
    vc = to_chunks(i_val, B_VAL_DIM)
    causal = jnp.tril(jnp.ones((CHUNK, CHUNK), dtype=bool))[None, None, :, :, None]

    def step(state, blk):
        q_b, k_b, lf_b, v_b = blk
        cum = jnp.cumsum(lf_b, axis=2)
        diff = cum[:, :, :, None, :] - cum[:, :, None, :, :]
        decay = jnp.exp(jnp.where(causal, diff, -jnp.inf))
        scores = jnp.einsum('bhid,bhjd,bhijd->bhij', q_b, k_b, decay)
        o = (jnp.einsum('bhij,bhjv->bhiv', scores, v_b)
             + jnp.einsum('bhid,bhdv->bhiv', q_b * jnp.exp(cum), state))
        last = cum[:, :, -1:, :]
        state = (jnp.exp(last[:, :, 0, :])[..., None] * state
                 + jnp.einsum('bhjd,bhjv->bhdv', k_b * jnp.exp(last - cum), v_b))
        return state, o

    s0 = jnp.zeros((bsz, B_HEADS, B_KEY_DIM, B_VAL_DIM), f32)
    _, o = lax.scan(step, s0, (qc, k, log_f, vc))
    o = o.transpose(1, 0, 3, 2, 4).reshape(bsz, seq, B_HEADS, B_VAL_DIM)
    o = rmsnorm(o, norm_g) * jax.nn.silu(g.astype(f32).reshape(bsz, seq, B_HEADS, B_VAL_DIM))
    return o.reshape(bsz, seq, B_VWIDTH).astype(q.dtype)

def mla_attention(c_q, c_kv, k_rope_raw, positions, q_norm_g, kv_norm_g, w_uq, w_ukv):
    bsz, seq, _ = c_q.shape
    q = (rmsnorm(c_q, q_norm_g) @ w_uq).reshape(bsz, seq, C_HEADS, C_NOPE + C_ROPE)
    kv = (rmsnorm(c_kv, kv_norm_g) @ w_ukv).reshape(bsz, seq, C_HEADS, C_NOPE + C_V)
    q_nope, q_rope = q[..., :C_NOPE], q[..., C_NOPE:]
    k_nope, v = kv[..., :C_NOPE], kv[..., C_NOPE:]
    inv_freq = ROPE_BASE ** (-jnp.arange(0, C_ROPE, 2, dtype=jnp.float32) / C_ROPE)
    ang = positions.astype(jnp.float32)[..., None] * inv_freq
    cos, sin = jnp.cos(ang)[:, :, None, :], jnp.sin(ang)[:, :, None, :]
    q_rope = rope(q_rope, cos, sin)
    k_rope = rope(k_rope_raw[:, :, None, :], cos, sin)[:, :, 0, :]
    n_blocks = seq // C_QBLOCK

    def blocks(t):
        return t.reshape(bsz, n_blocks, C_QBLOCK, C_HEADS, t.shape[-1]).transpose(1, 0, 2, 3, 4)

    key_chunk = jnp.arange(seq) // CHUNK
    scale = (C_NOPE + C_ROPE) ** -0.5

    def one_block(args):
        blk, qn, qr = args
        s = (jnp.einsum('bqhd,bkhd->bhqk', qn, k_nope)
             + jnp.einsum('bqhr,bkr->bhqk', qr, k_rope)).astype(jnp.float32) * scale
        q_chunk = (blk * C_QBLOCK + jnp.arange(C_QBLOCK)) // CHUNK
        mask = key_chunk[None, :] <= q_chunk[:, None]
        s = jnp.where(mask[None, None], s, -jnp.inf)
        p = jax.nn.softmax(s, axis=-1).astype(v.dtype)
        return jnp.einsum('bhqk,bkhd->bqhd', p, v)

    out = lax.map(one_block, (jnp.arange(n_blocks), blocks(q_nope), blocks(q_rope)))
    return out.transpose(1, 0, 2, 3, 4).reshape(bsz, seq, C_WIDTH)

def first_inputs(seed: int = 0) -> dict:
    key = jax.random.key(seed)
    ks = jax.random.split(key, 20)
    f32 = jnp.float32

    def nrm(k, shape, fan_in):
        return jax.random.normal(k, shape, f32) * (fan_in ** -0.5)

    def gain(k, shape):
        return 1.0 + 0.05 * jax.random.normal(k, shape, f32)

    x = jax.random.normal(ks[0], (BATCH, SEQ, D_MODEL), f32)
    offset = jax.random.randint(ks[1], (BATCH, 1), 0, 4096, dtype=jnp.int32)
    positions = offset + jnp.arange(SEQ, dtype=jnp.int32)[None, :]
    return {
        'x': x,
        'positions': positions,
        'norm_mix_g': gain(ks[2], (DEPTH, D_MODEL)),
        'w_in': nrm(ks[3], (DEPTH, D_MODEL, IN_COLS), D_MODEL),
        'rel_bias': 0.2 * jax.random.normal(ks[4], (DEPTH, A_HEADS, 2 * A_MAX_REL + 1), f32),
        'hgrn_lb_logits': jax.random.normal(ks[5], (DEPTH, B_KWIDTH), f32),
        'hgrn_norm_g': gain(ks[6], (DEPTH, B_VAL_DIM)),
        'mla_q_norm_g': gain(ks[7], (DEPTH, C_Q_RANK)),
        'mla_kv_norm_g': gain(ks[8], (DEPTH, C_KV_RANK)),
        'mla_w_uq': nrm(ks[9], (DEPTH, C_Q_RANK, C_HEADS * (C_NOPE + C_ROPE)), C_Q_RANK),
        'mla_w_ukv': nrm(ks[10], (DEPTH, C_KV_RANK, C_HEADS * (C_NOPE + C_V)), C_KV_RANK),
        'w_branch': nrm(ks[11], (DEPTH, N_BRANCH, BRANCH_WIDTH, D_MODEL), BRANCH_WIDTH),
        'w_out': nrm(ks[12], (DEPTH, D_MODEL, D_MODEL), D_MODEL),
        'norm_ffn_g': gain(ks[13], (DEPTH, D_MODEL)),
        'w_ff1': nrm(ks[14], (DEPTH, D_MODEL, D_FF), D_MODEL),
        'w_ff2': nrm(ks[15], (DEPTH, D_FF, D_MODEL), D_FF),
        'final_norm_g': gain(ks[16], (D_MODEL,)),
    }

def first_block(x, positions, norm_mix_g, w_in, rel_bias, hgrn_lb_logits, hgrn_norm_g,
              mla_q_norm_g, mla_kv_norm_g, mla_w_uq, mla_w_ukv, w_branch, w_out,
              norm_ffn_g, w_ff1, w_ff2, final_norm_g):
    bsz, seq, _ = x.shape
    p_lb = jax.nn.softmax(hgrn_lb_logits.astype(jnp.float32), axis=0)
    lb_all = jnp.cumsum(p_lb, axis=0)
    lb_all = lb_all - lb_all[0:1]

    for l in range(DEPTH):
        h = rmsnorm(x, norm_mix_g[l])
        proj = h @ w_in[l]
        parts = []
        start = 0
        for size in IN_SPLIT_SIZES:
            parts.append(proj[..., start:start + size])
            start += size
        a_q, a_k, a_v, b_q, b_f, b_i, b_g, c_q, c_kv, c_kr, gate_logits = parts

        y_a = chunked_relpos_attention(
            a_q.reshape(bsz, seq, A_HEADS, A_HEAD_DIM),
            a_k.reshape(bsz, seq, A_HEADS, A_HEAD_DIM),
            a_v.reshape(bsz, seq, A_HEADS, A_HEAD_DIM),
            rel_bias[l])
        y_b = hgrn2_recurrence(b_q, b_f, b_i, b_g, lb_all[l], hgrn_norm_g[l])
        y_c = mla_attention(c_q, c_kv, c_kr, positions, mla_q_norm_g[l], mla_kv_norm_g[l],
                            mla_w_uq[l], mla_w_ukv[l])

        branches = jnp.stack([y_a.astype(h.dtype), y_b.astype(h.dtype), y_c.astype(h.dtype)], axis=2)
        up = jnp.einsum('bsnw,nwd->bsnd', branches, w_branch[l])
        gates = jax.nn.sigmoid(gate_logits.reshape(bsz, seq, N_BRANCH, D_MODEL))
        merged = jnp.sum(gates * up, axis=2)
        x = x + merged @ w_out[l]

        h2 = rmsnorm(x, norm_ffn_g[l])
        x = x + jnp.square(jax.nn.relu(h2 @ w_ff1[l])) @ w_ff2[l]

    return rmsnorm(x, final_norm_g)


DEPTH_2 = 2

HEAD_DIM = 64
N_FOX_HEADS = D_MODEL // (2 * HEAD_DIM)
N_RET_HEADS = D_MODEL // (2 * HEAD_DIM)
FOX_WIDTH = N_FOX_HEADS * HEAD_DIM
RET_WIDTH = N_RET_HEADS * HEAD_DIM
MIX_WIDTH = FOX_WIDTH + RET_WIDTH
D_FF_2 = -(-8 * D_MODEL // (3 * 128)) * 128
CONV_WIDTH = 3
PLE_DIM = 256
Q_BLOCK = 128
RET_CHUNK = 128
NORM_EPS = 1e-6
GN_EPS = 1e-5
IN_SIZES = (FOX_WIDTH, FOX_WIDTH, FOX_WIDTH, N_FOX_HEADS, RET_WIDTH, RET_WIDTH, RET_WIDTH, RET_WIDTH)
IN_WIDTH = sum(IN_SIZES)
SPLIT_POINTS = tuple(int(v) for v in np.cumsum(IN_SIZES)[:-1])


def rms_norm(x, w):
    xf = x.astype(jnp.float32)
    y = xf * lax.rsqrt(jnp.mean(xf * xf, axis=-1, keepdims=True) + NORM_EPS)
    return (y * w.astype(jnp.float32)).astype(x.dtype)

def split_heads(t, n_heads):
    b, s, _ = t.shape
    return t.reshape(b, s, n_heads, HEAD_DIM)

def rotary_tables(seq):
    inv_freq = ROPE_BASE ** (-jnp.arange(0, HEAD_DIM, 2, dtype=jnp.float32) / HEAD_DIM)
    ang = jnp.arange(seq, dtype=jnp.float32)[:, None] * inv_freq[None, :]
    return jnp.cos(ang), jnp.sin(ang)

def apply_rotary(t, cos, sin):
    half = HEAD_DIM // 2
    t1, t2 = t[..., :half], t[..., half:]
    c = cos[None, :, None, :]
    s = sin[None, :, None, :]
    return jnp.concatenate([t1 * c - t2 * s, t1 * s + t2 * c], axis=-1).astype(t.dtype)

def forgetting_attention(q, k, v, f_logit):
    b, s, h, d = q.shape
    q = q.transpose(0, 2, 1, 3)
    k = k.transpose(0, 2, 1, 3)
    v = v.transpose(0, 2, 1, 3)
    log_f = jax.nn.log_sigmoid(f_logit.astype(jnp.float32))
    cum = jnp.cumsum(log_f, axis=1).transpose(0, 2, 1)
    scale = HEAD_DIM ** -0.5
    kpos = jnp.arange(s)
    n_blocks = s // Q_BLOCK

    def one_block(bi):
        start = bi * Q_BLOCK
        qb = lax.dynamic_slice_in_dim(q, start, Q_BLOCK, axis=2)
        cq = lax.dynamic_slice_in_dim(cum, start, Q_BLOCK, axis=2)
        logits = jnp.einsum('bhqd,bhkd->bhqk', qb, k).astype(jnp.float32) * scale
        logits = logits + cq[..., :, None] - cum[..., None, :]
        qpos = start + jnp.arange(Q_BLOCK)
        logits = jnp.where(kpos[None, :] <= qpos[:, None], logits, -jnp.inf)
        probs = jax.nn.softmax(logits, axis=-1)
        return jnp.einsum('bhqk,bhkd->bhqd', probs.astype(v.dtype), v)

    out = lax.map(one_block, jnp.arange(n_blocks))
    return out.transpose(1, 0, 3, 2, 4).reshape(b, s, h * d)

def chunkwise_retention(q, k, v, log_gamma):
    b, s, h, d = q.shape
    n_chunks = s // RET_CHUNK

    def to_chunks(t):
        return t.reshape(b, n_chunks, RET_CHUNK, h, d).transpose(1, 0, 3, 2, 4)

    idx = jnp.arange(RET_CHUNK, dtype=jnp.float32)
    rel = idx[:, None] - idx[None, :]
    lg = log_gamma[:, None, None]
    intra_decay = jnp.where(rel >= 0, jnp.exp(lg * jnp.maximum(rel, 0.0)), 0.0)
    q_decay = jnp.exp(log_gamma[:, None] * (idx + 1.0))
    k_decay = jnp.exp(log_gamma[:, None] * (RET_CHUNK - 1.0 - idx))
    chunk_decay = jnp.exp(log_gamma * RET_CHUNK)

    def step(state, qkv):
        qc, kc, vc = qkv
        scores = jnp.einsum('bhid,bhjd->bhij', qc, kc) * intra_decay
        inner = jnp.einsum('bhij,bhje->bhie', scores, vc)
        cross = jnp.einsum('bhid,bhde->bhie', qc, state) * q_decay[:, :, None]
        new_state = state * chunk_decay[:, None, None] + jnp.einsum(
            'bhjd,bhje->bhde', kc * k_decay[:, :, None], vc)
        return new_state, inner + cross

    state0 = jnp.zeros((b, h, d, d), jnp.float32)
    _, out = lax.scan(step, state0, (to_chunks(q), to_chunks(k), to_chunks(v)))
    return out.transpose(1, 0, 3, 2, 4).reshape(b, s, h, d)

def head_group_norm(y):
    yf = y.astype(jnp.float32)
    mu = jnp.mean(yf, axis=-1, keepdims=True)
    var = jnp.mean(jnp.square(yf - mu), axis=-1, keepdims=True)
    return (yf - mu) * lax.rsqrt(var + GN_EPS)

def causal_depthwise_conv(a, w, bias):
    s = a.shape[1]
    ap = jnp.pad(a, ((0, 0), (CONV_WIDTH - 1, 0), (0, 0)))
    y = bias
    for j in range(CONV_WIDTH):
        y = y + ap[:, j:j + s, :] * w[j]
    return y

def gated_conv_ffn(u, w_up, conv_w, conv_b, w_down):
    up = u @ w_up
    a, g = up[..., :D_FF_2], up[..., D_FF_2:]
    a = causal_depthwise_conv(a, conv_w, conv_b)
    return (jax.nn.gelu(a, approximate=False) * g) @ w_down

def second_inputs(seed: int = 0) -> dict:
    key = jax.random.key(seed)
    ks = jax.random.split(key, 16)
    nrm = jax.random.normal
    f32 = jnp.float32
    return {
        'x': nrm(ks[0], (BATCH, SEQ, D_MODEL), f32),
        'p': nrm(ks[1], (DEPTH_2, BATCH, SEQ, PLE_DIM), f32),
        'attn_norm_w': 1.0 + 0.05 * nrm(ks[2], (DEPTH_2, D_MODEL), f32),
        'w_in': nrm(ks[3], (DEPTH_2, D_MODEL, IN_WIDTH), f32) * D_MODEL ** -0.5,
        'forget_bias': 2.0 + 0.1 * nrm(ks[4], (DEPTH_2, N_FOX_HEADS), f32),
        'w_out': nrm(ks[5], (DEPTH_2, MIX_WIDTH, D_MODEL), f32) * MIX_WIDTH ** -0.5,
        'ffn_norm_w': 1.0 + 0.05 * nrm(ks[6], (DEPTH_2, D_MODEL), f32),
        'w_up': nrm(ks[7], (DEPTH_2, D_MODEL, 2 * D_FF_2), f32) * D_MODEL ** -0.5,
        'conv_w': nrm(ks[8], (DEPTH_2, CONV_WIDTH, D_FF_2), f32) * CONV_WIDTH ** -0.5,
        'conv_b': 0.01 * nrm(ks[9], (DEPTH_2, D_FF_2), f32),
        'w_down': nrm(ks[10], (DEPTH_2, D_FF_2, D_MODEL), f32) * D_FF_2 ** -0.5,
        'ple_norm_w': 1.0 + 0.05 * nrm(ks[11], (DEPTH_2, D_MODEL), f32),
        'w_ple_gate': nrm(ks[12], (DEPTH_2, D_MODEL, D_MODEL), f32) * D_MODEL ** -0.5,
        'w_ple_proj': nrm(ks[13], (DEPTH_2, PLE_DIM, D_MODEL), f32) * PLE_DIM ** -0.5,
        'final_norm_w': 1.0 + 0.05 * nrm(ks[14], (D_MODEL,), f32),
    }

def second_block(x, p, attn_norm_w, w_in, forget_bias, w_out, ffn_norm_w, w_up, conv_w, conv_b,
              w_down, ple_norm_w, w_ple_gate, w_ple_proj, final_norm_w):
    seq = x.shape[1]
    cos, sin = rotary_tables(seq)
    log_gamma = jnp.log1p(-jnp.exp2(-5.0 - jnp.arange(N_RET_HEADS, dtype=jnp.float32)))
    h = x
    for i in range(DEPTH_2):
        u = rms_norm(h, attn_norm_w[i])
        proj = u @ w_in[i]
        fq, fk, fv, f_logit, rq, rk, rv, rg = jnp.split(proj, SPLIT_POINTS, axis=-1)
        fox = forgetting_attention(split_heads(fq, N_FOX_HEADS), split_heads(fk, N_FOX_HEADS),
                                   split_heads(fv, N_FOX_HEADS), f_logit + forget_bias[i])
        rq_h = apply_rotary(split_heads(rq, N_RET_HEADS), cos, sin)
        rk_h = apply_rotary(split_heads(rk, N_RET_HEADS), cos, sin) * (HEAD_DIM ** -0.5)
        ret = chunkwise_retention(rq_h, rk_h, split_heads(rv, N_RET_HEADS), log_gamma)
        ret = head_group_norm(ret).reshape(ret.shape[0], seq, RET_WIDTH)
        ret = (jax.nn.silu(rg.astype(jnp.float32)) * ret).astype(x.dtype)
        mixed = jnp.concatenate([fox.astype(x.dtype), ret], axis=-1)
        h = h + mixed @ w_out[i]
        h = h + gated_conv_ffn(rms_norm(h, ffn_norm_w[i]), w_up[i], conv_w[i], conv_b[i], w_down[i])
        gate = jax.nn.sigmoid(rms_norm(h, ple_norm_w[i]) @ w_ple_gate[i])
        h = h + gate * (p[i] @ w_ple_proj[i])
    return rms_norm(h, final_norm_w)


def setup_inputs(seed=0):
    out = dict(first_inputs(seed))
    for name, value in second_inputs(seed + 1).items():
        if name != "x":
            out[name + "_2"] = value
    return out


def reference(
    x, positions, norm_mix_g, w_in, rel_bias, hgrn_lb_logits, hgrn_norm_g, mla_q_norm_g,
    mla_kv_norm_g, mla_w_uq, mla_w_ukv, w_branch, w_out, norm_ffn_g, w_ff1, w_ff2, final_norm_g,
    p_2, attn_norm_w_2, w_in_2, forget_bias_2, w_out_2, ffn_norm_w_2, w_up_2, conv_w_2,
    conv_b_2, w_down_2, ple_norm_w_2, w_ple_gate_2, w_ple_proj_2, final_norm_w_2,
):
    x = first_block(
        x, positions, norm_mix_g, w_in, rel_bias, hgrn_lb_logits, hgrn_norm_g, mla_q_norm_g,
        mla_kv_norm_g, mla_w_uq, mla_w_ukv, w_branch, w_out, norm_ffn_g, w_ff1, w_ff2,
        final_norm_g,
    )
    return second_block(
        x, p_2, attn_norm_w_2, w_in_2, forget_bias_2, w_out_2, ffn_norm_w_2, w_up_2, conv_w_2,
        conv_b_2, w_down_2, ple_norm_w_2, w_ple_gate_2, w_ple_proj_2, final_norm_w_2,
    )


_drawn_inputs = setup_inputs


def setup_inputs(seed=0):
    import zlib

    import numpy as np

    out = dict(_drawn_inputs(seed))
    spreads = {}
    factors = {'rel_bias': 8.766,
     'mla_q_norm_g': 7.885,
     'mla_kv_norm_g': 6.112,
     'forget_bias_2': 25.696,
     'conv_b_2': 8.0,
     'ple_norm_w_2': 5.489,
     'hgrn_norm_g': 6.527}
    for name, (base, spread) in spreads.items():
        noise = np.random.default_rng([zlib.crc32(name.encode()), seed]).standard_normal(out[name].shape)
        drawn = base * np.exp(spread * noise) if base else spread * noise
        out[name] = __import__('jax').numpy.asarray(drawn.astype(out[name].dtype))
    for name, factor in factors.items():
        out[name] = (out[name] * factor).astype(out[name].dtype)
    return out
```

```python
import numpy as np

import concourse.bass as bass
from concourse import mybir

F32 = mybir.dt.float32
F32R = mybir.dt.float32r
U32 = mybir.dt.uint32
I32 = mybir.dt.int32
ALU = mybir.AluOpType
ACT = mybir.ActivationFunctionType
AX = mybir.AxisListType

P = 128
T = 512
D = 1024
KD = D // P
TT = T // P
HEADS = 8
PAIRS = HEADS // 2
HD = 64
CHUNK = 64
EPS = 1e-6
GN_EPS = 1e-5
LAYERS = 2
FF1 = 4 * D
FF2 = -(-8 * D // (3 * 128)) * 128
FT2 = FF2 // P
CHUNKS2 = (8, 8, FT2 - 16)
A_REL = 128
QR, KVR, NOPE, ROPE = 256, 128, 64, 32
QH = NOPE + ROPE
MASKED = -1.0e30
LEVELS = (0, 256, 128, 64, 32, 16, 8, 4, 2, 1)
LOOK = 2

N_AQK, N_AV, N_BQFG, N_BV, N_C, N_UP, N_MERGE, N_O, N_FF = 0, 8, 12, 24, 28, 32, 36, 84, 92
N_BLOCK1 = N_FF + 64
O_FL, O_FQK, O_FV, O_RQK, O_RG, O_RV, O_O = 0, 1, 9, 13, 21, 25, 29
O_FFN = (37, 61, 85)
O_GATE, O_PLE = 105, 113
PER_LAYER = 116
N_PANELS = N_BLOCK1 + LAYERS * PER_LAYER
SEGMENTS1 = ["in1", "c_q", "c_kv"]
SEGMENTS2 = ["in2", "ffn_wide", "ffn_narrow", "ple_gate", "ple_a", "ple_b"]

CONSTS = ["ident", "anti", "ones", "head_mean", "chunk_mask", "causal_mask", "rope_c", "rope_r"]
N_MASKS = 7
PARAMS = {}
for _name, _n in [("one", 1), ("eps", 1), ("gn_eps", 1), ("inv_freq", 1), ("mix_g", KD), ("ffn_g", KD), ("q_g", 2), ("kv_g", 1),
                  ("hgrn_g", 1), ("lb", PAIRS), ("mid_g", KD), ("final_g", KD), ("attn_w", LAYERS * KD), ("ffn_w", LAYERS * KD),
                  ("ple_w", LAYERS * KD), ("f_bias", LAYERS), ("conv_b", LAYERS * FT2), ("conv_w", LAYERS * FT2 * 3)]:
    PARAMS[_name] = (sum(n for _, n in PARAMS.values()), _n)
N_PARAMS = sum(n for _, n in PARAMS.values())


def build(nc, dram, out):
    offset = {}

    def sb(name, shape, dt=F32):
        offset[name] = nc.sbuf_base
        return nc.alloc_sbuf_tensor(name, shape, dt)

    def alias(name, base, shape, dt=F32, skip=0):
        return nc.alloc_sbuf_tensor_at(name, shape, dt, offset=offset[base] + skip)

    x = sb("x", [P, KD, T])
    act_hi = sb("act_hi", [P, KD, T], F32R)
    act_lo = sb("act_lo", [P, KD, T], F32R)
    raw = sb("raw", [P, 2, 1024])
    w_hi = sb("w_hi", [P, 4, 1024], F32R)
    w_lo = sb("w_lo", [P, 4, 1024], F32R)
    y_hi = sb("y_hi", [P, 12, T], F32R)
    y_lo = sb("y_lo", [P, 12, T], F32R)
    wa = sb("wa", [P, 8, T])
    wb = sb("wb", [P, 8, T])
    wv = sb("wv", [P, TT, T])
    qcur = sb("qcur", [P, 2, T])
    kcur = sb("kcur", [P, 2, T])
    vcur = sb("vcur", [P, TT, P])
    probs = sb("probs", [P, 2, T])
    probs_t = sb("probs_t", [P, 2, T])
    tab = sb("tab", [P, 2, T])
    consts = sb("consts", [P, len(CONSTS), P])
    masks = sb("masks", [P, N_MASKS, P])
    params = sb("params", [P, N_PARAMS])
    cols = sb("cols", [P, 16])
    c = {n: consts[:, i, :] for i, n in enumerate(CONSTS)}
    neg_max = [cols[:, 0:1], cols[:, 1:2]]
    prob_sum = [cols[:, 2:3], cols[:, 3:4]]
    inv_sum = [cols[:, 8:9], cols[:, 9:10]]
    lower, rest = cols[:, 4:8], cols[:, 10:14]
    merged_hi = alias("merged_hi", "wa", [P, KD, T], F32R)
    merged_lo = alias("merged_lo", "wb", [P, KD, T], F32R)
    positions = alias("positions", "vcur", [P, T], I32)
    tail = 8 * T * 4
    decay_tmp = alias("decay_tmp", "y_hi", [P, 4, T], skip=tail)
    s_diag = alias("s_diag", "y_hi", [P, 2, TT, P], skip=tail)
    s_256 = alias("s_256", "y_hi", [P, 2, 2, 256], skip=tail + 2 * T * 4)
    s_128 = alias("s_128", "y_lo", [P, 2, 2, P], skip=tail)
    cums = alias("cums", "y_lo", [P, 3, T], skip=tail + T * 4)
    resets = alias("resets", "probs", [P, 3, T])
    s_ret = [alias("s_ret0", "y_hi", [P, 1280], skip=tail), alias("s_ret1", "y_lo", [P, 1280], skip=tail)]
    s_off = (0, 512, 896, 1152)
    augq, augk = wb[0:2, 0:2, :], wb[0:2, 2:4, :]
    padded = alias("padded", "tab", [P, T + 2])

    acc = nc.alloc_psum_tensor("acc", [P, 4, T], F32)
    sc = nc.alloc_psum_tensor("sc", [P, 2, T], F32)
    po = nc.alloc_psum_tensor("po", [P, T], F32)
    pt = nc.alloc_psum_tensor("pt", [P, T], F32)
    lev_bank = [sc[:, 0, :], sc[:, 1, :], acc[:, 0, :], acc[:, 1, :]]
    cum_dram = nc.dram_tensor("cum_dram", (2, HEADS, T), F32).ap()

    def par(name, i=0, rows=P):
        first = PARAMS[name][0]
        if isinstance(i, int):
            return params[0:rows, first + i:first + i + 1]
        return params[0:rows, bass.ds(i + first, 1)]

    sems, starts = {}, {}

    def S(name, start=0):
        if name not in sems:
            sems[name] = nc.alloc_semaphore(name)
            if start:
                starts[name] = start
        assert starts.get(name, 0) == start, name
        return sems[name]

    started = S("started")
    passed = S("passed")
    raw_loaded = [S("raw_loaded0"), S("raw_loaded1")]
    hi_done = S("hi_done")
    lo_done = S("lo_done", 2)
    gemm_done = S("gemm_done", 4)
    acc_free = S("acc_free", 4)

    def high_free(n):
        return n + 1

    def settle(eng):
        eng.sem_inc(passed, 1)

    def panel_done(n):
        return n + 5

    block = nc.Block()
    with block as blk:

        @blk.sync
        def _(sp):
            sp.wait_ge(started, 1)

            def load(src, layer, first, count):
                width = src.shape[-1]

                def one(i, number, slot):
                    sp.wait_ge(lo_done, layer + number + 1)
                    sp.dma_start(raw[:, slot, 0:width], src[i]).then_inc(raw_loaded[slot], 16)

                pairs = count // 2 if count >= 4 else 0
                if pairs:
                    with sp.Fori(0, pairs) as i:
                        for j in range(2):
                            one(i * 2 + j, i * 2 + (first + j), (first + j) % 2)
                for j in range(2 * pairs, count):
                    one(j, first + j, (first + j) % 2)
                return first + count

            n = 0
            for name in SEGMENTS1:
                n = load(dram["w_" + name], 0, n, dram["w_" + name].shape[0])
            assert n == N_MERGE
            with sp.Fori(0, 24) as i:
                sp.wait_ge(lo_done, i * 2 + (N_MERGE + 1))
                sp.dma_start(raw[:, 0, :], dram["w_gate"][i]).then_inc(raw_loaded[0], 16)
                sp.wait_ge(lo_done, i * 2 + (N_MERGE + 2))
                sp.dma_start(raw[:, 1, 0:512], dram["w_branch"][i]).then_inc(raw_loaded[1], 16)
            load(dram["w_rest1"], 0, N_O, 8 + 64)
            with sp.Fori(0, LAYERS) as l:
                n = N_BLOCK1
                for name in SEGMENTS2:
                    src = dram["w_" + name][l]
                    n = load(src, l * PER_LAYER, n, src.shape[0])
                assert n == N_BLOCK1 + PER_LAYER
            load(dram["w_in1"][0:LOOK], 0, N_PANELS, LOOK)
            sp.wait_ge(lo_done, N_PANELS + LOOK + 2)

        @blk.tensor
        def _(pe):
            pe.wait_ge(started, 1)
            pe.wait_ge(S("const_loaded"), 48)

            def products(dst, w, src, start, stop):
                nc.tensor.matmul(dst, w[0], src[0], start=start, stop=False)
                nc.tensor.matmul(dst, w[0], src[1], start=False, stop=False)
                return nc.tensor.matmul(dst, w[1], src[0], start=False, stop=stop)

            def tile_products(dst, slot, unit, width, k_tiles, src, base=0):
                for k in range(k_tiles):
                    cut = slice(unit + k * width, unit + (k + 1) * width)
                    last = products(dst, (w_hi[:, slot, cut], w_lo[:, slot, cut]),
                                    (src[0][:, base + k, :], src[1][:, base + k, :]), k == 0, k == k_tiles - 1)
                return last

            act_in, y_in, merged_in = (act_hi, act_lo), (y_hi, y_lo), (merged_hi, merged_lo)

            def gemm(layer, first, count, k_tiles, src, base=0):
                def one(n, slot):
                    pe.wait_ge(lo_done, n + 3)
                    pe.wait_ge(acc_free, n + 1)
                    tile_products(acc[:, slot, :], slot, 0, P, k_tiles, src, base).then_inc(gemm_done, 1)

                fours = count // 4 if count >= 8 else 0
                if fours:
                    with pe.Fori(0, fours) as i:
                        for j in range(4):
                            one(layer + i * 4 + (first + j), (first + j) % 4)
                for j in range(4 * fours, count):
                    one(layer + (first + j), (first + j) % 4)

            def gemm_values(layer, first, k_tiles, src, base=0):
                per = min(2, k_tiles)
                for q in range(k_tiles // per):
                    n, slot = layer + (first + q), (first + q) % 4
                    pe.wait_ge(lo_done, n + 3)
                    if q == 0:
                        pe.wait_ge(acc_free, n + 4)
                    for kk in range(per):
                        k = q * per + kk
                        w = [m[:, slot, kk * 512:(kk + 1) * 512] for m in (w_hi, w_lo)]
                        for t in range(TT):
                            a = [m[:, base + k, t * P:(t + 1) * P] for m in src]
                            last = products(acc[:, t, :], a, w, k == 0, k == k_tiles - 1)
                    last.then_inc(gemm_done, 1)

            def norm(r):
                for k in range(KD):
                    pe.wait_ge(S("norm_sq"), r * 8 + (k + 1))
                    last = nc.tensor.matmul(sc[:, 0, :], c["ones"], wb[:, k, :], start=k == 0, stop=k == KD - 1)
                last.then_inc(S("norm_sum"), 1)

            def softmax_pair(pair, scores_of):
                unit0 = pair * 8

                def outputs(u):
                    hh, qt = divmod(u, 4)
                    rows = slice(HD * hh, HD * hh + HD)
                    pe.wait_ge(S("soft_tcopy", 1), unit0 + (u + 2))
                    if u == 0:
                        pe.wait_ge(S("soft_ofree", 1), pair + 1)
                    for kb in range(qt + 1):
                        last = nc.tensor.matmul(po[rows, qt * P:(qt + 1) * P], vcur[:, kb, rows],
                                                probs_t[:, u % 2, kb * P:(kb + 1) * P], start=kb == 0, stop=kb == qt)
                    last.then_inc(S("soft_pv", 2), 1)

                def transposes(u):
                    pe.wait_ge(S("soft_p"), unit0 + (u + 1))
                    pe.wait_ge(S("soft_tcopy", 1), unit0 + (u + 1))
                    for kb in range(u % 4 + 1):
                        last = nc.tensor.transpose(pt[:, kb * P:(kb + 1) * P], probs[:, u % 2, kb * P:(kb + 1) * P],
                                                   c["ident"])
                    last.then_inc(S("soft_t", 2), 1)

                for u in range(8 + 2):
                    if u < 8:
                        pe.wait_ge(S("soft_exp", 2), unit0 + (u + 1))
                        scores_of(u).then_inc(S("soft_s"), 1)
                    if 1 <= u <= 8:
                        transposes(u - 1)
                    if u >= 2:
                        outputs(u - 2)

            def head_scores(u, wide):
                hh, qt = divmod(u, 4)
                kw = (qt + 1) * P
                rows, b = (slice(0, QH), hh) if wide else (slice(HD * hh, HD * hh + HD), 0)
                nc.tensor.matmul(sc[:, u % 2, 0:kw], qcur[rows, b, qt * P:kw], kcur[rows, b, 0:kw],
                                 start=True, stop=False)
                return hh, qt, kw

            def add_mask(u, qt, name):
                return nc.tensor.matmul(sc[:, u % 2, qt * P:(qt + 1) * P], c["ident"], c[name], start=False, stop=True)

            def scores_a(u):
                hh, qt, kw = head_scores(u, False)
                nc.tensor.matmul(sc[:, u % 2, 0:kw], c["anti"], tab[:, hh, T - kw:T], start=False, stop=False)
                return add_mask(u, qt, "chunk_mask")

            def scores_c(u):
                hh, qt, kw = head_scores(u, True)
                return add_mask(u, qt, "chunk_mask")

            def scores_f(u):
                hh, qt, kw = head_scores(u, False)
                nc.tensor.matmul(sc[:, u % 2, 0:kw], augq[:, hh, qt * P:kw], augk[:, hh, 0:kw],
                                 start=False, stop=False)
                return add_mask(u, qt, "causal_mask")

            def linear_outputs(name, pair, piece):
                pe.wait_ge(S(name + "_st", 1), pair + 2)
                pe.wait_ge(S(name + "_ofree", 1), pair + 1)
                for hh in range(2):
                    rows = slice(HD * hh, HD * hh + HD)
                    for it in range(TT):
                        for jt in range(it + 1):
                            last = nc.tensor.matmul(po[rows, it * P:(it + 1) * P], vcur[:, jt, rows],
                                                    piece(hh, jt, it), start=jt == 0, stop=jt == it)
                last.then_inc(S(name + "_pv"), 1)

            def head_mean(ready, done, r, src):
                pe.wait_ge(S(ready), r + 1)
                nc.tensor.matmul(pt[:, :], c["head_mean"], src, start=True, stop=True).then_inc(S(done), 1)

            norm(0)
            pe.wait_ge(S("norm_split"), 8)
            gemm(0, N_AQK, 8, KD, act_in)
            gemm_values(0, N_AV, KD, act_in)
            with pe.Fori(0, PAIRS) as p:
                pe.wait_ge(S("soft_stage"), p + 1)
                pe.wait_ge(S("a_bias"), p * 16 + 16)
                softmax_pair(p, scores_a)
            gemm(0, N_BQFG, 12, KD, act_in)
            gemm_values(0, N_BV, KD, act_in)
            pe.wait_ge(acc_free, N_C + 4)

            def hgrn_piece(hh, jt, it):
                if jt == it:
                    return s_diag[:, hh, jt, :]
                if it // 2 == jt // 2:
                    return s_128[:, hh, jt // 2, :]
                return s_256[:, hh, jt, (it - 2) * P:(it - 1) * P]

            with pe.Fori(0, PAIRS) as p:
                pe.wait_ge(S("b_stage"), p + 1)
                for v, half in enumerate(LEVELS):
                    if v:
                        pe.wait_ge(S("b_x"), p * 9 + v)
                    for hh in range(2):
                        rows = slice(HD * hh, HD * hh + HD)
                        unit = 2 * v + hh
                        bank = lev_bank[unit % 4]
                        pe.wait_ge(S("b_sfree", 4), p * 20 + (unit + 1))
                        if half == 0:
                            cuts = [(kcur[rows, 0, t * P:(t + 1) * P], qcur[rows, 0, t * P:(t + 1) * P], P)
                                    for t in range(TT)]
                        elif half == 256:
                            cuts = [(tab[rows, v % 2, t * P:(t + 1) * P], tab[rows, v % 2, 256:512], 256)
                                    for t in range(2)]
                        elif half == 128:
                            cuts = [(tab[rows, v % 2, t * 256:t * 256 + P], tab[rows, v % 2, t * 256 + P:(t + 1) * 256], P)
                                    for t in range(2)]
                        else:
                            cuts = [(tab[rows, v % 2, t * P:(t + 1) * P], tab[rows, v % 2, t * P:(t + 1) * P], P)
                                    for t in range(TT)]
                        for t, (keys, queries, w) in enumerate(cuts):
                            last = nc.tensor.matmul(bank[:, t * w:(t + 1) * w], keys, queries, start=True, stop=True)
                        last.then_inc(S("b_s"), 1)
                linear_outputs("b", p, hgrn_piece)
                head_mean("b_sq", "b_mean", p, kcur[:, 1, :])
            pe.wait_ge(S("b_ofree", 1), PAIRS + 1)

            gemm(0, N_C, 4, KD, act_in)
            for first, count in ((0, 2), (2, 1)):
                for k in range(first, first + count):
                    pe.wait_ge(S("c_sq"), k + 1)
                    last = nc.tensor.matmul(sc[:, first // 2, :], c["ones"], wb[:, k, :],
                                            start=k == first, stop=k == first + count - 1)
                last.then_inc(S("c_sum"), 1)
            pe.wait_ge(S("c_rotin"), 1)
            nc.tensor.matmul(po[:, :], c["rope_c"], wv[:, 3, :], start=True, stop=True).then_inc(S("c_rot"), 1)
            pe.wait_ge(S("cn_split"), 3)
            for q in range(2):
                n, slot = N_UP + q, (N_UP + q) % 4
                pe.wait_ge(lo_done, n + 3)
                pe.wait_ge(acc_free, n + 4)
                for h in range(4):
                    last = tile_products(acc[0:QH, h, :], slot, h * 2 * QH, QH, 2, y_in, 8)
                last.then_inc(gemm_done, 1)
            n, slot = N_UP + 2, (N_UP + 2) % 4
            pe.wait_ge(lo_done, n + 3)
            pe.wait_ge(acc_free, n + 4)
            for h in range(4):
                last = tile_products(acc[:, h, :], slot, h * P, P, 1, y_in, 10)
            last.then_inc(gemm_done, 1)
            gemm_values(0, N_UP + 3, 1, y_in, 10)
            for h in range(HEADS):
                pe.wait_ge(S("c_rotin"), 2 + h // 4)
                pe.wait_ge(S("c_rotused"), 1 + h)
                nc.tensor.matmul(po[0:QH, :], consts[0:QH, CONSTS.index("rope_c"), 0:QH], wa[0:QH, h, :],
                                 start=True, stop=True).then_inc(S("c_rot"), 1)
            pe.wait_ge(S("c_rotused"), 1 + HEADS)
            with pe.Fori(0, PAIRS) as p:
                pe.wait_ge(S("soft_stage"), p + 5)
                softmax_pair(p + 4, scores_c)

            pe.wait_ge(S("soft_y"), 2 * PAIRS)
            with pe.Fori(0, 4) as i:
                for j in range(12):
                    n, slot = i * 12 + (N_MERGE + j), (N_MERGE + j) % 4
                    pe.wait_ge(lo_done, n + 3)
                    pe.wait_ge(acc_free, n + 1)
                    if j % 2 == 0:
                        last = tile_products(acc[:, slot, :], slot, 0, P, KD, act_in)
                    else:
                        last = tile_products(acc[:, slot, :], slot, 0, P, 4, y_in, 4 * (j // 2 % 3))
                    last.then_inc(gemm_done, 1)
            pe.wait_ge(S("m_split"), 8)
            gemm(0, N_O, 8, KD, merged_in)
            norm(1)
            pe.wait_ge(S("norm_split"), 16)
            with pe.Fori(0, 4) as i:
                gemm(i * 16, N_FF, 8, KD, act_in)
                pe.wait_ge(S("g_split"), i * 8 + 8)
                settle(pe)
                gemm(i * 16, N_FF + 8, 8, KD, y_in)

            norm(2)

            with pe.Fori(0, LAYERS) as l:
                layer = l * PER_LAYER
                norm(l * 3 + 3)
                pe.wait_ge(S("norm_split"), l * 24 + 24)
                settle(pe)
                gemm(layer, N_BLOCK1 + O_FL, 1, KD, act_in)
                gemm(layer, N_BLOCK1 + O_FQK, 8, KD, act_in)
                gemm_values(layer, N_BLOCK1 + O_FV, KD, act_in)
                with pe.Fori(0, PAIRS) as p:
                    pair = l * 4 + p
                    pe.wait_ge(S("soft_stage"), pair + 9)
                    pe.wait_ge(S("f_aug"), pair * 32 + 32)
                    softmax_pair(pair + 8, scores_f)
                gemm(layer, N_BLOCK1 + O_RQK, 8, KD, act_in)
                gemm(layer, N_BLOCK1 + O_RG, 4, KD, act_in)
                gemm_values(layer, N_BLOCK1 + O_RV, KD, act_in)
                pe.wait_ge(acc_free, layer + (N_BLOCK1 + O_O + 4))
                pe.wait_ge(S("soft_ofree", 1), l * 4 + 13)
                for i in range(8):
                    pe.wait_ge(S("r_rotused", 1), l * 8 + (i + 1))
                    nc.tensor.matmul(po[:, :], c["rope_r"], wa[:, i, :], start=True,
                                     stop=True).then_inc(S("r_rot"), 1)
                pe.wait_ge(S("r_rotused", 1), l * 8 + 9)
                settle(pe)
                with pe.Fori(0, PAIRS) as p:
                    pair = l * 4 + p
                    pe.wait_ge(S("r_stage"), pair + 1)
                    for u in range(8):
                        hh, jt = divmod(u, 4)
                        rows = slice(HD * hh, HD * hh + HD)
                        pe.wait_ge(S("r_sfree", 4), pair * 8 + (u + 1))
                        nc.tensor.matmul(lev_bank[u % 4][:, 0:T - jt * P], kcur[rows, 0, jt * P:(jt + 1) * P],
                                         qcur[rows, 0, jt * P:T], start=True, stop=True).then_inc(S("r_s"), 1)
                    linear_outputs("r", pair,
                                   lambda hh, jt, it: s_ret[hh][:, s_off[jt] + (it - jt) * P:
                                                                s_off[jt] + (it - jt + 1) * P])
                    head_mean("r_o", "r_mean", pair, probs[:, 0, :])
                    head_mean("r_sq", "r_var", pair, probs_t[:, 0, :])
                pe.wait_ge(S("r_y"), l * 4 + 4)
                settle(pe)
                gemm(layer, N_BLOCK1 + O_O, 8, KD, y_in)
                norm(l * 3 + 4)
                pe.wait_ge(S("norm_split"), l * 24 + 32)
                settle(pe)
                done = 0
                for ch, tiles in enumerate(CHUNKS2):
                    gemm(layer, N_BLOCK1 + O_FFN[ch], 2 * tiles, KD, act_in)
                    done += tiles
                    pe.wait_ge(S("h_split"), l * FT2 + done)
                    settle(pe)
                    gemm(layer, N_BLOCK1 + O_FFN[ch] + 2 * tiles, 8, tiles, y_in)
                norm(l * 3 + 5)
                pe.wait_ge(S("norm_split"), l * 24 + 40)
                settle(pe)
                gemm(layer, N_BLOCK1 + O_GATE, 8, KD, act_in)
                pe.wait_ge(S("e_split"), l * 2 + 2)
                for q in range(3):
                    n, slot = layer + (N_BLOCK1 + O_PLE + q), (O_PLE + q) % 4
                    pe.wait_ge(lo_done, n + 3)
                    pe.wait_ge(acc_free, n + 4)
                    for m in range(3 if q < 2 else 2):
                        last = tile_products(acc[:, m, :], slot, m * 2 * P, P, 2, y_in, 8)
                    last.then_inc(gemm_done, 1)
            norm(9)

        @blk.scalar
        def _(act):
            act.dma_start(consts[:, :, :], dram["consts"]).then_inc(S("const_loaded"), 16)
            act.dma_start(masks[:, :, :], dram["masks"]).then_inc(S("const_loaded"), 16)
            act.dma_start(params[:, :], dram["params"]).then_inc(S("const_loaded"), 16)
            act.dma_start(x[:, :, :], dram["x"]).then_inc(S("x_loaded"), 16)
            act.wait_ge(started, 1)

            def high(half, full, number):
                act.wait_ge(raw_loaded[number % 2], (half + number // 2) * 16 + 16)
                act.wait_ge(gemm_done, high_free(full + number))
                nc.scalar.copy(w_hi[:, number % 4, :], raw[:, number % 2, :]).then_inc(hi_done, 1)

            def split_ahead(half, full, first, count, body=None):
                fours = count // 4 if count >= 8 else 0
                if fours:
                    with act.Fori(0, fours) as i:
                        for j in range(4):
                            high(half + i * 2, full + i * 4, first + LOOK + j)
                            if body:
                                body(i * 4 + j)
                for j in range(4 * fours, count):
                    high(half, full, first + LOOK + j)
                    if body:
                        body(j)

            def high_of_tile(name, k, dst, src):
                act.wait_ge(S(name + "_h"), k + 1)
                nc.scalar.copy(dst, src).then_inc(S(name + "_hi"), 1)

            def factor(dst, src, scale, eps):
                nc.scalar.activation(dst, src, ACT.Ln, bias=par(eps), scale=scale)
                act.drain()
                return nc.scalar.activation(dst, dst, ACT.Exp, scale=-0.5)

            def norm(r, split=None):
                for k in range(KD):
                    nc.scalar.activation(wb[:, k, :], x[:, k, :], ACT.Square).then_inc(S("norm_sq"), 1)
                act.wait_ge(S("norm_sum"), r + 1)
                factor(probs[:, 0, :], sc[:, 0, :], 1.0 / D, "eps").then_inc(S("norm_rstd"), 1)
                if split is not None:
                    for k in range(KD):
                        high_of_tile("norm", split * 8 + k, act_hi[:, k, :], wb[:, k, :])

            def softmax_pair(pair):
                unit0 = pair * 8

                def expo(u):
                    kw = (u % 4 + 1) * P
                    act.wait_ge(S("soft_max"), unit0 + (u + 1))
                    act.wait_ge(S("soft_t", 2), unit0 + (u + 1))
                    nc.scalar.activation(probs[:, u % 2, 0:kw], sc[:, u % 2, 0:kw], ACT.Exp, bias=neg_max[u % 2],
                                         accum_out=prob_sum[u % 2]).then_inc(S("soft_exp", 2), 1)

                def copy_t(u):
                    kw = (u % 4 + 1) * P
                    act.wait_ge(S("soft_t", 2), unit0 + (u + 3))
                    act.wait_ge(S("soft_pv", 2), unit0 + (u + 1))
                    nc.scalar.copy(probs_t[:, u % 2, 0:kw], pt[:, 0:kw]).then_inc(S("soft_tcopy", 1), 1)

                for u in range(9):
                    if u < 8:
                        expo(u)
                    if u >= 1:
                        copy_t(u - 1)

            def in_place(func, ready, done, k, tile, **kw):
                act.wait_ge(S(ready), k + 1)
                nc.scalar.activation(tile, tile, func, **kw).then_inc(S(done), 1)

            high(0, 0, 0)
            high(0, 0, 1)
            act.wait_ge(S("x_loaded"), 16)
            act.wait_ge(S("const_loaded"), 48)
            norm(0, 0)
            split_ahead(0, 0, N_AQK, 8)
            split_ahead(0, 0, N_AV, 4)
            with act.Fori(0, PAIRS) as p:
                act.dma_start(tab[:, :, :], dram["bias"][p]).then_inc(S("a_bias"), 16)
                softmax_pair(p)

            split_ahead(0, 0, N_BQFG, 4, lambda j: in_place(ACT.Silu, "b_q", "b_qsilu", j, wa[:, j, :]))
            split_ahead(0, 0, N_BQFG + 4, 4)
            split_ahead(0, 0, N_BQFG + 8, 4, lambda j: in_place(ACT.Silu, "b_g", "b_gsilu", j, wb[:, 4 + j, :]))
            split_ahead(0, 0, N_BV, 4)
            in_place(ACT.Exp, "b_lb", "b_lbexp", 0, lower)
            act.wait_ge(S("b_z"), 1)
            nc.scalar.activation(wa[:, 4:8, :], wb[:, 0:4, :], ACT.Sigmoid, scale=-1.0).then_inc(S("b_key"), 1)
            nc.scalar.activation(decay_tmp[:, :, :], decay_tmp[:, :, :], ACT.Exp)
            act.drain()
            nc.scalar.activation(decay_tmp[:, :, :], decay_tmp[:, :, :], ACT.Ln, bias=par("one")).then_inc(S("b_softplus"), 1)
            in_place(ACT.Exp, "b_neglog", "b_inv", 0, decay_tmp[:, :, :])
            in_place(ACT.Ln, "b_mixed", "b_mixedlog", 0, decay_tmp[:, :, :])

            with act.Fori(0, PAIRS) as p:
                for v in range(1, len(LEVELS)):
                    e = kcur[:, 1, :] if v % 2 else qcur[:, 1, :]
                    in_place(ACT.Exp, "b_d", "b_e", p * 9 + (v - 1), e)
                act.wait_ge(S("b_pv"), p + 1)
                act.wait_ge(S("b_st", 1), p + 2)
                nc.scalar.activation(kcur[:, 1, :], po[:, :], ACT.Square).then_inc(S("b_sq"), 1)
                act.wait_ge(S("b_mean"), p + 1)
                factor(qcur[:, 1, :], pt[:, :], 1.0, "eps").then_inc(S("b_rstd"), 1)

            act.dma_start(positions[:, :], dram["positions"].partition_broadcast(P)).then_inc(S("pos_loaded"), 16)
            split_ahead(0, 0, N_C, 4)
            act.wait_ge(S("c_raw"), 3)
            for k in range(3):
                nc.scalar.activation(wb[:, k, :], wv[:, k, :], ACT.Square).then_inc(S("c_sq"), 1)
            act.wait_ge(S("c_sum"), 1)
            act.wait_ge(S("b_ofree", 1), PAIRS + 1)
            factor(probs[:, 0, :], sc[:, 0, :], 1.0 / QR, "eps").then_inc(S("c_rstd"), 1)
            act.wait_ge(S("c_sum"), 2)
            factor(probs[:, 1, :], sc[:, 1, :], 1.0 / KVR, "eps").then_inc(S("c_rstd"), 1)
            for k in range(3):
                high_of_tile("cn", k, y_hi[:, 8 + k, :], wb[:, k, :])
            for k in range(2):
                in_place(ACT.Sin, "c_angle", "c_sincos", k, tab[:, k, :])
            split_ahead(0, 0, N_UP, 4)
            with act.Fori(0, PAIRS) as p:
                softmax_pair(p + 4)

            with act.Fori(0, 4) as i:
                for j in range(12):
                    high(i * 6, i * 12, N_MERGE + LOOK + j)
                    n = i * 12 + (N_MERGE + j)
                    if j % 2 == 0:
                        act.wait_ge(gemm_done, panel_done(n))
                        act.wait_ge(acc_free, n + 2)
                        nc.scalar.activation(probs[:, j // 2 % 2, :], acc[:, (N_MERGE + j) % 4, :],
                                             ACT.Sigmoid).then_inc(S("m_gate"), 1)
                    if j % 6 == 5:
                        high_of_tile("m", i * 2 + j // 6, merged_hi[:, i * 2 + j // 6, :], probs_t[:, 1, :])
            split_ahead(0, 0, N_O, 8)
            act.wait_ge(S("norm_x"), 1)
            norm(1, 1)
            with act.Fori(0, 4) as i:
                with act.Fori(0, 2) as ii:
                    for j in range(4):
                        high(i * 8 + ii * 2, i * 16 + ii * 4, N_FF + LOOK + j)
                        high_of_tile("g", i * 8 + ii * 4 + j, y_hi[:, ii * 4 + j, :], probs[:, 0, :])
                split_ahead(i * 8, i * 16, N_FF + 8, 8)

            act.wait_ge(S("norm_x"), 2)
            norm(2)

            with act.Fori(0, LAYERS) as l:
                half, full = l * (PER_LAYER // 2), l * PER_LAYER
                act.wait_ge(S("norm_x"), l * 3 + 3)
                norm(l * 3 + 3, l * 3 + 2)
                split_ahead(half, full, N_BLOCK1 + O_FL, 1)
                fl = wb[0:8, 6, :]
                act.wait_ge(S("f_z"), l + 1)
                nc.scalar.activation(fl, fl, ACT.Exp)
                act.drain()
                nc.scalar.activation(fl, fl, ACT.Ln, bias=par("one", rows=8)).then_inc(S("f_softplus"), 1)
                act.wait_ge(S("f_cum"), l + 1)
                act.dma_start(cum_dram[0], wb[0:8, 6, :]).then_inc(S("cum_stored"), 16)
                act.dma_start(cum_dram[1], wb[0:8, 7, :]).then_inc(S("cum_stored"), 16)
                split_ahead(half, full, N_BLOCK1 + O_FQK, 8)
                split_ahead(half, full, N_BLOCK1 + O_FV, 4)
                act.wait_ge(S("cum_stored"), l * 32 + 32)
                with act.Fori(0, PAIRS) as p:
                    pair = l * 4 + p
                    act.dma_start(wb[0:1, 0:2, :], cum_dram[0:1, bass.ds(p * 2, 2), :]).then_inc(S("f_aug"), 16)
                    act.dma_start(wb[1:2, 2:4, :], cum_dram[1:2, bass.ds(p * 2, 2), :]).then_inc(S("f_aug"), 16)
                    softmax_pair(pair + 8)
                act.dma_start(tab[:, :, :], dram["rotary"]).then_inc(S("rotary_loaded"), 16)
                split_ahead(half, full, N_BLOCK1 + O_RQK, 8)
                split_ahead(half, full, N_BLOCK1 + O_RG, 4,
                            lambda j: in_place(ACT.Silu, "r_g", "r_gsilu", l * 4 + j, wb[:, 4 + j, :]))
                split_ahead(half, full, N_BLOCK1 + O_RV, 4)
                act.wait_ge(S("r_rotused", 1), l * 8 + 9)
                with act.Fori(0, PAIRS) as p:
                    pair = l * 4 + p
                    act.wait_ge(S("r_st", 1), pair + 1)
                    act.dma_start(tab[:, :, :], dram["decay"][p]).then_inc(S("decay_loaded"), 16)
                    act.wait_ge(S("r_d"), pair + 1)
                    nc.scalar.activation(probs_t[:, 0, :], probs[:, 0, :], ACT.Square).then_inc(S("r_sq"), 1)
                    act.wait_ge(S("r_var"), pair + 1)
                    factor(probs[:, 1, :], pt[:, :], 1.0, "gn_eps").then_inc(S("r_rstd"), 1)
                split_ahead(half, full, N_BLOCK1 + O_O, 8)
                act.wait_ge(S("norm_x"), l * 3 + 4)
                norm(l * 3 + 4, l * 3 + 3)
                done = 0
                for ch, count in enumerate(CHUNKS2):
                    first = N_BLOCK1 + O_FFN[ch]
                    with act.Fori(0, count // 2) as i:
                        for j in range(4):
                            high(half + i * 2, full + i * 4, first + LOOK + j)
                            if j % 2:
                                act.wait_ge(S("h_conv"), l * FT2 + i * 2 + (done + j // 2 + 1))
                                nc.scalar.activation(probs_t[:, 1, :], probs_t[:, 0, :],
                                                     ACT.Gelu).then_inc(S("h_gelu"), 1)
                                high_of_tile("h", l * FT2 + i * 2 + (done + j // 2), y_hi[:, i * 2 + j // 2, :],
                                             probs[:, 0, :])
                    split_ahead(half, full, first + 2 * count, 8)
                    done += count
                act.dma_start(wv[:, 0:2, :], dram["p"][l]).then_inc(S("e_loaded"), 16)
                act.wait_ge(S("e_loaded"), l * 16 + 16)
                act.wait_ge(S("norm_x"), l * 3 + 5)
                for k in range(2):
                    nc.scalar.copy(y_hi[:, 8 + k, :], wv[:, k, :]).then_inc(S("e_hi"), 1)
                norm(l * 3 + 5, l * 3 + 4)
                split_ahead(half, full, N_BLOCK1 + O_GATE, 8,
                            lambda j: in_place(ACT.Sigmoid, "e_g", "e_gate", l * 8 + j, wa[:, j, :]))
                split_ahead(half, full, N_BLOCK1 + O_PLE, 3)
            act.wait_ge(S("norm_x"), 9)
            norm(9)
            for k in range(KD):
                act.wait_ge(S("out_ready"), k + 1)
                act.dma_start(out[k * P:(k + 1) * P, :], wb[:, k, :]).then_inc(S("out_stored"), 16)
            act.wait_ge(S("out_stored"), 16 * KD)

        @blk.vector
        def _(dve):
            v = nc.vector
            dve.wait_ge(started, 1)
            dve.wait_ge(S("const_loaded"), 48)

            def each(layer, first, count, body):
                fours = count // 4 if count >= 8 else 0
                if fours:
                    with dve.Fori(0, fours) as i:
                        for j in range(4):
                            body(layer + i * 4 + (first + j), (first + j) % 4, i * 4 + j)
                for j in range(4 * fours, count):
                    body(layer + (first + j), (first + j) % 4, j)

            def evacuate(layer, first, count, dst_of, signal=None):
                def one(n, slot, i):
                    dve.wait_ge(gemm_done, panel_done(n))
                    v.tensor_copy(dst_of(i), acc[:, slot, :]).then_inc(acc_free, 1)
                    if signal:
                        dve.drain().then_inc(S(signal), 1)
                each(layer, first, count, one)

            def values(layer, first, count=4):
                dve.wait_ge(gemm_done, panel_done(layer + (first + count - 1)))
                v.tensor_copy(wv[:, :, :], acc[:, :, :]).then_inc(acc_free, count)

            def add_to_x(layer, first, signal):
                def one(n, slot, i):
                    dve.wait_ge(gemm_done, panel_done(n))
                    v.tensor_tensor(x[:, i, :], x[:, i, :], acc[:, slot, :], ALU.add).then_inc(acc_free, 1)
                each(layer, first, 8, one)
                if signal:
                    dve.drain().then_inc(S(signal), 1)

            def low_of_tile(name, k, src, hi, lo):
                dve.wait_ge(S(name + "_hi"), k + 1)
                v.tensor_tensor(lo, src, hi, ALU.subtract).then_inc(S(name + "_split"), 1)
                if name != "norm":
                    dve.drain()

            def norm(r, split, gains, i0):
                dve.wait_ge(S("norm_rstd"), r + 1)
                for k in range(KD + 1):
                    if k < KD:
                        v.scalar_tensor_tensor(wb[:, k, :], x[:, k, :], par(gains, i0 + k), probs[:, 0, :],
                                               ALU.mult, ALU.mult).then_inc(S("norm_h"), 1)
                    if k:
                        low_of_tile("norm", split * 8 + (k - 1), wb[:, k - 1, :], act_hi[:, k - 1, :], act_lo[:, k - 1, :])

            def split_here(src, tile, done):
                v.tensor_copy(y_hi[:, tile, :], src)
                dve.drain()
                v.tensor_tensor(y_lo[:, tile, :], src, y_hi[:, tile, :], ALU.subtract).then_inc(S(done), 1)

            def stage(name, p, scale=1.0):
                v.tensor_scalar(qcur[:, 0, :], wa[:, p, :], scale, None, ALU.mult)
                v.tensor_copy(kcur[:, 0, :], wa[:, p + 4, :])
                v.tensor_copy(vcur[:, :, :], wv[:, :, bass.ds(p * P, P)])
                dve.drain().then_inc(S(name + "_stage"), 1)

            def softmax_pair(pair, tile):
                unit0 = pair * 8

                def row_max(u):
                    kw = (u % 4 + 1) * P
                    dve.wait_ge(S("soft_s"), unit0 + (u + 1))
                    v.tensor_reduce(neg_max[u % 2], sc[:, u % 2, 0:kw], AX.X, ALU.max,
                                    negate=True).then_inc(S("soft_max"), 1)

                def normalise(u):
                    kw = (u % 4 + 1) * P
                    dve.wait_ge(S("soft_exp", 2), unit0 + (u + 3))
                    v.reciprocal(inv_sum[u % 2], prob_sum[u % 2])
                    dve.drain()
                    v.tensor_scalar(probs[:, u % 2, 0:kw], probs[:, u % 2, 0:kw], inv_sum[u % 2], None,
                                    ALU.mult).then_inc(S("soft_p"), 1)

                for u in range(9):
                    if u < 8:
                        row_max(u)
                    if u:
                        normalise(u - 1)
                dve.wait_ge(S("soft_pv", 2), unit0 + 10)
                v.tensor_copy(y_hi[:, tile, :], po[:, :])
                dve.drain()
                v.tensor_tensor(y_lo[:, tile, :], po[:, :], y_hi[:, tile, :], ALU.subtract)
                dve.drain().then_inc(S("soft_ofree", 1), 1)
                dve.nop().then_inc(S("soft_y"), 1)

            def rotate(tile, rows, sin, cos):
                v.tensor_tensor(probs_t[0:rows, 0, :], po[0:rows, :], sin, ALU.mult)
                v.tensor_tensor(tile, tile, cos, ALU.mult)
                dve.drain()
                return v.tensor_tensor(tile, tile, probs_t[0:rows, 0, :], ALU.add)

            norm(0, 0, "mix_g", 0)
            evacuate(0, N_AQK, 8, lambda i: wa[:, i, :])
            values(0, N_AV)
            dve.drain()
            with dve.Fori(0, PAIRS) as p:
                stage("soft", p, HD ** -0.5)
                softmax_pair(p, p)

            evacuate(0, N_BQFG, 4, lambda i: wa[:, i, :], "b_q")
            evacuate(0, N_BQFG + 4, 4, lambda i: wb[:, i, :])
            evacuate(0, N_BQFG + 8, 4, lambda i: wb[:, 4 + i, :], "b_g")
            values(0, N_BV)
            lb = params[:, PARAMS["lb"][0]:PARAMS["lb"][0] + PAIRS]
            v.tensor_tensor(lower, lb, lb, ALU.subtract).then_inc(S("b_lb"), 1)
            dve.wait_ge(S("b_lbexp"), 1)
            v.reciprocal(rest, lower)
            dve.drain()
            v.tensor_tensor(lower, lower, rest, ALU.mult)
            dve.drain()
            v.tensor_tensor(lower, lower, lower, ALU.subtract)
            dve.drain()
            v.tensor_scalar(rest, lower, -1.0, 1.0, ALU.mult, ALU.add)
            z, keys, tmp = wb[:, 0:4, :], wa[:, 4:8, :], decay_tmp[:, :, :]
            v.scalar_tensor_tensor(tmp, z, -1.0, z, ALU.mult, ALU.min)
            dve.drain().then_inc(S("b_z"), 1)
            for i, h in enumerate((64, 128, 256)):
                v.memset(resets[:, i, :], 1.0)
                dve.drain()
                v.memset(resets[:, i, :].rearrange("p (b h) -> p b h", h=h)[:, :, 0:1], 0.0)
            dve.wait_ge(S("b_key"), 1)
            dve.wait_ge(S("b_softplus"), 1)
            v.scalar_tensor_tensor(z, z, 0.0, tmp, ALU.min, ALU.subtract)
            for i in range(PAIRS):
                v.tensor_scalar(wa[:, 4 + i, :], wa[:, 4 + i, :], rest[:, i:i + 1], None, ALU.mult)
            dve.drain()
            v.tensor_scalar(tmp, z, -1.0, 40.0, ALU.mult, ALU.min).then_inc(S("b_neglog"), 1)
            dve.wait_ge(S("b_inv"), 1)
            for i in range(PAIRS):
                v.tensor_scalar(decay_tmp[:, i, :], decay_tmp[:, i, :], lower[:, i:i + 1], rest[:, i:i + 1],
                                ALU.mult, ALU.add)
            dve.drain().then_inc(S("b_mixed"), 1)
            dve.wait_ge(S("b_mixedlog"), 1)
            v.tensor_tensor(z, z, tmp, ALU.add)
            dve.wait_ge(S("b_qsilu"), 4)
            dve.wait_ge(S("b_gsilu"), 4)
            dve.drain()

            def halves(ap, h):
                w = ap.rearrange("p (b two h) -> p b two h", two=2, h=h)
                return w[:, :, 0, :], w[:, :, 1, :]

            with dve.Fori(0, PAIRS) as p:
                for i in range(3):
                    v.tensor_tensor_scan(cums[:, i, :], resets[:, i, :], wb[:, p, :], 0.0, ALU.mult, ALU.add)
                stage("b", p)

                def exponents(n):
                    h = LEVELS[n]
                    e = kcur[:, 1, :] if n % 2 else qcur[:, 1, :]
                    cum = cums[:, {256: 2, 128: 1}.get(h, 0), :]
                    (e0, e1), (c0, c1) = halves(e, h), halves(cum, h)
                    mid = c0[:, :, h - 1:h].broadcast_to([P, T // (2 * h), h])
                    v.tensor_tensor(e0, mid, c0, ALU.subtract)
                    if h >= 64:
                        v.tensor_copy(e1, c1)
                    else:
                        v.tensor_tensor(e1, c1, mid, ALU.subtract)
                    dve.drain().then_inc(S("b_d"), 1)

                def decayed(n):
                    h = LEVELS[n]
                    e = kcur[:, 1, :] if n % 2 else qcur[:, 1, :]
                    dve.wait_ge(S("b_e"), p * 9 + n)
                    (e0, e1), (x0, x1) = halves(e, h), halves(tab[:, n % 2, :], h)
                    k0, q1 = halves(kcur[:, 0, :], h)[0], halves(qcur[:, 0, :], h)[1]
                    v.tensor_tensor(x0, e0, k0, ALU.mult)
                    v.tensor_tensor(x1, e1, q1, ALU.mult)
                    dve.drain().then_inc(S("b_x"), 1)

                def collect(n):
                    h = LEVELS[n]
                    for hh in range(2):
                        bank = lev_bank[(2 * n + hh) % 4]
                        dve.wait_ge(S("b_s"), p * 20 + (2 * n + hh + 1))
                        settle(dve)
                        tiles = bank.rearrange("p (t i) -> p t i", i=P)
                        if h == 0:
                            ident = c["ident"].rearrange("p (o i) -> p o i", o=1).broadcast_to([P, TT, P])
                            last = v.tensor_tensor(s_diag[:, hh, :, :], tiles, ident, ALU.mult)
                        elif h == 256:
                            last = v.tensor_copy(s_256[:, hh, :, :], bank.rearrange("p (t i) -> p t i", i=256))
                        elif h == 128:
                            last = v.tensor_copy(s_128[:, hh, :, :], tiles[:, 0:2, :])
                        else:
                            mask = masks[:, n - 3, :].bitcast(mybir.dt.uint32).rearrange("p (o i) -> p o i", o=1)
                            last = v.copy_predicated(s_diag[:, hh, :, :], mask.broadcast_to([P, TT, P]), tiles)
                        last.then_inc(S("b_sfree", 4), 1)

                exponents(1)
                for n in range(1, len(LEVELS)):
                    if n + 1 < len(LEVELS):
                        exponents(n + 1)
                    decayed(n)
                    collect(n - 1)
                dve.drain()
                collect(len(LEVELS) - 1)
                dve.drain().then_inc(S("b_st", 1), 1)
                dve.wait_ge(S("b_rstd"), p + 1)
                t = probs_t[:, 1, :]
                v.scalar_tensor_tensor(t, po[:, :], par("hgrn_g"), qcur[:, 1, :], ALU.mult, ALU.mult)
                dve.drain()
                v.tensor_tensor(t, t, wb[:, p + 4, :], ALU.mult)
                dve.drain()
                split_here(t, p + 4, "b_y")
                dve.drain().then_inc(S("b_ofree", 1), 1)

            two_pi = 2.0 * np.pi
            c1 = 6.28125
            c2 = float(np.round((two_pi - c1) * 2 ** 22) / 2 ** 22)
            c3 = two_pi - c1 - c2
            magic = 1.5 * 2 ** 23
            ang, turn = probs_t[:, 0, :], probs_t[:, 1, :]
            dve.wait_ge(S("pos_loaded"), 16)
            v.tensor_copy(ang, positions[:, :])
            dve.drain()
            v.tensor_scalar(ang, ang, par("inv_freq"), None, ALU.mult)
            dve.drain()
            v.tensor_scalar(turn, ang, 1.0 / two_pi, magic, ALU.mult, ALU.add)
            dve.drain()
            v.tensor_scalar(turn, turn, magic, None, ALU.subtract)
            dve.drain()
            for part in (c1, c2, c3):
                v.scalar_tensor_tensor(ang, turn, -part, ang, ALU.mult, ALU.add)
                dve.drain()
            pi = 3.1415925
            v.tensor_scalar(tab[:, 0, :], ang, pi, -pi, ALU.min, ALU.max).then_inc(S("c_angle"), 1)
            v.tensor_scalar(ang, ang, 0.5 * np.pi, None, ALU.add)
            dve.drain()
            v.tensor_scalar(turn, ang, np.pi, -two_pi, ALU.is_gt, ALU.mult)
            dve.drain()
            v.tensor_tensor(ang, ang, turn, ALU.add)
            dve.drain()
            v.tensor_scalar(tab[:, 1, :], ang, pi, -pi, ALU.min, ALU.max).then_inc(S("c_angle"), 1)
            sin, cos = tab[:, 0, :], tab[:, 1, :]
            evacuate(0, N_C, 4, lambda i: wv[:, i, :], "c_raw")
            dve.nop().then_inc(S("c_rotin"), 1)
            for k in range(3):
                dve.wait_ge(S("c_rstd"), 1 + k // 2)
                gain = par("q_g", k) if k < 2 else par("kv_g")
                v.scalar_tensor_tensor(wb[:, k, :], wv[:, k, :], gain, probs[:, k // 2, :],
                                       ALU.mult, ALU.mult).then_inc(S("cn_h"), 1)
                low_of_tile("cn", k, wb[:, k, :], y_hi[:, 8 + k, :], y_lo[:, 8 + k, :])
            dve.wait_ge(S("c_sincos"), 2)
            dve.wait_ge(S("c_rot"), 1)
            rotate(wv[:, 3, :], P, sin, cos)
            dve.drain()
            for b in range(2):
                v.tensor_copy(kcur[NOPE:QH, b, :], wv[NOPE:QH, 3, :])
            dve.drain().then_inc(S("c_rotused"), 1)
            for q in range(2):
                dve.wait_ge(gemm_done, panel_done(N_UP + q))
                v.tensor_copy(wa[0:QH, 4 * q:4 * q + 4, :], acc[0:QH, :, :]).then_inc(acc_free, 1)
                dve.drain().then_inc(S("c_rotin"), 1)
            dve.wait_ge(gemm_done, panel_done(N_UP + 2))
            by_pair = wb[0:HD, :, :].rearrange("p (h two) t -> p h two t", two=2)
            v.tensor_copy(by_pair[:, :, 0, :], acc[0:HD, :, :])
            v.tensor_copy(by_pair[:, :, 1, :], acc[HD:P, :, :]).then_inc(acc_free, 1)
            values(0, N_UP + 3, 1)
            for h in range(HEADS):
                dve.wait_ge(S("c_rot"), 2 + h)
                rotate(wa[0:QH, h, :], QH, sin[0:QH], cos[0:QH]).then_inc(S("c_rotused"), 1)
            dve.drain()
            with dve.Fori(0, PAIRS) as p:
                for b in range(2):
                    v.tensor_scalar(qcur[0:QH, b, :], wa[0:QH, p * 2 + b, :], QH ** -0.5, None, ALU.mult)
                    v.tensor_copy(kcur[0:NOPE, b, :], wb[0:NOPE, p * 2 + b, :])
                v.tensor_copy(vcur[:, :, :], wv[:, :, bass.ds(p * P, P)])
                dve.drain().then_inc(S("soft_stage"), 1)
                softmax_pair(p + 4, p + 8)

            with dve.Fori(0, 4) as i:
                for b in range(6):
                    n = i * 12 + (N_MERGE + 2 * b + 1)
                    dve.wait_ge(S("m_gate"), i * 6 + (b + 1))
                    dve.wait_ge(gemm_done, panel_done(n))
                    total, term = probs_t[:, 1, :], probs_t[:, 0, :]
                    v.tensor_tensor(total if b % 3 == 0 else term, acc[:, (N_MERGE + 2 * b + 1) % 4, :],
                                    probs[:, b % 2, :], ALU.mult).then_inc(acc_free, 2)
                    dve.drain()
                    if b % 3:
                        v.tensor_tensor(total, total, term, ALU.add)
                        dve.drain()
                    if b % 3 == 2:
                        m = i * 2 + b // 3
                        dve.nop().then_inc(S("m_h"), 1)
                        low_of_tile("m", m, total, merged_hi[:, m, :], merged_lo[:, m, :])
            add_to_x(0, N_O, "norm_x")
            norm(1, 1, "ffn_g", 0)

            with dve.Fori(0, 4) as i:
                def relu_squared(n, slot, j):
                    dve.wait_ge(gemm_done, panel_done(n))
                    v.tensor_scalar(probs[:, 1, :], acc[:, slot, :], 0.0, None, ALU.max).then_inc(acc_free, 1)
                    dve.drain()
                    v.tensor_tensor(probs[:, 0, :], probs[:, 1, :], probs[:, 1, :], ALU.mult).then_inc(S("g_h"), 1)
                    low_of_tile("g", i * 8 + j, probs[:, 0, :], y_hi[:, j, :], y_lo[:, j, :])
                each(i * 16, N_FF, 8, relu_squared)
                add_to_x(i * 16, N_FF + 8, None)
            dve.drain().then_inc(S("norm_x"), 1)

            dve.wait_ge(S("norm_rstd"), 3)
            for k in range(KD):
                v.scalar_tensor_tensor(x[:, k, :], x[:, k, :], par("mid_g", k), probs[:, 0, :], ALU.mult, ALU.mult)
            dve.drain().then_inc(S("norm_x"), 1)

            with dve.Fori(0, LAYERS) as l:
                layer = l * PER_LAYER
                norm(l * 3 + 3, l * 3 + 2, "attn_w", l * KD)
                dve.wait_ge(gemm_done, panel_done(layer + (N_BLOCK1 + O_FL)))
                fz, ft, fneg, fone = (wb[0:8, i, :] for i in (5, 6, 7, 4))
                v.tensor_scalar(fz, acc[0:8, O_FL % 4, :], par("f_bias", l, 8), None, ALU.add).then_inc(acc_free, 1)
                v.memset(wb[0:8, 0:5, :], 1.0)
                dve.drain()
                v.scalar_tensor_tensor(ft, fz, -1.0, fz, ALU.mult, ALU.min).then_inc(S("f_z"), 1)
                dve.wait_ge(S("f_softplus"), l + 1)
                v.scalar_tensor_tensor(fz, fz, 0.0, ft, ALU.min, ALU.subtract)
                dve.drain()
                v.tensor_tensor_scan(ft, fone, fz, 0.0, ALU.mult, ALU.add)
                dve.drain()
                v.tensor_scalar(fneg, ft, -1.0, None, ALU.mult).then_inc(S("f_cum"), 1)
                evacuate(layer, N_BLOCK1 + O_FQK, 8, lambda i: wa[:, i, :])
                values(layer, N_BLOCK1 + O_FV)
                dve.drain()
                with dve.Fori(0, PAIRS) as p:
                    stage("soft", p, HD ** -0.5)
                    softmax_pair(l * 4 + p + 8, p)

                evacuate(layer, N_BLOCK1 + O_RQK, 8, lambda i: wa[:, i, :])
                evacuate(layer, N_BLOCK1 + O_RG, 4, lambda i: wb[:, 4 + i, :], "r_g")
                values(layer, N_BLOCK1 + O_RV)
                dve.wait_ge(S("rotary_loaded"), l * 16 + 16)
                for i in range(8):
                    dve.wait_ge(S("r_rot"), l * 8 + (i + 1))
                    rotate(wa[:, i, :], P, tab[:, 0, :], tab[:, 1, :]).then_inc(S("r_rotused", 1), 1)
                dve.wait_ge(S("r_gsilu"), l * 4 + 4)
                settle(dve)
                dve.drain()
                with dve.Fori(0, PAIRS) as p:
                    pair = l * 4 + p
                    stage("r", p)
                    dve.wait_ge(S("decay_loaded"), pair * 16 + 16)
                    for u in range(8):
                        hh, jt = divmod(u, 4)
                        w = T - jt * P
                        dve.wait_ge(S("r_s"), pair * 8 + (u + 1))
                        v.tensor_tensor(s_ret[hh][:, s_off[jt]:s_off[jt] + w], lev_bank[u % 4][:, 0:w],
                                        tab[:, hh, 0:w], ALU.mult).then_inc(S("r_sfree", 4), 1)
                    dve.drain().then_inc(S("r_st", 1), 1)
                    dve.wait_ge(S("r_pv"), pair + 1)
                    o = probs[:, 0, :]
                    v.tensor_copy(o, po[:, :]).then_inc(S("r_o"), 1)
                    dve.wait_ge(S("r_mean"), pair + 1)
                    v.tensor_tensor(o, o, pt[:, :], ALU.subtract).then_inc(S("r_d"), 1)
                    dve.wait_ge(S("r_rstd"), pair + 1)
                    v.tensor_tensor(o, o, probs[:, 1, :], ALU.mult)
                    dve.drain()
                    v.tensor_tensor(o, o, wb[:, p + 4, :], ALU.mult)
                    dve.drain()
                    split_here(o, p + 4, "r_y")
                    dve.drain().then_inc(S("r_ofree", 1), 1)
                add_to_x(layer, N_BLOCK1 + O_O, "norm_x")
                norm(l * 3 + 4, l * 3 + 3, "ffn_w", l * KD)

                v.memset(padded[:, 0:2], 0.0)
                done = 0
                for ch, tiles in enumerate(CHUNKS2):
                    first = N_BLOCK1 + O_FFN[ch]
                    with dve.Fori(0, tiles // 2) as i:
                        for j in range(2):
                            n = layer + i * 4 + (first + 2 * j)
                            slot = (first + 2 * j) % 4
                            tile = l * FT2 + i * 2 + (done + j)
                            y_tile = i * 2 + j
                            conv = probs_t[:, 0, :]
                            dve.wait_ge(gemm_done, panel_done(n))
                            v.tensor_copy(padded[:, 2:T + 2], acc[:, slot, :]).then_inc(acc_free, 1)
                            dve.drain()
                            v.tensor_scalar(conv, padded[:, 0:T], par("conv_w", tile * 3), par("conv_b", tile),
                                            ALU.mult, ALU.add)
                            dve.drain()
                            v.scalar_tensor_tensor(conv, padded[:, 1:T + 1], par("conv_w", tile * 3 + 1), conv,
                                                   ALU.mult, ALU.add)
                            dve.drain()
                            v.scalar_tensor_tensor(conv, padded[:, 2:T + 2], par("conv_w", tile * 3 + 2), conv,
                                                   ALU.mult, ALU.add).then_inc(S("h_conv"), 1)
                            dve.wait_ge(S("h_gelu"), tile + 1)
                            dve.wait_ge(gemm_done, panel_done(n + 1))
                            v.tensor_tensor(probs[:, 0, :], acc[:, (slot + 1) % 4, :], probs_t[:, 1, :],
                                            ALU.mult).then_inc(acc_free, 1)
                            dve.drain().then_inc(S("h_h"), 1)
                            low_of_tile("h", tile, probs[:, 0, :], y_hi[:, y_tile, :], y_lo[:, y_tile, :])
                    add_to_x(layer, first + 2 * tiles, "norm_x" if ch == 2 else None)
                    done += tiles
                for k in range(2):
                    dve.wait_ge(S("e_hi"), l * 2 + (k + 1))
                    v.tensor_tensor(y_lo[:, 8 + k, :], wv[:, k, :], y_hi[:, 8 + k, :],
                                    ALU.subtract).then_inc(S("e_split"), 1)
                norm(l * 3 + 5, l * 3 + 4, "ple_w", l * KD)
                evacuate(layer, N_BLOCK1 + O_GATE, 8, lambda i: wa[:, i, :], "e_g")
                dve.wait_ge(S("e_gate"), l * 8 + 8)
                for q in range(3):
                    dve.wait_ge(gemm_done, panel_done(layer + (N_BLOCK1 + O_PLE + q)))
                    w = 3 if q < 2 else 2
                    gate = wa[:, 3 * q:3 * q + w, :]
                    v.tensor_tensor(gate, gate, acc[:, 0:w, :], ALU.mult).then_inc(acc_free, 1)
                    dve.drain()
                    v.tensor_tensor(x[:, 3 * q:3 * q + w, :], x[:, 3 * q:3 * q + w, :], gate, ALU.add)
                dve.drain().then_inc(S("norm_x"), 1)
            dve.wait_ge(S("norm_rstd"), 10)
            for k in range(KD):
                v.scalar_tensor_tensor(wb[:, k, :], x[:, k, :], par("final_g", k), probs[:, 0, :],
                                       ALU.mult, ALU.mult).then_inc(S("out_ready"), 1)

        @blk.gpsimd
        def _(pool):
            for name, start in starts.items():
                pool.sem_inc(sems[name], start)
            pool.sem_inc(started, 1)

            def low(n, slot):
                pool.wait_ge(hi_done, n + 1)
                nc.gpsimd.tensor_tensor(w_lo[:, slot, :], raw[:, slot % 2, :], w_hi[:, slot, :],
                                        ALU.subtract).then_inc(lo_done, 1)

            with pool.Fori(0, N_PANELS // 4) as i:
                for j in range(4):
                    low(i * 4 + j, j)
            for j in range(LOOK):
                low(N_PANELS + j, j)


def constant_arrays():
    i = np.arange(P)
    k, q = i[:, None], i[None, :]
    table = {"ident": k == q, "anti": k + q == P - 1, "ones": np.ones((P, P)), "head_mean": (k // HD == q // HD) / HD}
    table["chunk_mask"] = np.where(q // CHUNK <= k // CHUNK, 0.0, MASKED)
    table["causal_mask"] = np.where(q <= k, 0.0, MASKED)
    rope_c = np.zeros((P, P))
    for r in range(ROPE // 2):
        rope_c[NOPE + ROPE // 2 + r, NOPE + r] = -1.0
        rope_c[NOPE + r, NOPE + ROPE // 2 + r] = 1.0
    rope_r = np.zeros((P, P))
    for h in (0, HD):
        for r in range(HD // 2):
            rope_r[h + HD // 2 + r, h + r] = -1.0
            rope_r[h + r, h + HD // 2 + r] = 1.0
    table["rope_c"], table["rope_r"] = rope_c, rope_r
    consts = np.stack([np.asarray(table[n], np.float32) for n in CONSTS], 1)
    masks = np.stack([(k // (2 * h) == q // (2 * h)) & (k % (2 * h) < h) & (q % (2 * h) >= h)
                      for h in LEVELS[3:]], 1).astype(np.float32)
    freq = np.float32(10000.0) ** (-np.arange(0, HD, 2, dtype=np.float32) / np.float32(HD))
    ang = np.arange(T, dtype=np.float32)[None, :] * freq.astype(np.float32)[i % (HD // 2)][:, None]
    rotary = np.stack([np.sin(ang.astype(np.float64)), np.cos(ang.astype(np.float64))], 1).astype(np.float32)
    log_gamma = np.log1p(-(2.0 ** (-5.0 - np.arange(HEADS))))
    rel = np.arange(T)[None, :] - k
    decay = np.where(rel >= 0, HD ** -0.5 * np.exp(log_gamma[:, None, None] * np.maximum(rel, 0)), 0.0)
    decay = decay.reshape(PAIRS, 2, P, T).transpose(0, 2, 1, 3).astype(np.float32)
    inv_freq = np.zeros((P, 1), np.float32)
    inv_freq[NOPE:QH, 0] = np.tile(np.float32(10000.0) ** (-np.arange(0, ROPE, 2, dtype=np.float32) / np.float32(ROPE)), 2)
    return {"consts": consts, "masks": masks, "rotary": rotary, "decay": decay}, inv_freq


def columns(a, rows=P):
    return np.moveaxis(a.reshape(*a.shape[:-1], -1, rows), -1, 0).reshape(rows, -1)


def feature_panels(w, width=P):
    k, m = w.shape[0] // P, w.shape[1] // width
    return w.reshape(k, P, m, width).transpose(2, 1, 0, 3).reshape(m, P, k * width)


def value_panels(w):
    per = min(2, w.shape[0] // P)
    return w.reshape(-1, per, P, 512).transpose(0, 2, 1, 3).reshape(-1, P, per * 512)


def padded_columns(w, first):
    out = np.zeros((w.shape[0], P), w.dtype)
    out[:, first:first + w.shape[1]] = w
    return out


def lay_out(a):
    arrays, inv_freq = constant_arrays()
    f = lambda v: np.asarray(v)
    w = f(a["w_in"])[0]
    s = np.cumsum([0, 512, 512, 512, 512, 512, 512, 512, QR, KVR, ROPE, 3 * D])
    aq, ak, av, bq, bf, bi, bg, cq, ckv, ckr, gates = (w[:, s[i]:s[i + 1]] for i in range(11))
    cat = np.concatenate
    arrays["w_in1"] = cat([feature_panels(aq), feature_panels(ak), value_panels(av), feature_panels(bq),
                           feature_panels(bf), feature_panels(bg), value_panels(bi), feature_panels(cq),
                           feature_panels(ckv), feature_panels(padded_columns(ckr, NOPE))])
    arrays["w_c_q"] = feature_panels(f(a["mla_w_uq"])[0], QH).reshape(2, 4, P, 2 * QH).transpose(0, 2, 1, 3).reshape(2, P, -1)
    ukv = f(a["mla_w_ukv"])[0].reshape(KVR, HEADS, 2, HD)
    arrays["w_c_kv"] = np.stack([ukv[:, :, 0].reshape(P, 512), ukv[:, :, 1].reshape(P, 512)])
    gate = feature_panels(gates).reshape(3, KD, P, 1024).transpose(1, 0, 2, 3)
    branch = np.stack([feature_panels(f(a["w_branch"])[0, b]) for b in range(3)], 1)
    arrays["w_gate"], arrays["w_branch"] = gate.reshape(24, P, 1024), branch.reshape(24, P, 512)
    ff1 = feature_panels(f(a["w_ff1"])[0]).reshape(4, 8, P, 1024)
    ff2 = np.stack([feature_panels(part) for part in f(a["w_ff2"])[0].reshape(4, D, D)])
    arrays["w_rest1"] = cat([feature_panels(f(a["w_out"])[0]), cat([ff1, ff2], 1).reshape(64, P, 1024)])
    layers = {n: [] for n in SEGMENTS2}
    for l in range(LAYERS):
        w = f(a["w_in_2"])[l]
        s = np.cumsum([0, 512, 512, 512, HEADS, 512, 512, 512, 512])
        fq, fk, fv, fl, rq, rk, rv, rg = (w[:, s[i]:s[i + 1]] for i in range(8))
        up, down = f(a["w_up_2"])[l], f(a["w_down_2"])[l]
        both = np.stack([feature_panels(up[:, :FF2]), feature_panels(up[:, FF2:])], 1)
        wide, narrow, at = [], [], 0
        for tiles in CHUNKS2:
            part = [both[at:at + tiles].reshape(-1, P, 1024), feature_panels(down[at * P:(at + tiles) * P])]
            if tiles == 8:
                wide += part
            else:
                wide.append(part[0])
                narrow.append(part[1])
            at += tiles
        layers["in2"].append(cat([feature_panels(padded_columns(fl, 0)), feature_panels(fq), feature_panels(fk),
                                  value_panels(fv), feature_panels(rq), feature_panels(rk), feature_panels(rg),
                                  value_panels(rv), feature_panels(f(a["w_out_2"])[l])]))
        layers["ffn_wide"].append(cat(wide))
        layers["ffn_narrow"].append(cat(narrow))
        layers["ple_gate"].append(feature_panels(f(a["w_ple_gate_2"])[l]))
        proj = feature_panels(f(a["w_ple_proj_2"])[l])
        layers["ple_a"].append(proj[0:6].reshape(2, 3, P, 256).transpose(0, 2, 1, 3).reshape(2, P, 768))
        layers["ple_b"].append(proj[6:8].transpose(1, 0, 2).reshape(1, P, 512))
    for n, parts in layers.items():
        arrays["w_" + n] = np.stack(parts)
    r = f(a["rel_bias"])[0][:, ::-1]
    ext = r[:, np.clip(np.arange(640) - (T - 1) + A_REL, 0, 2 * A_REL)]
    arrays["bias"] = ext
    arrays["x"] = f(a["x"])[0].T.reshape(KD, P, T).transpose(1, 0, 2)
    arrays["p"] = f(a["p_2"])[:, 0].transpose(0, 2, 1).reshape(LAYERS, 2, P, T).transpose(0, 2, 1, 3)
    arrays["positions"] = f(a["positions"])[0]
    one = np.ones((P, 1), np.float32)
    bias8 = np.zeros((P, LAYERS), np.float32)
    bias8[:HEADS] = f(a["forget_bias_2"]).T
    conv_w = f(a["conv_w_2"]).reshape(LAYERS, 3, FT2, P).transpose(3, 0, 2, 1).reshape(P, -1)
    parts = {"one": one, "eps": one * np.float32(EPS), "gn_eps": one * np.float32(GN_EPS), "inv_freq": inv_freq,
             "mix_g": columns(f(a["norm_mix_g"])), "ffn_g": columns(f(a["norm_ffn_g"])),
             "q_g": columns(f(a["mla_q_norm_g"])), "kv_g": columns(f(a["mla_kv_norm_g"])),
             "hgrn_g": cat([f(a["hgrn_norm_g"])[0]] * 2)[:, None], "lb": columns(f(a["hgrn_lb_logits"])),
             "mid_g": columns(f(a["final_norm_g"])), "final_g": columns(f(a["final_norm_w_2"])), "attn_w": columns(f(a["attn_norm_w_2"])),
             "ffn_w": columns(f(a["ffn_norm_w_2"])), "ple_w": columns(f(a["ple_norm_w_2"])), "f_bias": bias8,
             "conv_b": columns(f(a["conv_b_2"])), "conv_w": conv_w}
    arrays["params"] = cat([parts[n] for n in PARAMS], 1)
    return {n: np.ascontiguousarray(v) for n, v in arrays.items()}


def program(nc, arrays):
    dram = {}
    for n, v in arrays.items():
        dram[n] = nc.dram_tensor("in_" + n, v.shape, mybir.dt.from_np(v.dtype), kind="ExternalInput").ap()
    ext = dram["bias"]
    dram["bias"] = BiasWindows(ext)
    out = nc.dram_tensor("out", (D, T), F32, kind="ExternalOutput").ap()
    build(nc, dram, out)


class BiasWindows:

    def __init__(self, ext):
        self.ext = ext

    def __getitem__(self, pair):
        rows = self.ext[bass.ds(pair * 2, 2), 0:T]
        return bass.AP(rows.tensor, rows.offset, [[1, P], [640, 2], [1, T]])


def kernel(**inputs):
    import concourse.bacc as bacc
    from concourse.bass_utils import run_bass_kernel_spmd

    arrays = lay_out(inputs)
    nc = bacc.Bacc("TRN2", target_bir_lowering=False, num_devices=1)
    program(nc, arrays)
    r = run_bass_kernel_spmd(nc, [{"in_" + n: v for n, v in arrays.items()}], core_ids=[0])
    return r.results[0]["out"].T.reshape(1, T, D)
```

```python
import numpy as np

import concourse.bass as bass
from concourse import mybir

F32 = mybir.dt.float32
F32R = mybir.dt.float32r
U32 = mybir.dt.uint32
I32 = mybir.dt.int32
ALU = mybir.AluOpType
ACT = mybir.ActivationFunctionType
AX = mybir.AxisListType

P = 128
T = 512
D = 1024
KD = D // P
TT = T // P
HEADS = 8
PAIRS = HEADS // 2
HD = 64
CHUNK = 64
EPS = 1e-6
GN_EPS = 1e-5
LAYERS = 2
FF1 = 4 * D
FF2 = -(-8 * D // (3 * 128)) * 128
FT2 = FF2 // P
CHUNKS2 = (8, 8, FT2 - 16)
A_REL = 128
QR, KVR, NOPE, ROPE = 256, 128, 64, 32
QH = NOPE + ROPE
MASKED = -1.0e30
LEVELS = (0, 256, 128, 64, 32, 16, 8, 4, 2, 1)
LOOK = 2

N_A, N_B, N_C, N_UP, N_MERGE, N_O, N_FF = 0, 12, 28, 32, 36, 84, 92
N_BLOCK1 = N_FF + 64
O_FL, O_F, O_R, O_O = 0, 1, 13, 29
O_FFN = (37, 61, 85)
O_GATE, O_PLE = 105, 113
PER_LAYER = 116
N_PANELS = N_BLOCK1 + LAYERS * PER_LAYER
SEGMENTS1 = ["in1", "c_q", "c_kv"]
SEGMENTS2 = ["in2", "ffn_wide", "ffn_narrow", "ple_gate", "ple_a", "ple_b"]

CONSTS = ["ident", "anti", "ones", "head_mean", "mask", "rope"]
N_MASKS = 7
PARAMS = {}
for _name, _n in [("one", 1), ("eps", 1), ("gn_eps", 1), ("inv_freq", 1), ("mix_g", KD), ("ffn_g", KD), ("q_g", 2), ("kv_g", 1),
                  ("hgrn_g", 1), ("lb", PAIRS), ("mid_g", KD), ("final_g", KD), ("attn_w", LAYERS * KD), ("ffn_w", LAYERS * KD),
                  ("ple_w", LAYERS * KD), ("f_bias", LAYERS), ("conv_b", LAYERS * FT2), ("conv_w", LAYERS * FT2 * 3)]:
    PARAMS[_name] = (sum(n for _, n in PARAMS.values()), _n)
N_PARAMS = sum(n for _, n in PARAMS.values())


def build(nc, dram, out):
    offset = {}

    def sb(name, shape, dt=F32):
        offset[name] = nc.sbuf_base
        return nc.alloc_sbuf_tensor(name, shape, dt)

    def alias(name, base, shape, dt=F32, skip=0):
        return nc.alloc_sbuf_tensor_at(name, shape, dt, offset=offset[base] + skip)

    x = sb("x", [P, KD, T])
    act_hi = sb("act_hi", [P, KD, T], F32R)
    act_lo = sb("act_lo", [P, KD, T], F32R)
    raw = sb("raw", [P, 2, 1024])
    w_hi = sb("w_hi", [P, 4, 1024], F32R)
    w_lo = sb("w_lo", [P, 4, 1024], F32R)
    y_hi = sb("y_hi", [P, 12, T], F32R)
    y_lo = sb("y_lo", [P, 12, T], F32R)
    wa = sb("wa", [P, 8, T])
    wb = sb("wb", [P, 8, T])
    wv = sb("wv", [P, TT, T])
    qcur = sb("qcur", [P, 2, T])
    kcur = sb("kcur", [P, 2, T])
    vcur = sb("vcur", [P, TT, P])
    probs = sb("probs", [P, 2, T])
    probs_t = sb("probs_t", [P, 2, T])
    tab = sb("tab", [P, 2, T])
    consts = sb("consts", [P, len(CONSTS), P])
    masks = sb("masks", [P, N_MASKS, P])
    params = sb("params", [P, N_PARAMS])
    cols = sb("cols", [P, 16])
    rstd = sb("rstd", [P, T])
    c = {n: consts[:, i, :] for i, n in enumerate(CONSTS)}
    neg_max = [cols[:, 0:1], cols[:, 1:2]]
    prob_sum = [cols[:, 2:3], cols[:, 3:4]]
    inv_sum = [cols[:, 8:9], cols[:, 9:10]]
    lower, rest = cols[:, 4:8], cols[:, 10:14]
    merged_hi = alias("merged_hi", "wa", [P, KD, T], F32R)
    merged_lo = alias("merged_lo", "wb", [P, KD, T], F32R)
    positions = alias("positions", "vcur", [P, T], I32)
    tail = 8 * T * 4
    decay_tmp = alias("decay_tmp", "y_hi", [P, T], skip=tail)
    s_diag = alias("s_diag", "y_hi", [P, 2, TT, P], skip=tail)
    s_256 = alias("s_256", "y_hi", [P, 2, 2, 256], skip=tail + 2 * T * 4)
    s_128 = alias("s_128", "y_lo", [P, 2, 2, P], skip=tail)
    cums = alias("cums", "y_lo", [P, 3, T], skip=tail + T * 4)
    resets = alias("resets", "probs", [P, 3, T])
    s_ret = [alias("s_ret0", "y_hi", [P, 1280], skip=tail), alias("s_ret1", "y_lo", [P, 1280], skip=tail)]
    s_off = (0, 512, 896, 1152)
    augq, augk = wb[0:2, 0:2, :], wb[0:2, 2:4, :]
    padded = alias("padded", "tab", [P, T + 2])

    acc = nc.alloc_psum_tensor("acc", [P, 4, T], F32)
    sc = nc.alloc_psum_tensor("sc", [P, 2, T], F32)
    po = nc.alloc_psum_tensor("po", [P, T], F32)
    pt = nc.alloc_psum_tensor("pt", [P, T], F32)
    vstage = qcur[:, 1, :]
    lev_bank = [sc[:, 0, :], sc[:, 1, :], acc[:, 0, :], acc[:, 1, :]]
    cum_dram = nc.dram_tensor("cum_dram", (2, HEADS, T), F32).ap()

    def par(name, i=0, rows=P):
        first = PARAMS[name][0]
        if isinstance(i, int):
            return params[0:rows, first + i:first + i + 1]
        return params[0:rows, bass.ds(i + first, 1)]

    sems, starts = {}, {}

    def S(name, start=0):
        if name not in sems:
            sems[name] = nc.alloc_semaphore(name)
            if start:
                starts[name] = start
        assert starts.get(name, 0) == start, name
        return sems[name]

    started = S("started")
    passed = S("passed")
    raw_loaded = [S("raw_loaded0"), S("raw_loaded1")]
    hi_done = S("hi_done")
    lo_done = S("lo_done", 2)
    gemm_done = S("gemm_done", 4)
    acc_free = S("acc_free", 4)

    def high_free(n):
        return n + 1

    def settle(eng):
        eng.sem_inc(passed, 1)

    def panel_done(n):
        return n + 5

    block = nc.Block()
    with block as blk:

        @blk.sync
        def _(sp):
            sp.wait_ge(started, 1)

            def load(src, layer, first, count):
                width = src.shape[-1]

                def one(i, number, slot):
                    sp.wait_ge(lo_done, layer + number + 1)
                    sp.dma_start(raw[:, slot, 0:width], src[i]).then_inc(raw_loaded[slot], 16)

                pairs = count // 2 if count >= 4 else 0
                if pairs:
                    with sp.Fori(0, pairs) as i:
                        for j in range(2):
                            one(i * 2 + j, i * 2 + (first + j), (first + j) % 2)
                for j in range(2 * pairs, count):
                    one(j, first + j, (first + j) % 2)
                return first + count

            n = 0
            for name in SEGMENTS1:
                n = load(dram["w_" + name], 0, n, dram["w_" + name].shape[0])
            assert n == N_MERGE
            with sp.Fori(0, 24) as i:
                sp.wait_ge(lo_done, i * 2 + (N_MERGE + 1))
                sp.dma_start(raw[:, 0, :], dram["w_gate"][i]).then_inc(raw_loaded[0], 16)
                sp.wait_ge(lo_done, i * 2 + (N_MERGE + 2))
                sp.dma_start(raw[:, 1, 0:512], dram["w_branch"][i]).then_inc(raw_loaded[1], 16)
            load(dram["w_rest1"], 0, N_O, 8 + 64)
            with sp.Fori(0, LAYERS) as l:
                n = N_BLOCK1
                for name in SEGMENTS2:
                    src = dram["w_" + name][l]
                    n = load(src, l * PER_LAYER, n, src.shape[0])
                assert n == N_BLOCK1 + PER_LAYER
            load(dram["w_in1"][0:LOOK], 0, N_PANELS, LOOK)
            sp.wait_ge(lo_done, N_PANELS + LOOK + 2)

        @blk.tensor
        def _(pe):
            pe.wait_ge(started, 1)
            pe.wait_ge(S("const_loaded"), 48)

            def products(dst, w, src, start, stop):
                nc.tensor.matmul(dst, w[0], src[0], start=start, stop=False)
                nc.tensor.matmul(dst, w[0], src[1], start=False, stop=False)
                return nc.tensor.matmul(dst, w[1], src[0], start=False, stop=stop)

            def tile_products(dst, slot, unit, width, k_tiles, src, base=0, ready=None, part=None):
                for k in part or range(k_tiles):
                    if ready:
                        pe.wait_ge(ready[0], ready[1] + (k + 1))
                    cut = slice(unit + k * width, unit + (k + 1) * width)
                    last = products(dst, (w_hi[:, slot, cut], w_lo[:, slot, cut]),
                                    (src[0][:, base + k, :], src[1][:, base + k, :]), k == 0, k == k_tiles - 1)
                return last

            act_in, y_in, merged_in = (act_hi, act_lo), (y_hi, y_lo), (merged_hi, merged_lo)

            def gemm(layer, first, count, k_tiles, src, ready=None):
                def one(n, slot, ready):
                    pe.wait_ge(lo_done, n + 3)
                    pe.wait_ge(acc_free, n + 1)
                    tile_products(acc[:, slot, :], slot, 0, P, k_tiles, src, 0, ready).then_inc(gemm_done, 1)

                fours = count // 4 if count >= 8 else 0
                if fours:
                    with pe.Fori(0, fours) as i:
                        for j in range(4):
                            one(layer + i * 4 + (first + j), (first + j) % 4, ready if j == 0 else None)
                for j in range(4 * fours, count):
                    one(layer + (first + j), (first + j) % 4, ready if j == 0 else None)

            def transpose_values(name, pair, bank):
                for t in range(TT):
                    last = nc.tensor.transpose(bank[:, t * P:(t + 1) * P], vstage[:, t * P:(t + 1) * P], c["ident"])
                last.then_inc(S(name + "_vt"), 1)

            def norm(r):
                pe.wait_ge(S("norm_total"), r + 1)
                nc.tensor.matmul(sc[:, 0, :], c["ones"], probs[:, 0, :], start=True, stop=True).then_inc(S("norm_sum"), 1)

            def normed_gemm(layer, first, count, r, split):
                gemm(layer, first, 1, KD, act_in, (S("norm_split"), split * 8))
                norm(r)
                gemm(layer, first + 1, count - 1, KD, act_in)

            def softmax_pair(pair, scores_of, values=None, guest=None):
                unit0 = pair * 8

                def outputs(u):
                    hh, qt = divmod(u, 4)
                    rows = slice(HD * hh, HD * hh + HD)
                    pe.wait_ge(S("soft_tcopy", 1), unit0 + (u + 2))
                    if u == 0:
                        pe.wait_ge(S("soft_ofree", 1), pair + 1)
                        if values is not None:
                            pe.wait_ge(S("soft_v"), values + 1)
                    for kb in range(qt + 1):
                        last = nc.tensor.matmul(po[rows, qt * P:(qt + 1) * P], vcur[:, kb, rows],
                                                probs_t[:, u % 2, kb * P:(kb + 1) * P], start=kb == 0, stop=kb == qt)
                    last.then_inc(S("soft_pv", 2), 1)

                def transposes(u):
                    pe.wait_ge(S("soft_p"), unit0 + (u + 1))
                    pe.wait_ge(S("soft_tcopy", 1), unit0 + (u + 1))
                    for kb in range(u % 4 + 1):
                        last = nc.tensor.transpose(pt[:, kb * P:(kb + 1) * P], probs[:, u % 2, kb * P:(kb + 1) * P],
                                                   c["ident"])
                    last.then_inc(S("soft_t", 2), 1)

                for u in range(8 + 2):
                    if u < 8:
                        pe.wait_ge(S("soft_exp", 2), unit0 + (u + 1))
                        scores_of(u).then_inc(S("soft_s"), 1)
                    if u == 0 and values is not None:
                        pe.wait_ge(S("soft_ofree", 1), pair + 1)
                        transpose_values("soft", pair, po)
                    if u < 8 and guest:
                        guest(u)
                    if 1 <= u <= 8:
                        transposes(u - 1)
                    if u >= 2:
                        outputs(u - 2)

            def guest_panels(n0, slot0):
                def half(u):
                    n, slot = n0 + u // 2, (slot0 + u // 2) % 4
                    if u % 2 == 0:
                        pe.wait_ge(lo_done, n + 3)
                        pe.wait_ge(acc_free, n + 1)
                        tile_products(acc[:, slot, :], slot, 0, P, KD, act_in, part=range(0, 4))
                    else:
                        tile_products(acc[:, slot, :], slot, 0, P, KD, act_in, part=range(4, KD)).then_inc(gemm_done, 1)
                return half

            def head_scores(u, wide):
                hh, qt = divmod(u, 4)
                kw = (qt + 1) * P
                rows, b = (slice(0, QH), hh) if wide else (slice(HD * hh, HD * hh + HD), 0)
                nc.tensor.matmul(sc[:, u % 2, 0:kw], qcur[rows, b, qt * P:kw], kcur[rows, b, 0:kw],
                                 start=True, stop=False)
                return hh, qt, kw

            def add_mask(u, qt, name):
                return nc.tensor.matmul(sc[:, u % 2, qt * P:(qt + 1) * P], c["ident"], c[name], start=False, stop=True)

            def scores_a(u):
                hh, qt, kw = head_scores(u, False)
                nc.tensor.matmul(sc[:, u % 2, 0:kw], c["anti"], tab[:, hh, T - kw:T], start=False, stop=False)
                return add_mask(u, qt, "mask")

            def scores_c(u):
                hh, qt, kw = head_scores(u, True)
                return add_mask(u, qt, "mask")

            def scores_f(u):
                hh, qt, kw = head_scores(u, False)
                nc.tensor.matmul(sc[:, u % 2, 0:kw], augq[:, hh, qt * P:kw], augk[:, hh, 0:kw],
                                 start=False, stop=False)
                return add_mask(u, qt, "mask")

            def linear_outputs(name, pair, piece):
                pe.wait_ge(S(name + "_st", 1), pair + 2)
                pe.wait_ge(S(name + "_ofree", 1), pair + 1)
                for hh in range(2):
                    rows = slice(HD * hh, HD * hh + HD)
                    for it in range(TT):
                        for jt in range(it + 1):
                            last = nc.tensor.matmul(po[rows, it * P:(it + 1) * P], vcur[:, jt, rows],
                                                    piece(hh, jt, it), start=jt == 0, stop=jt == it)
                last.then_inc(S(name + "_pv"), 1)

            def head_mean(ready, done, r, src):
                pe.wait_ge(S(ready), r + 1)
                nc.tensor.matmul(pt[:, :], c["head_mean"], src, start=True, stop=True).then_inc(S(done), 1)

            normed_gemm(0, N_A, 12, 0, 0)
            with pe.Fori(0, PAIRS) as p:
                pe.wait_ge(S("soft_stage"), p + 1)
                pe.wait_ge(S("a_bias"), p * 16 + 16)
                softmax_pair(p, scores_a, p, guest_panels(p * 4 + N_B, N_B))
            pe.wait_ge(acc_free, N_C + 4)

            def hgrn_piece(hh, jt, it):
                if jt == it:
                    return s_diag[:, hh, jt, :]
                if it // 2 == jt // 2:
                    return s_128[:, hh, jt // 2, :]
                return s_256[:, hh, jt, (it - 2) * P:(it - 1) * P]

            with pe.Fori(0, PAIRS) as p:
                pe.wait_ge(S("b_stage"), p + 1)
                pe.wait_ge(S("b_ofree", 1), p + 1)
                transpose_values("b", p, po)
                for v, half in enumerate(LEVELS):
                    if v:
                        pe.wait_ge(S("b_x"), p * 9 + v)
                    for hh in range(2):
                        rows = slice(HD * hh, HD * hh + HD)
                        unit = 2 * v + hh
                        bank = lev_bank[unit % 4]
                        pe.wait_ge(S("b_sfree", 4), p * 20 + (unit + 1))
                        if half == 0:
                            cuts = [(kcur[rows, 0, t * P:(t + 1) * P], qcur[rows, 0, t * P:(t + 1) * P], P)
                                    for t in range(TT)]
                        elif half == 256:
                            cuts = [(tab[rows, v % 2, t * P:(t + 1) * P], tab[rows, v % 2, 256:512], 256)
                                    for t in range(2)]
                        elif half == 128:
                            cuts = [(tab[rows, v % 2, t * 256:t * 256 + P], tab[rows, v % 2, t * 256 + P:(t + 1) * 256], P)
                                    for t in range(2)]
                        else:
                            cuts = [(tab[rows, v % 2, t * P:(t + 1) * P], tab[rows, v % 2, t * P:(t + 1) * P], P)
                                    for t in range(TT)]
                        for t, (keys, queries, w) in enumerate(cuts):
                            last = nc.tensor.matmul(bank[:, t * w:(t + 1) * w], keys, queries, start=True, stop=True)
                        last.then_inc(S("b_s"), 1)
                linear_outputs("b", p, hgrn_piece)
                head_mean("b_sq", "b_mean", p, kcur[:, 1, :])
            pe.wait_ge(S("b_ofree", 1), PAIRS + 1)

            gemm(0, N_C, 4, KD, act_in)
            for first, count in ((0, 2), (2, 1)):
                for k in range(first, first + count):
                    pe.wait_ge(S("c_sq"), k + 1)
                    last = nc.tensor.matmul(sc[:, first // 2, :], c["ones"], wb[:, k, :],
                                            start=k == first, stop=k == first + count - 1)
                last.then_inc(S("c_sum"), 1)
            pe.wait_ge(S("c_rotin"), 1)
            nc.tensor.matmul(po[:, :], c["rope"], wv[:, 3, :], start=True, stop=True).then_inc(S("c_rot"), 1)
            pe.wait_ge(S("cn_split"), 3)
            for q in range(2):
                n, slot = N_UP + q, (N_UP + q) % 4
                pe.wait_ge(lo_done, n + 3)
                pe.wait_ge(acc_free, n + 4)
                for h in range(4):
                    last = tile_products(acc[0:QH, h, :], slot, h * 2 * QH, QH, 2, y_in, 8)
                last.then_inc(gemm_done, 1)
            n, slot = N_UP + 2, (N_UP + 2) % 4
            pe.wait_ge(lo_done, n + 3)
            pe.wait_ge(acc_free, n + 4)
            for h in range(4):
                last = tile_products(acc[:, h, :], slot, h * P, P, 1, y_in, 10)
            last.then_inc(gemm_done, 1)
            n, slot = N_UP + 3, (N_UP + 3) % 4
            pe.wait_ge(lo_done, n + 3)
            pe.wait_ge(acc_free, n + 4)
            for t in range(TT):
                cut = slice(t * P, (t + 1) * P)
                last = products(acc[:, t, :], (y_hi[:, 10, cut], y_lo[:, 10, cut]),
                                (w_hi[:, slot, 0:512], w_lo[:, slot, 0:512]), True, True)
            last.then_inc(gemm_done, 1)
            for h in range(HEADS):
                pe.wait_ge(S("c_rotin"), 2 + h // 4)
                pe.wait_ge(S("c_rotused"), 1 + h)
                nc.tensor.matmul(po[0:QH, :], consts[0:QH, CONSTS.index("rope"), 0:QH], wa[0:QH, h, :],
                                 start=True, stop=True).then_inc(S("c_rot"), 1)
            pe.wait_ge(S("c_rotused"), 1 + HEADS)
            with pe.Fori(0, PAIRS) as p:
                pe.wait_ge(S("soft_stage"), p + 5)
                softmax_pair(p + 4, scores_c)

            pe.wait_ge(S("soft_y"), 2 * PAIRS)
            with pe.Fori(0, 4) as i:
                for j in range(12):
                    n, slot = i * 12 + (N_MERGE + j), (N_MERGE + j) % 4
                    pe.wait_ge(lo_done, n + 3)
                    pe.wait_ge(acc_free, n + 1)
                    if j % 2 == 0:
                        last = tile_products(acc[:, slot, :], slot, 0, P, KD, act_in)
                    else:
                        last = tile_products(acc[:, slot, :], slot, 0, P, 4, y_in, 4 * (j // 2 % 3))
                    last.then_inc(gemm_done, 1)
            gemm(0, N_O, 8, KD, merged_in, (S("m_split"), 0))
            norm(1)
            with pe.Fori(0, 4) as i:
                gemm(i * 16, N_FF, 8, KD, act_in, (S("norm_split"), 8))
                gemm(i * 16, N_FF + 8, 8, KD, y_in, (S("g_split"), i * 8))
            norm(2)
            pe.wait_ge(S("const_loaded"), 64)

            with pe.Fori(0, LAYERS) as l:
                layer = l * PER_LAYER
                normed_gemm(layer, N_BLOCK1 + O_FL, 13, l * 3 + 3, l * 3 + 2)
                with pe.Fori(0, PAIRS) as p:
                    pair = l * 4 + p
                    pe.wait_ge(S("soft_stage"), pair + 9)
                    pe.wait_ge(S("f_aug"), pair * 32 + 32)
                    softmax_pair(pair + 8, scores_f, pair + 4,
                                 guest_panels(layer + p * 4 + (N_BLOCK1 + O_R), O_R))
                pe.wait_ge(acc_free, layer + (N_BLOCK1 + O_O + 4))
                pe.wait_ge(S("soft_ofree", 1), l * 4 + 13)
                settle(pe)
                with pe.Fori(0, PAIRS) as p:
                    pair = l * 4 + p
                    pe.wait_ge(S("r_ofree", 1), pair + 1)
                    nc.tensor.matmul(po[:, :], c["rope"], wa[:, p, :], start=True, stop=True).then_inc(S("r_rot"), 1)
                    nc.tensor.matmul(pt[:, :], c["rope"], wa[:, p + 4, :], start=True, stop=True).then_inc(S("r_rot"), 1)
                    pe.wait_ge(S("r_stage"), pair + 1)
                    transpose_values("r", pair, acc[:, 2, :])
                    for u in range(8):
                        hh, jt = divmod(u, 4)
                        rows = slice(HD * hh, HD * hh + HD)
                        pe.wait_ge(S("r_sfree", 4), pair * 8 + (u + 1))
                        nc.tensor.matmul(lev_bank[u % 4][:, 0:T - jt * P], kcur[rows, 0, jt * P:(jt + 1) * P],
                                         qcur[rows, 0, jt * P:T], start=True, stop=True).then_inc(S("r_s"), 1)
                    linear_outputs("r", pair,
                                   lambda hh, jt, it: s_ret[hh][:, s_off[jt] + (it - jt) * P:
                                                                s_off[jt] + (it - jt + 1) * P])
                    head_mean("r_o", "r_mean", pair, probs[:, 0, :])
                    head_mean("r_sq", "r_var", pair, probs_t[:, 0, :])
                pe.wait_ge(S("r_y"), l * 4 + 4)
                settle(pe)
                gemm(layer, N_BLOCK1 + O_O, 8, KD, y_in)
                done = 0
                for ch, tiles in enumerate(CHUNKS2):
                    first = N_BLOCK1 + O_FFN[ch]
                    if ch == 0:
                        normed_gemm(layer, first, 2 * tiles, l * 3 + 4, l * 3 + 3)
                    else:
                        gemm(layer, first, 2 * tiles, KD, act_in)
                    gemm(layer, first + 2 * tiles, 8, tiles, y_in, (S("h_split"), l * FT2 + done))
                    done += tiles
                normed_gemm(layer, N_BLOCK1 + O_GATE, 8, l * 3 + 5, l * 3 + 4)
                pe.wait_ge(S("e_split"), l * 2 + 2)
                for q in range(3):
                    n, slot = layer + (N_BLOCK1 + O_PLE + q), (O_PLE + q) % 4
                    pe.wait_ge(lo_done, n + 3)
                    pe.wait_ge(acc_free, n + 4)
                    for m in range(3 if q < 2 else 2):
                        last = tile_products(acc[:, m, :], slot, m * 2 * P, P, 2, y_in, 8)
                    last.then_inc(gemm_done, 1)
            norm(9)

        @blk.scalar
        def _(act):
            act.dma_start(consts[:, :, :], dram["consts"]).then_inc(S("const_loaded"), 16)
            act.dma_start(masks[:, :, :], dram["masks"]).then_inc(S("const_loaded"), 16)
            act.dma_start(params[:, :], dram["params"]).then_inc(S("const_loaded"), 16)
            act.dma_start(x[:, :, :], dram["x"]).then_inc(S("x_loaded"), 16)
            act.wait_ge(started, 1)

            def high(half, full, number):
                act.wait_ge(raw_loaded[number % 2], (half + number // 2) * 16 + 16)
                act.wait_ge(gemm_done, high_free(full + number))
                nc.scalar.copy(w_hi[:, number % 4, :], raw[:, number % 2, :]).then_inc(hi_done, 1)

            def split_ahead(half, full, first, count, body=None):
                fours = count // 4 if count >= 8 else 0
                if fours:
                    with act.Fori(0, fours) as i:
                        for j in range(4):
                            high(half + i * 2, full + i * 4, first + LOOK + j)
                            if body:
                                body(i * 4 + j, j % 2)
                for j in range(4 * fours, count):
                    high(half, full, first + LOOK + j)
                    if body:
                        body(j, j % 2)

            def high_of_tile(name, k, dst, src):
                act.wait_ge(S(name + "_h"), k + 1)
                nc.scalar.copy(dst, src).then_inc(S(name + "_hi"), 1)

            def factor(dst, src, scale, eps):
                nc.scalar.activation(dst, src, ACT.Ln, bias=par(eps), scale=scale)
                act.drain()
                return nc.scalar.activation(dst, dst, ACT.Exp, scale=-0.5)

            def norm_tile(r, k, odd, split=None, gains=None, i0=0):
                if isinstance(r, int) and r == 0:
                    if k == 0:
                        act.wait_ge(S("x_loaded"), 16)
                else:
                    act.wait_ge(S("norm_x"), (r - 1) * 8 + k + 1)
                    settle(act)
                if split is not None:
                    nc.scalar.activation(act_hi[:, k, :], x[:, k, :], ACT.Copy,
                                         scale=par(gains, i0 + k)).then_inc(S("norm_hi"), 1)
                act.wait_ge(S("norm_added", 2), r * 8 + k + 1)
                settle(act)
                nc.scalar.activation(probs_t[:, odd, :], x[:, k, :], ACT.Square).then_inc(S("norm_sq"), 1)

            def norm_factor(r):
                act.wait_ge(S("norm_sum"), r + 1)
                factor(rstd[:, :], sc[:, 0, :], 1.0 / D, "eps").then_inc(S("norm_rstd"), 1)

            def norm(r, split=None, gains=None, i0=0):
                for k in range(KD):
                    norm_tile(r, k, k % 2, split, gains, i0)
                norm_factor(r)

            def softmax_pair(pair, guest=None, work=None):
                unit0 = pair * 8

                def expo(u):
                    kw = (u % 4 + 1) * P
                    act.wait_ge(S("soft_max"), unit0 + (u + 1))
                    act.wait_ge(S("soft_t", 2), unit0 + (u + 1))
                    nc.scalar.activation(probs[:, u % 2, 0:kw], sc[:, u % 2, 0:kw], ACT.Exp, bias=neg_max[u % 2],
                                         accum_out=prob_sum[u % 2]).then_inc(S("soft_exp", 2), 1)

                def copy_t(u):
                    kw = (u % 4 + 1) * P
                    act.wait_ge(S("soft_t", 2), unit0 + (u + 3))
                    act.wait_ge(S("soft_pv", 2), unit0 + (u + 1))
                    nc.scalar.copy(probs_t[:, u % 2, 0:kw], pt[:, 0:kw]).then_inc(S("soft_tcopy", 1), 1)

                for u in range(9):
                    if u < 8:
                        expo(u)
                        if guest and u % 2 == 0:
                            guest(u // 2)
                    if u >= 1:
                        copy_t(u - 1)
                    if work:
                        work(u)

            def in_place(func, ready, done, k, tile, **kw):
                act.wait_ge(S(ready), k + 1)
                settle(act)
                nc.scalar.activation(tile, tile, func, **kw).then_inc(S(done), 1)

            high(0, 0, 0)
            high(0, 0, 1)
            act.wait_ge(S("const_loaded"), 48)
            norm(0, 0, "mix_g")
            in_place(ACT.Exp, "b_lb", "b_lbexp", 0, lower)
            split_ahead(0, 0, N_A, 12)
            with act.Fori(0, PAIRS) as p:
                act.dma_start(tab[:, :, :], dram["bias"][p]).then_inc(S("a_bias"), 16)

                def gates_b(u):
                    tmp = decay_tmp[:, :]
                    if u == 5:
                        act.wait_ge(S("b_z"), p + 1)
                        settle(act)
                        nc.scalar.activation(wa[:, p + 4, :], wb[:, p, :], ACT.Sigmoid, scale=-1.0).then_inc(S("b_key"), 1)
                        nc.scalar.activation(tmp, tmp, ACT.Exp)
                        act.drain()
                        nc.scalar.activation(tmp, tmp, ACT.Ln, bias=par("one")).then_inc(S("b_softplus"), 1)
                    if u == 8:
                        in_place(ACT.Exp, "b_neglog", "b_inv", p, tmp)
                        in_place(ACT.Ln, "b_mixed", "b_mixedlog", p, tmp)
                        in_place(ACT.Silu, "b_g", "b_gsilu", p, wb[:, p + 4, :])
                        nc.scalar.activation(wa[:, p, :], wa[:, p, :], ACT.Silu).then_inc(S("b_qsilu"), 1)

                softmax_pair(p, lambda j: high(p * 2, p * 4, N_B + LOOK + j), gates_b)

            with act.Fori(0, PAIRS) as p:
                for v in range(1, len(LEVELS)):
                    e = kcur[:, 1, :] if v % 2 else qcur[:, 1, :]
                    in_place(ACT.Exp, "b_d", "b_e", p * 9 + (v - 1), e)
                act.wait_ge(S("b_pv"), p + 1)
                act.wait_ge(S("b_st", 1), p + 2)
                nc.scalar.activation(kcur[:, 1, :], po[:, :], ACT.Square).then_inc(S("b_sq"), 1)
                act.wait_ge(S("b_mean"), p + 1)
                factor(qcur[:, 1, :], pt[:, :], 1.0, "eps").then_inc(S("b_rstd"), 1)

            act.dma_start(positions[:, :], dram["positions"].partition_broadcast(P)).then_inc(S("pos_loaded"), 16)
            split_ahead(0, 0, N_C, 4)
            act.wait_ge(S("c_raw"), 3)
            for k in range(3):
                nc.scalar.activation(wb[:, k, :], wv[:, k, :], ACT.Square).then_inc(S("c_sq"), 1)
            act.wait_ge(S("c_sum"), 1)
            act.wait_ge(S("b_ofree", 1), PAIRS + 1)
            factor(probs[:, 0, :], sc[:, 0, :], 1.0 / QR, "eps").then_inc(S("c_rstd"), 1)
            act.wait_ge(S("c_sum"), 2)
            factor(probs[:, 1, :], sc[:, 1, :], 1.0 / KVR, "eps").then_inc(S("c_rstd"), 1)
            for k in range(3):
                high_of_tile("cn", k, y_hi[:, 8 + k, :], wb[:, k, :])
            for k in range(2):
                in_place(ACT.Sin, "c_angle", "c_sincos", k, tab[:, k, :])
            split_ahead(0, 0, N_UP, 4)
            with act.Fori(0, PAIRS) as p:
                softmax_pair(p + 4)

            with act.Fori(0, 4) as i:
                for j in range(12):
                    high(i * 6, i * 12, N_MERGE + LOOK + j)
                    if j % 2 == 0:
                        in_place(ACT.Sigmoid, "m_z", "m_gate", i * 6 + j // 2, probs[:, j // 2 % 2, :])
                    if j % 6 == 5:
                        high_of_tile("m", i * 2 + j // 6, merged_hi[:, i * 2 + j // 6, :], probs_t[:, 1, :])
            split_ahead(0, 0, N_O, 8, lambda k, odd: norm_tile(1, k, odd, 1, "ffn_g"))
            norm_factor(1)
            with act.Fori(0, 4) as i:
                with act.Fori(0, 2) as ii:
                    for j in range(4):
                        high(i * 8 + ii * 2, i * 16 + ii * 4, N_FF + LOOK + j)
                        high_of_tile("g", i * 8 + ii * 4 + j, y_hi[:, ii * 4 + j, :], probs[:, 0, :])
                split_ahead(i * 8, i * 16, N_FF + 8, 8)
            act.dma_start(consts[:, 4:6, :], dram["consts2"]).then_inc(S("const_loaded"), 16)
            norm(2)

            with act.Fori(0, LAYERS) as l:
                half, full = l * (PER_LAYER // 2), l * PER_LAYER
                norm(l * 3 + 3, l * 3 + 2, "attn_w", l * KD)
                split_ahead(half, full, N_BLOCK1 + O_FL, 1)
                fl = wb[0:8, 6, :]
                act.wait_ge(S("f_z"), l + 1)
                nc.scalar.activation(fl, fl, ACT.Exp)
                act.drain()
                nc.scalar.activation(fl, fl, ACT.Ln, bias=par("one", rows=8)).then_inc(S("f_softplus"), 1)
                act.wait_ge(S("f_cum"), l + 1)
                act.dma_start(cum_dram[0], wb[0:8, 6, :]).then_inc(S("cum_stored"), 16)
                act.dma_start(cum_dram[1], wb[0:8, 7, :]).then_inc(S("cum_stored"), 16)
                split_ahead(half, full, N_BLOCK1 + O_F, 12)
                act.wait_ge(S("cum_stored"), l * 32 + 32)
                with act.Fori(0, PAIRS) as p:
                    pair = l * 4 + p
                    act.dma_start(wb[0:1, 0:2, :], cum_dram[0:1, bass.ds(p * 2, 2), :]).then_inc(S("f_aug"), 16)
                    act.dma_start(wb[1:2, 2:4, :], cum_dram[1:2, bass.ds(p * 2, 2), :]).then_inc(S("f_aug"), 16)
                    def gates_r(u):
                        if u == 8:
                            in_place(ACT.Silu, "r_g", "r_gsilu", pair, wb[:, p + 4, :])

                    softmax_pair(pair + 8, lambda j: high(half + p * 2, full + p * 4, N_BLOCK1 + O_R + LOOK + j), gates_r)
                act.dma_start(wb[:, 0:2, :], dram["rotary"]).then_inc(S("rotary_loaded"), 16)
                with act.Fori(0, PAIRS) as p:
                    pair = l * 4 + p
                    act.wait_ge(S("r_st", 1), pair + 1)
                    act.dma_start(tab[:, :, :], dram["decay"][p]).then_inc(S("decay_loaded"), 16)
                    act.wait_ge(S("r_d"), pair + 1)
                    nc.scalar.activation(probs_t[:, 0, :], probs[:, 0, :], ACT.Square).then_inc(S("r_sq"), 1)
                    act.wait_ge(S("r_var"), pair + 1)
                    factor(probs[:, 1, :], pt[:, :], 1.0, "gn_eps").then_inc(S("r_rstd"), 1)
                split_ahead(half, full, N_BLOCK1 + O_O, 8,
                            lambda k, odd: norm_tile(l * 3 + 4, k, odd, l * 3 + 3, "ffn_w", l * KD))
                norm_factor(l * 3 + 4)
                act.dma_start(wv[:, 0:2, :], dram["p"][l]).then_inc(S("e_loaded"), 16)
                done = 0
                for ch, count in enumerate(CHUNKS2):
                    first = N_BLOCK1 + O_FFN[ch]
                    with act.Fori(0, count // 2) as i:
                        for j in range(4):
                            high(half + i * 2, full + i * 4, first + LOOK + j)
                            if j % 2:
                                act.wait_ge(S("h_conv"), l * FT2 + i * 2 + (done + j // 2 + 1))
                                nc.scalar.activation(probs_t[:, 1, :], probs_t[:, 0, :],
                                                     ACT.Gelu).then_inc(S("h_gelu"), 1)
                                high_of_tile("h", l * FT2 + i * 2 + (done + j // 2), y_hi[:, i * 2 + j // 2, :],
                                             probs[:, 0, :])
                    split_ahead(half, full, first + 2 * count, 8, None if ch < 2 else
                                lambda k, odd: norm_tile(l * 3 + 5, k, odd, l * 3 + 4, "ple_w", l * KD))
                    done += count
                norm_factor(l * 3 + 5)
                act.wait_ge(S("e_loaded"), l * 16 + 16)
                for k in range(2):
                    nc.scalar.copy(y_hi[:, 8 + k, :], wv[:, k, :]).then_inc(S("e_hi"), 1)
                split_ahead(half, full, N_BLOCK1 + O_GATE, 8,
                            lambda j, odd: in_place(ACT.Sigmoid, "e_g", "e_gate", l * 8 + j, wa[:, j, :]))
                split_ahead(half, full, N_BLOCK1 + O_PLE, 3)
            norm(9)
            for k in range(KD):
                act.wait_ge(S("out_ready"), k + 1)
                act.dma_start(out[k * P:(k + 1) * P, :], wb[:, k, :]).then_inc(S("out_stored"), 16)
            act.wait_ge(S("out_stored"), 16 * KD)

        @blk.vector
        def _(dve):
            v = nc.vector
            dve.wait_ge(started, 1)
            dve.wait_ge(S("const_loaded"), 48)

            def each(layer, first, count, body):
                fours = count // 4 if count >= 8 else 0
                if fours:
                    with dve.Fori(0, fours) as i:
                        for j in range(4):
                            body(layer + i * 4 + (first + j), (first + j) % 4, i * 4 + j)
                for j in range(4 * fours, count):
                    body(layer + (first + j), (first + j) % 4, j)

            def evacuate(layer, first, count, dst_of, signal=None):
                def one(n, slot, i):
                    dve.wait_ge(gemm_done, panel_done(n))
                    v.tensor_tensor(dst_of(i), acc[:, slot, :], rstd[:, :], ALU.mult).then_inc(acc_free, 1)
                    if signal:
                        dve.drain().then_inc(S(signal), 1)
                each(layer, first, count, one)

            def add_to_x(layer, first, normed=None):
                def one(n, slot, i):
                    dve.wait_ge(gemm_done, panel_done(n))
                    v.tensor_tensor(x[:, i, :], x[:, i, :], acc[:, slot, :], ALU.add).then_inc(acc_free, 1)
                    if normed:
                        dve.drain().then_inc(S("norm_x"), 1)
                        norm_tile(normed[0], i, slot % 2 ^ first % 2, *normed[1:])
                if normed:
                    norm_start()
                each(layer, first, 8, one)
                if normed:
                    norm_end()

            def low_of_tile(name, k, src, hi, lo):
                dve.wait_ge(S(name + "_hi"), k + 1)
                v.tensor_tensor(lo, src, hi, ALU.subtract).then_inc(S(name + "_split"), 1)
                dve.drain()

            def norm_start():
                v.memset(probs[:, 0, :], 0.0)
                dve.drain()

            def norm_tile(r, k, odd, split=None, gains=None, i0=0):
                if split is not None:
                    dve.wait_ge(S("norm_hi"), split * 8 + k + 1)
                    v.scalar_tensor_tensor(act_lo[:, k, :], x[:, k, :], par(gains, i0 + k), act_hi[:, k, :],
                                           ALU.mult, ALU.subtract).then_inc(S("norm_split"), 1)
                dve.wait_ge(S("norm_sq"), r * 8 + k + 1)
                v.tensor_tensor(probs[:, 0, :], probs[:, 0, :], probs_t[:, odd, :],
                                ALU.add).then_inc(S("norm_added", 2), 1)

            def norm_end():
                dve.drain().then_inc(S("norm_total"), 1)

            def norm(r, split=None, gains=None, i0=0):
                norm_start()
                for k in range(KD):
                    norm_tile(r, k, k % 2, split, gains, i0)
                    dve.drain()
                norm_end()

            def split_here(src, tile, done):
                v.tensor_copy(y_hi[:, tile, :], src)
                dve.drain()
                v.tensor_tensor(y_lo[:, tile, :], src, y_hi[:, tile, :], ALU.subtract).then_inc(S(done), 1)

            def stage(name, p, scale=1.0):
                v.tensor_scalar(qcur[:, 0, :], wa[:, p, :], scale, None, ALU.mult)
                v.tensor_copy(kcur[:, 0, :], wa[:, p + 4, :])
                v.tensor_copy(vstage, wv[:, p, :])
                dve.drain().then_inc(S(name + "_stage"), 1)

            def copy_values(name, pair, bank):
                dve.wait_ge(S(name + "_vt"), pair + 1)
                v.tensor_copy(vcur[:, :, :], bank.rearrange("p (t f) -> p t f", f=P)).then_inc(S(name + "_v"), 1)

            def guest(n, slot, dst, signal=None):
                dve.wait_ge(gemm_done, panel_done(n))
                v.tensor_tensor(dst, acc[:, slot, :], rstd[:, :], ALU.mult).then_inc(acc_free, 1)
                dve.drain()
                if signal:
                    dve.nop().then_inc(S(signal), 1)

            def softmax_pair(pair, tile, values=None, work=None):
                unit0 = pair * 8

                def row_max(u):
                    kw = (u % 4 + 1) * P
                    dve.wait_ge(S("soft_s"), unit0 + (u + 1))
                    v.tensor_reduce(neg_max[u % 2], sc[:, u % 2, 0:kw], AX.X, ALU.max,
                                    negate=True).then_inc(S("soft_max"), 1)

                def normalise(u):
                    kw = (u % 4 + 1) * P
                    dve.wait_ge(S("soft_exp", 2), unit0 + (u + 3))
                    v.reciprocal(inv_sum[u % 2], prob_sum[u % 2])
                    dve.drain()
                    v.tensor_scalar(probs[:, u % 2, 0:kw], probs[:, u % 2, 0:kw], inv_sum[u % 2], None,
                                    ALU.mult).then_inc(S("soft_p"), 1)

                for u in range(9):
                    if u < 8:
                        row_max(u)
                    if u == 0 and values is not None:
                        copy_values("soft", values, po[:, :])
                    if u:
                        normalise(u - 1)
                    if work:
                        work(u)
                dve.wait_ge(S("soft_pv", 2), unit0 + 10)
                v.tensor_copy(y_hi[:, tile, :], po[:, :])
                dve.drain()
                v.tensor_tensor(y_lo[:, tile, :], po[:, :], y_hi[:, tile, :], ALU.subtract)
                dve.drain().then_inc(S("soft_ofree", 1), 1)
                dve.nop().then_inc(S("soft_y"), 1)

            def rotate(tile, rows, sin, cos):
                v.tensor_tensor(probs_t[0:rows, 0, :], po[0:rows, :], sin, ALU.mult)
                v.tensor_tensor(tile, tile, cos, ALU.mult)
                dve.drain()
                return v.tensor_tensor(tile, tile, probs_t[0:rows, 0, :], ALU.add)

            lb = params[:, PARAMS["lb"][0]:PARAMS["lb"][0] + PAIRS]
            v.tensor_tensor(lower, lb, lb, ALU.subtract).then_inc(S("b_lb"), 1)
            norm(0, 0, "mix_g", 0)
            dve.wait_ge(S("b_lbexp"), 1)
            v.reciprocal(rest, lower)
            dve.drain()
            v.tensor_tensor(lower, lower, rest, ALU.mult)
            dve.drain()
            v.tensor_tensor(lower, lower, lower, ALU.subtract)
            dve.drain()
            v.tensor_scalar(rest, lower, -1.0, 1.0, ALU.mult, ALU.add)
            dve.wait_ge(S("norm_rstd"), 1)
            evacuate(0, N_A, 8, lambda i: wa[:, i, :])
            evacuate(0, N_A + 8, 4, lambda i: wv[:, i, :])
            dve.drain()
            with dve.Fori(0, PAIRS) as p:
                stage("soft", p, HD ** -0.5)

                def gates_b(u):
                    n = p * 4 + N_B
                    z, key, tmp = wb[:, p, :], wa[:, p + 4, :], decay_tmp[:, :]
                    if u == 2:
                        guest(n, N_B % 4, wa[:, p, :])
                    if u == 4:
                        guest(n + 1, (N_B + 1) % 4, z)
                        v.scalar_tensor_tensor(tmp, z, -1.0, z, ALU.mult, ALU.min)
                        dve.drain().then_inc(S("b_z"), 1)
                    if u == 6:
                        guest(n + 2, (N_B + 2) % 4, wv[:, p, :])
                    if u == 7:
                        dve.wait_ge(S("b_softplus"), p + 1)
                        v.scalar_tensor_tensor(z, z, 0.0, tmp, ALU.min, ALU.subtract)
                        v.tensor_scalar(key, key, cols[:, bass.ds(p + 10, 1)], None, ALU.mult)
                        dve.drain()
                        v.tensor_scalar(tmp, z, -1.0, 40.0, ALU.mult, ALU.min).then_inc(S("b_neglog"), 1)
                    if u == 8:
                        dve.wait_ge(S("b_inv"), p + 1)
                        v.tensor_scalar(tmp, tmp, cols[:, bass.ds(p + 4, 1)], cols[:, bass.ds(p + 10, 1)],
                                        ALU.mult, ALU.add).then_inc(S("b_mixed"), 1)
                        guest(n + 3, (N_B + 3) % 4, wb[:, p + 4, :], "b_g")

                softmax_pair(p, p, p, gates_b)
                dve.wait_ge(S("b_mixedlog"), p + 1)
                v.tensor_tensor(wb[:, p, :], wb[:, p, :], decay_tmp[:, :], ALU.add)
                dve.drain()

            for i, h in enumerate((64, 128, 256)):
                v.memset(resets[:, i, :], 1.0)
                dve.drain()
                v.memset(resets[:, i, :].rearrange("p (b h) -> p b h", h=h)[:, :, 0:1], 0.0)
            dve.wait_ge(S("b_qsilu"), 4)
            dve.drain()

            def halves(ap, h):
                w = ap.rearrange("p (b two h) -> p b two h", two=2, h=h)
                return w[:, :, 0, :], w[:, :, 1, :]

            with dve.Fori(0, PAIRS) as p:
                for i in range(3):
                    v.tensor_tensor_scan(cums[:, i, :], resets[:, i, :], wb[:, p, :], 0.0, ALU.mult, ALU.add)
                stage("b", p)

                def exponents(n):
                    h = LEVELS[n]
                    e = kcur[:, 1, :] if n % 2 else qcur[:, 1, :]
                    cum = cums[:, {256: 2, 128: 1}.get(h, 0), :]
                    (e0, e1), (c0, c1) = halves(e, h), halves(cum, h)
                    mid = c0[:, :, h - 1:h].broadcast_to([P, T // (2 * h), h])
                    v.tensor_tensor(e0, mid, c0, ALU.subtract)
                    if h >= 64:
                        v.tensor_copy(e1, c1)
                    else:
                        v.tensor_tensor(e1, c1, mid, ALU.subtract)
                    dve.drain().then_inc(S("b_d"), 1)

                def decayed(n):
                    h = LEVELS[n]
                    e = kcur[:, 1, :] if n % 2 else qcur[:, 1, :]
                    dve.wait_ge(S("b_e"), p * 9 + n)
                    (e0, e1), (x0, x1) = halves(e, h), halves(tab[:, n % 2, :], h)
                    k0, q1 = halves(kcur[:, 0, :], h)[0], halves(qcur[:, 0, :], h)[1]
                    v.tensor_tensor(x0, e0, k0, ALU.mult)
                    v.tensor_tensor(x1, e1, q1, ALU.mult)
                    dve.drain().then_inc(S("b_x"), 1)

                def collect(n):
                    h = LEVELS[n]
                    for hh in range(2):
                        bank = lev_bank[(2 * n + hh) % 4]
                        dve.wait_ge(S("b_s"), p * 20 + (2 * n + hh + 1))
                        settle(dve)
                        tiles = bank.rearrange("p (t i) -> p t i", i=P)
                        if h == 0:
                            ident = c["ident"].rearrange("p (o i) -> p o i", o=1).broadcast_to([P, TT, P])
                            last = v.tensor_tensor(s_diag[:, hh, :, :], tiles, ident, ALU.mult)
                        elif h == 256:
                            last = v.tensor_copy(s_256[:, hh, :, :], bank.rearrange("p (t i) -> p t i", i=256))
                        elif h == 128:
                            last = v.tensor_copy(s_128[:, hh, :, :], tiles[:, 0:2, :])
                        else:
                            mask = masks[:, n - 3, :].bitcast(mybir.dt.uint32).rearrange("p (o i) -> p o i", o=1)
                            last = v.copy_predicated(s_diag[:, hh, :, :], mask.broadcast_to([P, TT, P]), tiles)
                        last.then_inc(S("b_sfree", 4), 1)

                exponents(1)
                copy_values("b", p, po[:, :])
                for n in range(1, len(LEVELS)):
                    if n + 1 < len(LEVELS):
                        exponents(n + 1)
                    decayed(n)
                    collect(n - 1)
                dve.drain()
                collect(len(LEVELS) - 1)
                dve.drain().then_inc(S("b_st", 1), 1)
                dve.wait_ge(S("b_rstd"), p + 1)
                t = probs_t[:, 1, :]
                v.scalar_tensor_tensor(t, po[:, :], par("hgrn_g"), qcur[:, 1, :], ALU.mult, ALU.mult)
                dve.drain()
                v.tensor_tensor(t, t, wb[:, p + 4, :], ALU.mult)
                dve.drain()
                split_here(t, p + 4, "b_y")
                dve.drain().then_inc(S("b_ofree", 1), 1)

            two_pi = 2.0 * np.pi
            c1 = 6.28125
            c2 = float(np.round((two_pi - c1) * 2 ** 22) / 2 ** 22)
            c3 = two_pi - c1 - c2
            magic = 1.5 * 2 ** 23
            ang, turn = probs_t[:, 0, :], probs_t[:, 1, :]
            dve.wait_ge(S("pos_loaded"), 16)
            v.tensor_copy(ang, positions[:, :])
            dve.drain()
            v.tensor_scalar(ang, ang, par("inv_freq"), None, ALU.mult)
            dve.drain()
            v.tensor_scalar(turn, ang, 1.0 / two_pi, magic, ALU.mult, ALU.add)
            dve.drain()
            v.tensor_scalar(turn, turn, magic, None, ALU.subtract)
            dve.drain()
            for part in (c1, c2, c3):
                v.scalar_tensor_tensor(ang, turn, -part, ang, ALU.mult, ALU.add)
                dve.drain()
            pi = 3.1415925
            v.tensor_scalar(tab[:, 0, :], ang, pi, -pi, ALU.min, ALU.max).then_inc(S("c_angle"), 1)
            v.tensor_scalar(ang, ang, 0.5 * np.pi, None, ALU.add)
            dve.drain()
            v.tensor_scalar(turn, ang, np.pi, -two_pi, ALU.is_gt, ALU.mult)
            dve.drain()
            v.tensor_tensor(ang, ang, turn, ALU.add)
            dve.drain()
            v.tensor_scalar(tab[:, 1, :], ang, pi, -pi, ALU.min, ALU.max).then_inc(S("c_angle"), 1)
            sin, cos = tab[:, 0, :], tab[:, 1, :]
            evacuate(0, N_C, 4, lambda i: wv[:, i, :], "c_raw")
            dve.nop().then_inc(S("c_rotin"), 1)
            for k in range(3):
                dve.wait_ge(S("c_rstd"), 1 + k // 2)
                gain = par("q_g", k) if k < 2 else par("kv_g")
                v.scalar_tensor_tensor(wb[:, k, :], wv[:, k, :], gain, probs[:, k // 2, :],
                                       ALU.mult, ALU.mult).then_inc(S("cn_h"), 1)
                low_of_tile("cn", k, wb[:, k, :], y_hi[:, 8 + k, :], y_lo[:, 8 + k, :])
            dve.wait_ge(S("c_sincos"), 2)
            dve.wait_ge(S("c_rot"), 1)
            rotate(wv[:, 3, :], P, sin, cos)
            dve.drain()
            for b in range(2):
                v.tensor_copy(kcur[NOPE:QH, b, :], wv[NOPE:QH, 3, :])
            dve.drain().then_inc(S("c_rotused"), 1)
            for q in range(2):
                dve.wait_ge(gemm_done, panel_done(N_UP + q))
                v.tensor_copy(wa[0:QH, 4 * q:4 * q + 4, :], acc[0:QH, :, :]).then_inc(acc_free, 1)
                dve.drain().then_inc(S("c_rotin"), 1)
            dve.wait_ge(gemm_done, panel_done(N_UP + 2))
            by_pair = wb[0:HD, :, :].rearrange("p (h two) t -> p h two t", two=2)
            v.tensor_copy(by_pair[:, :, 0, :], acc[0:HD, :, :])
            v.tensor_copy(by_pair[:, :, 1, :], acc[HD:P, :, :]).then_inc(acc_free, 1)
            dve.wait_ge(gemm_done, panel_done(N_UP + 3))
            v.tensor_copy(wv[:, :, :], acc[:, :, :]).then_inc(acc_free, 1)
            for h in range(HEADS):
                dve.wait_ge(S("c_rot"), 2 + h)
                rotate(wa[0:QH, h, :], QH, sin[0:QH], cos[0:QH]).then_inc(S("c_rotused"), 1)
            dve.drain()
            with dve.Fori(0, PAIRS) as p:
                for b in range(2):
                    v.tensor_scalar(qcur[0:QH, b, :], wa[0:QH, p * 2 + b, :], QH ** -0.5, None, ALU.mult)
                    v.tensor_copy(kcur[0:NOPE, b, :], wb[0:NOPE, p * 2 + b, :])
                v.tensor_copy(vcur[:, :, :], wv[:, :, bass.ds(p * P, P)])
                dve.drain().then_inc(S("soft_stage"), 1)
                softmax_pair(p + 4, p + 8)

            with dve.Fori(0, 4) as i:
                for b in range(6):
                    n = i * 12 + (N_MERGE + 2 * b)
                    gate = probs[:, b % 2, :]
                    dve.wait_ge(gemm_done, panel_done(n))
                    v.tensor_tensor(gate, acc[:, (N_MERGE + 2 * b) % 4, :], rstd[:, :], ALU.mult).then_inc(acc_free, 1)
                    dve.drain().then_inc(S("m_z"), 1)
                    dve.wait_ge(S("m_gate"), i * 6 + (b + 1))
                    dve.wait_ge(gemm_done, panel_done(n + 1))
                    total, term = probs_t[:, 1, :], probs_t[:, 0, :]
                    v.tensor_tensor(total if b % 3 == 0 else term, acc[:, (N_MERGE + 2 * b + 1) % 4, :],
                                    gate, ALU.mult).then_inc(acc_free, 1)
                    dve.drain()
                    if b % 3:
                        v.tensor_tensor(total, total, term, ALU.add)
                        dve.drain()
                    if b % 3 == 2:
                        m = i * 2 + b // 3
                        dve.nop().then_inc(S("m_h"), 1)
                        low_of_tile("m", m, total, merged_hi[:, m, :], merged_lo[:, m, :])
            add_to_x(0, N_O, (1, 1, "ffn_g", 0))
            dve.wait_ge(S("norm_rstd"), 2)

            with dve.Fori(0, 4) as i:
                def relu_squared(n, slot, j):
                    dve.wait_ge(gemm_done, panel_done(n))
                    v.scalar_tensor_tensor(probs[:, 1, :], acc[:, slot, :], 0.0, rstd[:, :],
                                           ALU.max, ALU.mult).then_inc(acc_free, 1)
                    dve.drain()
                    v.tensor_tensor(probs[:, 0, :], probs[:, 1, :], probs[:, 1, :], ALU.mult).then_inc(S("g_h"), 1)
                    low_of_tile("g", i * 8 + j, probs[:, 0, :], y_hi[:, j, :], y_lo[:, j, :])
                each(i * 16, N_FF, 8, relu_squared)
                add_to_x(i * 16, N_FF + 8)
            dve.drain().then_inc(S("norm_x"), 8)
            norm(2)

            dve.wait_ge(S("norm_rstd"), 3)
            for k in range(KD):
                v.scalar_tensor_tensor(x[:, k, :], x[:, k, :], par("mid_g", k), rstd[:, :], ALU.mult,
                                       ALU.mult).then_inc(S("norm_x"), 1)
            dve.drain()

            with dve.Fori(0, LAYERS) as l:
                layer = l * PER_LAYER
                norm(l * 3 + 3, l * 3 + 2, "attn_w", l * KD)
                dve.wait_ge(S("norm_rstd"), l * 3 + 4)
                dve.wait_ge(gemm_done, panel_done(layer + (N_BLOCK1 + O_FL)))
                fz, ft, fneg, fone = (wb[0:8, i, :] for i in (5, 6, 7, 4))
                v.tensor_tensor(fz, acc[0:8, O_FL % 4, :], rstd[0:8, :], ALU.mult).then_inc(acc_free, 1)
                v.memset(wb[0:8, 0:5, :], 1.0)
                dve.drain()
                v.tensor_scalar(fz, fz, par("f_bias", l, 8), None, ALU.add)
                dve.drain()
                v.scalar_tensor_tensor(ft, fz, -1.0, fz, ALU.mult, ALU.min).then_inc(S("f_z"), 1)
                dve.wait_ge(S("f_softplus"), l + 1)
                v.scalar_tensor_tensor(fz, fz, 0.0, ft, ALU.min, ALU.subtract)
                dve.drain()
                v.tensor_tensor_scan(ft, fone, fz, 0.0, ALU.mult, ALU.add)
                dve.drain()
                v.tensor_scalar(fneg, ft, -1.0, None, ALU.mult).then_inc(S("f_cum"), 1)
                evacuate(layer, N_BLOCK1 + O_F, 8, lambda i: wa[:, i, :])
                evacuate(layer, N_BLOCK1 + O_F + 8, 4, lambda i: wv[:, i, :])
                dve.drain()
                with dve.Fori(0, PAIRS) as p:
                    stage("soft", p, HD ** -0.5)

                    def projections_r(u):
                        n = layer + p * 4 + (N_BLOCK1 + O_R)
                        if u in (2, 4, 6, 8):
                            j = u // 2 - 1
                            guest(n + j, (O_R + j) % 4, (wa[:, p, :], wa[:, p + 4, :], wv[:, p, :], wb[:, p + 4, :])[j],
                                  "r_g" if j == 3 else None)

                    softmax_pair(l * 4 + p + 8, p, l * 4 + p + 4, projections_r)

                dve.wait_ge(S("rotary_loaded"), l * 16 + 16)
                dve.wait_ge(S("r_gsilu"), l * 4 + 4)
                settle(dve)
                dve.drain()
                with dve.Fori(0, PAIRS) as p:
                    pair = l * 4 + p
                    v.tensor_copy(vstage, wv[:, p, :])
                    for b, (rot, cur) in enumerate(((po, qcur[:, 0, :]), (pt, kcur[:, 0, :]))):
                        v.tensor_tensor(cur, wa[:, p + 4 * b, :], wb[:, 1, :], ALU.mult)
                        dve.wait_ge(S("r_rot"), pair * 2 + (b + 1))
                        v.tensor_tensor(probs_t[:, b, :], rot[:, :], wb[:, 0, :], ALU.mult)
                        dve.drain()
                        v.tensor_tensor(cur, cur, probs_t[:, b, :], ALU.add)
                    dve.drain().then_inc(S("r_stage"), 1)
                    copy_values("r", pair, acc[:, 2, :])
                    dve.wait_ge(S("decay_loaded"), pair * 16 + 16)
                    for u in range(8):
                        hh, jt = divmod(u, 4)
                        w = T - jt * P
                        dve.wait_ge(S("r_s"), pair * 8 + (u + 1))
                        v.tensor_tensor(s_ret[hh][:, s_off[jt]:s_off[jt] + w], lev_bank[u % 4][:, 0:w],
                                        tab[:, hh, 0:w], ALU.mult).then_inc(S("r_sfree", 4), 1)
                    dve.drain().then_inc(S("r_st", 1), 1)
                    dve.wait_ge(S("r_pv"), pair + 1)
                    o = probs[:, 0, :]
                    v.tensor_copy(o, po[:, :]).then_inc(S("r_o"), 1)
                    dve.wait_ge(S("r_mean"), pair + 1)
                    v.tensor_tensor(o, o, pt[:, :], ALU.subtract).then_inc(S("r_d"), 1)
                    dve.wait_ge(S("r_rstd"), pair + 1)
                    v.tensor_tensor(o, o, probs[:, 1, :], ALU.mult)
                    dve.drain()
                    v.tensor_tensor(o, o, wb[:, p + 4, :], ALU.mult)
                    dve.drain()
                    split_here(o, p + 4, "r_y")
                    dve.drain().then_inc(S("r_ofree", 1), 1)
                add_to_x(layer, N_BLOCK1 + O_O, (l * 3 + 4, l * 3 + 3, "ffn_w", l * KD))
                dve.wait_ge(S("norm_rstd"), l * 3 + 5)
                settle(dve)

                v.memset(padded[:, 0:2], 0.0)
                done = 0
                for ch, tiles in enumerate(CHUNKS2):
                    first = N_BLOCK1 + O_FFN[ch]
                    with dve.Fori(0, tiles // 2) as i:
                        for j in range(2):
                            n = layer + i * 4 + (first + 2 * j)
                            slot = (first + 2 * j) % 4
                            tile = l * FT2 + i * 2 + (done + j)
                            y_tile = i * 2 + j
                            conv = probs_t[:, 0, :]
                            dve.wait_ge(gemm_done, panel_done(n))
                            v.tensor_tensor(padded[:, 2:T + 2], acc[:, slot, :], rstd[:, :], ALU.mult).then_inc(acc_free, 1)
                            dve.drain()
                            v.tensor_scalar(conv, padded[:, 0:T], par("conv_w", tile * 3), par("conv_b", tile),
                                            ALU.mult, ALU.add)
                            dve.drain()
                            v.scalar_tensor_tensor(conv, padded[:, 1:T + 1], par("conv_w", tile * 3 + 1), conv,
                                                   ALU.mult, ALU.add)
                            dve.drain()
                            v.scalar_tensor_tensor(conv, padded[:, 2:T + 2], par("conv_w", tile * 3 + 2), conv,
                                                   ALU.mult, ALU.add).then_inc(S("h_conv"), 1)
                            dve.wait_ge(S("h_gelu"), tile + 1)
                            v.tensor_tensor(probs_t[:, 1, :], probs_t[:, 1, :], rstd[:, :], ALU.mult)
                            dve.drain()
                            dve.wait_ge(gemm_done, panel_done(n + 1))
                            v.tensor_tensor(probs[:, 0, :], acc[:, (slot + 1) % 4, :], probs_t[:, 1, :],
                                            ALU.mult).then_inc(acc_free, 1)
                            dve.drain().then_inc(S("h_h"), 1)
                            low_of_tile("h", tile, probs[:, 0, :], y_hi[:, y_tile, :], y_lo[:, y_tile, :])
                    add_to_x(layer, first + 2 * tiles, (l * 3 + 5, l * 3 + 4, "ple_w", l * KD) if ch == 2 else None)
                    done += tiles
                for k in range(2):
                    dve.wait_ge(S("e_hi"), l * 2 + (k + 1))
                    v.tensor_tensor(y_lo[:, 8 + k, :], wv[:, k, :], y_hi[:, 8 + k, :],
                                    ALU.subtract).then_inc(S("e_split"), 1)
                dve.wait_ge(S("norm_rstd"), l * 3 + 6)
                settle(dve)
                evacuate(layer, N_BLOCK1 + O_GATE, 8, lambda i: wa[:, i, :], "e_g")
                dve.wait_ge(S("e_gate"), l * 8 + 8)
                for q in range(3):
                    dve.wait_ge(gemm_done, panel_done(layer + (N_BLOCK1 + O_PLE + q)))
                    w = 3 if q < 2 else 2
                    gate = wa[:, 3 * q:3 * q + w, :]
                    v.tensor_tensor(gate, gate, acc[:, 0:w, :], ALU.mult).then_inc(acc_free, 1)
                    dve.drain()
                    v.tensor_tensor(x[:, 3 * q:3 * q + w, :], x[:, 3 * q:3 * q + w, :], gate, ALU.add)
                dve.drain().then_inc(S("norm_x"), 8)
            norm(9)
            dve.wait_ge(S("norm_rstd"), 10)
            for k in range(KD):
                v.scalar_tensor_tensor(wb[:, k, :], x[:, k, :], par("final_g", k), rstd[:, :],
                                       ALU.mult, ALU.mult).then_inc(S("out_ready"), 1)

        @blk.gpsimd
        def _(pool):
            for name, start in starts.items():
                pool.sem_inc(sems[name], start)
            pool.sem_inc(started, 1)

            def low(n, slot):
                pool.wait_ge(hi_done, n + 1)
                nc.gpsimd.tensor_tensor(w_lo[:, slot, :], raw[:, slot % 2, :], w_hi[:, slot, :],
                                        ALU.subtract).then_inc(lo_done, 1)

            with pool.Fori(0, N_PANELS // 4) as i:
                for j in range(4):
                    low(i * 4 + j, j)
            for j in range(LOOK):
                low(N_PANELS + j, j)


def constant_arrays():
    i = np.arange(P)
    k, q = i[:, None], i[None, :]
    table = {"ident": k == q, "anti": k + q == P - 1, "ones": np.ones((P, P)), "head_mean": (k // HD == q // HD) / HD}
    mask1 = np.where(q // CHUNK <= k // CHUNK, 0.0, MASKED)
    mask2 = np.where(q <= k, 0.0, MASKED)
    rope_c = np.zeros((P, P))
    for r in range(ROPE // 2):
        rope_c[NOPE + ROPE // 2 + r, NOPE + r] = -1.0
        rope_c[NOPE + r, NOPE + ROPE // 2 + r] = 1.0
    rope_r = np.zeros((P, P))
    for h in (0, HD):
        for r in range(HD // 2):
            rope_r[h + HD // 2 + r, h + r] = -1.0
            rope_r[h + r, h + HD // 2 + r] = 1.0
    table["mask"], table["rope"] = mask1, rope_c
    consts = np.stack([np.asarray(table[n], np.float32) for n in CONSTS], 1)
    consts2 = np.stack([mask2, rope_r], 1).astype(np.float32)
    masks = np.stack([(k // (2 * h) == q // (2 * h)) & (k % (2 * h) < h) & (q % (2 * h) >= h)
                      for h in LEVELS[3:]], 1).astype(np.float32)
    freq = np.float32(10000.0) ** (-np.arange(0, HD, 2, dtype=np.float32) / np.float32(HD))
    ang = np.arange(T, dtype=np.float32)[None, :] * freq.astype(np.float32)[i % (HD // 2)][:, None]
    rotary = np.stack([np.sin(ang.astype(np.float64)), np.cos(ang.astype(np.float64))], 1).astype(np.float32)
    log_gamma = np.log1p(-(2.0 ** (-5.0 - np.arange(HEADS))))
    rel = np.arange(T)[None, :] - k
    decay = np.where(rel >= 0, HD ** -0.5 * np.exp(log_gamma[:, None, None] * np.maximum(rel, 0)), 0.0)
    decay = decay.reshape(PAIRS, 2, P, T).transpose(0, 2, 1, 3).astype(np.float32)
    inv_freq = np.zeros((P, 1), np.float32)
    inv_freq[NOPE:QH, 0] = np.tile(np.float32(10000.0) ** (-np.arange(0, ROPE, 2, dtype=np.float32) / np.float32(ROPE)), 2)
    return {"consts": consts, "consts2": consts2, "masks": masks, "rotary": rotary, "decay": decay}, inv_freq


def columns(a, rows=P):
    return np.moveaxis(a.reshape(*a.shape[:-1], -1, rows), -1, 0).reshape(rows, -1)


def feature_panels(w, width=P):
    k, m = w.shape[0] // P, w.shape[1] // width
    return w.reshape(k, P, m, width).transpose(2, 1, 0, 3).reshape(m, P, k * width)


def in_turns(*parts):
    return np.stack(parts, 1).reshape(-1, *parts[0].shape[1:])


def padded_columns(w, first):
    out = np.zeros((w.shape[0], P), w.dtype)
    out[:, first:first + w.shape[1]] = w
    return out


def lay_out(a):
    arrays, inv_freq = constant_arrays()
    f = lambda v: np.asarray(v)
    w = f(a["w_in"])[0]
    s = np.cumsum([0, 512, 512, 512, 512, 512, 512, 512, QR, KVR, ROPE, 3 * D])
    aq, ak, av, bq, bf, bi, bg, cq, ckv, ckr, gates = (w[:, s[i]:s[i + 1]] for i in range(11))
    cat = np.concatenate
    fp = feature_panels
    arrays["w_in1"] = cat([fp(aq), fp(ak), fp(av), in_turns(fp(bq), fp(bf), fp(bi), fp(bg)), fp(cq), fp(ckv),
                           fp(padded_columns(ckr, NOPE))])
    arrays["w_c_q"] = feature_panels(f(a["mla_w_uq"])[0], QH).reshape(2, 4, P, 2 * QH).transpose(0, 2, 1, 3).reshape(2, P, -1)
    ukv = f(a["mla_w_ukv"])[0].reshape(KVR, HEADS, 2, HD)
    arrays["w_c_kv"] = np.stack([ukv[:, :, 0].reshape(P, 512), ukv[:, :, 1].reshape(P, 512)])
    gate = feature_panels(gates).reshape(3, KD, P, 1024).transpose(1, 0, 2, 3)
    branch = np.stack([feature_panels(f(a["w_branch"])[0, b]) for b in range(3)], 1)
    arrays["w_gate"], arrays["w_branch"] = gate.reshape(24, P, 1024), branch.reshape(24, P, 512)
    ff1 = feature_panels(f(a["w_ff1"])[0]).reshape(4, 8, P, 1024)
    ff2 = np.stack([feature_panels(part) for part in f(a["w_ff2"])[0].reshape(4, D, D)])
    arrays["w_rest1"] = cat([feature_panels(f(a["w_out"])[0]), cat([ff1, ff2], 1).reshape(64, P, 1024)])
    layers = {n: [] for n in SEGMENTS2}
    for l in range(LAYERS):
        w = f(a["w_in_2"])[l]
        s = np.cumsum([0, 512, 512, 512, HEADS, 512, 512, 512, 512])
        fq, fk, fv, fl, rq, rk, rv, rg = (w[:, s[i]:s[i + 1]] for i in range(8))
        up, down = f(a["w_up_2"])[l], f(a["w_down_2"])[l]
        both = np.stack([feature_panels(up[:, :FF2]), feature_panels(up[:, FF2:])], 1)
        wide, narrow, at = [], [], 0
        for tiles in CHUNKS2:
            part = [both[at:at + tiles].reshape(-1, P, 1024), feature_panels(down[at * P:(at + tiles) * P])]
            if tiles == 8:
                wide += part
            else:
                wide.append(part[0])
                narrow.append(part[1])
            at += tiles
        layers["in2"].append(cat([fp(padded_columns(fl, 0)), fp(fq), fp(fk), fp(fv),
                                  in_turns(fp(rq), fp(rk), fp(rv), fp(rg)), fp(f(a["w_out_2"])[l])]))
        layers["ffn_wide"].append(cat(wide))
        layers["ffn_narrow"].append(cat(narrow))
        layers["ple_gate"].append(feature_panels(f(a["w_ple_gate_2"])[l]))
        proj = feature_panels(f(a["w_ple_proj_2"])[l])
        layers["ple_a"].append(proj[0:6].reshape(2, 3, P, 256).transpose(0, 2, 1, 3).reshape(2, P, 768))
        layers["ple_b"].append(proj[6:8].transpose(1, 0, 2).reshape(1, P, 512))
    for n, parts in layers.items():
        arrays["w_" + n] = np.stack(parts)
    r = f(a["rel_bias"])[0][:, ::-1]
    ext = r[:, np.clip(np.arange(640) - (T - 1) + A_REL, 0, 2 * A_REL)]
    arrays["bias"] = ext
    arrays["x"] = f(a["x"])[0].T.reshape(KD, P, T).transpose(1, 0, 2)
    arrays["p"] = f(a["p_2"])[:, 0].transpose(0, 2, 1).reshape(LAYERS, 2, P, T).transpose(0, 2, 1, 3)
    arrays["positions"] = f(a["positions"])[0]
    one = np.ones((P, 1), np.float32)
    bias8 = np.zeros((P, LAYERS), np.float32)
    bias8[:HEADS] = f(a["forget_bias_2"]).T
    conv_w = f(a["conv_w_2"]).reshape(LAYERS, 3, FT2, P).transpose(3, 0, 2, 1).reshape(P, -1)
    parts = {"one": one, "eps": one * np.float32(EPS), "gn_eps": one * np.float32(GN_EPS), "inv_freq": inv_freq,
             "mix_g": columns(f(a["norm_mix_g"])), "ffn_g": columns(f(a["norm_ffn_g"])),
             "q_g": columns(f(a["mla_q_norm_g"])), "kv_g": columns(f(a["mla_kv_norm_g"])),
             "hgrn_g": cat([f(a["hgrn_norm_g"])[0]] * 2)[:, None], "lb": columns(f(a["hgrn_lb_logits"])),
             "mid_g": columns(f(a["final_norm_g"])), "final_g": columns(f(a["final_norm_w_2"])), "attn_w": columns(f(a["attn_norm_w_2"])),
             "ffn_w": columns(f(a["ffn_norm_w_2"])), "ple_w": columns(f(a["ple_norm_w_2"])), "f_bias": bias8,
             "conv_b": columns(f(a["conv_b_2"])), "conv_w": conv_w}
    arrays["params"] = cat([parts[n] for n in PARAMS], 1)
    return {n: np.ascontiguousarray(v) for n, v in arrays.items()}


def program(nc, arrays):
    dram = {}
    for n, v in arrays.items():
        dram[n] = nc.dram_tensor("in_" + n, v.shape, mybir.dt.from_np(v.dtype), kind="ExternalInput").ap()
    ext = dram["bias"]
    dram["bias"] = BiasWindows(ext)
    out = nc.dram_tensor("out", (D, T), F32, kind="ExternalOutput").ap()
    build(nc, dram, out)


class BiasWindows:

    def __init__(self, ext):
        self.ext = ext

    def __getitem__(self, pair):
        rows = self.ext[bass.ds(pair * 2, 2), 0:T]
        return bass.AP(rows.tensor, rows.offset, [[1, P], [640, 2], [1, T]])


def kernel(**inputs):
    import concourse.bacc as bacc
    from concourse.bass_utils import run_bass_kernel_spmd

    arrays = lay_out(inputs)
    nc = bacc.Bacc("TRN2", target_bir_lowering=False, num_devices=1)
    program(nc, arrays)
    r = run_bass_kernel_spmd(nc, [{"in_" + n: v for n, v in arrays.items()}], core_ids=[0])
    return r.results[0]["out"].T.reshape(1, T, D)
```

```python
import numpy as np

import concourse.bass as bass
from concourse import mybir

F32 = mybir.dt.float32
F32R = mybir.dt.float32r
U32 = mybir.dt.uint32
I32 = mybir.dt.int32
ALU = mybir.AluOpType
ACT = mybir.ActivationFunctionType
AX = mybir.AxisListType

P = 128
T = 512
D = 1024
KD = D // P
TT = T // P
HEADS = 8
PAIRS = HEADS // 2
HD = 64
CHUNK = 64
EPS = 1e-6
GN_EPS = 1e-5
LAYERS = 2
FF1 = 4 * D
FF2 = -(-8 * D // (3 * 128)) * 128
FT2 = FF2 // P
CHUNKS2 = (8, 8, FT2 - 16)
A_REL = 128
QR, KVR, NOPE, ROPE = 256, 128, 64, 32
QH = NOPE + ROPE
MASKED = -1.0e30
LEVELS = (0, 256, 128, 64, 32, 16, 8, 4, 2, 1)
LOOK = 2

N_A, N_B, N_C, N_UP, N_MERGE, N_O, N_FF = 0, 12, 28, 32, 36, 84, 92
N_BLOCK1 = N_FF + 64
O_FL, O_F, O_R, O_O = 0, 1, 13, 29
O_FFN = (37, 61, 85)
O_GATE, O_PLE = 105, 113
PER_LAYER = 116
N_PANELS = N_BLOCK1 + LAYERS * PER_LAYER
SEGMENTS1 = ["in1", "c_qn", "c_qr", "c_kv"]
SEGMENTS2 = ["in2", "ffn_wide", "ffn_narrow", "ple_gate", "ple_a", "ple_b"]

CONSTS = ["ident", "anti", "ones", "head_mean", "mask", "rope"]
N_MASKS = 7
PARAMS = {}
for _name, _n in [("one", 1), ("eps", 1), ("gn_eps", 1), ("inv_freq", 1), ("mix_g", KD), ("ffn_g", KD), ("q_g", 2), ("kv_g", 1),
                  ("hgrn_g", 1), ("lb", PAIRS), ("mid_g", KD), ("final_g", KD), ("attn_w", LAYERS * KD), ("ffn_w", LAYERS * KD),
                  ("ple_w", LAYERS * KD), ("f_bias", LAYERS), ("conv_b", LAYERS * FT2), ("conv_w", LAYERS * FT2 * 3)]:
    PARAMS[_name] = (sum(n for _, n in PARAMS.values()), _n)
N_PARAMS = sum(n for _, n in PARAMS.values())


def build(nc, dram, out):
    offset = {}

    def sb(name, shape, dt=F32):
        offset[name] = nc.sbuf_base
        return nc.alloc_sbuf_tensor(name, shape, dt)

    def alias(name, base, shape, dt=F32, skip=0):
        return nc.alloc_sbuf_tensor_at(name, shape, dt, offset=offset[base] + skip)

    x = sb("x", [P, KD, T])
    act_hi = sb("act_hi", [P, KD, T], F32R)
    act_lo = sb("act_lo", [P, KD, T], F32R)
    raw = sb("raw", [P, 2, 1024])
    w_hi = sb("w_hi", [P, 4, 1024], F32R)
    w_lo = sb("w_lo", [P, 4, 1024], F32R)
    y_hi = sb("y_hi", [P, 12, T], F32R)
    y_lo = sb("y_lo", [P, 12, T], F32R)
    wa = sb("wa", [P, 8, T])
    wb = sb("wb", [P, 8, T])
    wv = sb("wv", [P, TT, T])
    qcur = sb("qcur", [P, 2, T])
    kcur = sb("kcur", [P, 2, T])
    vcur = sb("vcur", [P, TT, P])
    probs = sb("probs", [P, 2, T])
    probs_t = sb("probs_t", [P, 2, T])
    tab = sb("tab", [P, 2, T])
    consts = sb("consts", [P, len(CONSTS), P])
    masks = sb("masks", [P, N_MASKS, P // 2])
    params = sb("params", [P, N_PARAMS])
    cols = sb("cols", [P, 16])
    rstd = sb("rstd", [P, T])
    c = {n: consts[:, i, :] for i, n in enumerate(CONSTS)}
    neg_max = [cols[:, 0:1], cols[:, 1:2]]
    prob_sum = [cols[:, 2:3], cols[:, 3:4]]
    inv_sum = [cols[:, 8:9], cols[:, 9:10]]
    lower, rest = cols[:, 4:8], cols[:, 10:14]
    merged_hi = alias("merged_hi", "wa", [P, KD, T], F32R)
    merged_lo = alias("merged_lo", "wb", [P, KD, T], F32R)
    positions = alias("positions", "vcur", [P, T], I32)
    tail = 8 * T * 4
    decay_tmp = alias("decay_tmp", "y_hi", [P, T], skip=tail)
    s_diag = alias("s_diag", "y_hi", [P, 2, TT, P], skip=tail)
    s_256 = alias("s_256", "y_hi", [P, 2, 2, 256], skip=tail + 2 * T * 4)
    s_128 = alias("s_128", "y_lo", [P, 2, 2, P], skip=tail)
    cums = alias("cums", "y_lo", [P, 3, T], skip=tail + T * 4)
    resets = alias("resets", "probs", [P, 2, T])
    x_queries = alias("x_queries", "probs_t", [P, 2, T])
    s_ret = [alias("s_ret0", "y_hi", [P, 1280], skip=tail), alias("s_ret1", "y_lo", [P, 1280], skip=tail)]
    s_off = (0, 512, 896, 1152)
    aug = slice(HD, HD + 2)
    padded = alias("padded", "tab", [P, T + 2])

    acc = nc.alloc_psum_tensor("acc", [P, 4, T], F32)
    sc = nc.alloc_psum_tensor("sc", [P, 2, T], F32)
    po = nc.alloc_psum_tensor("po", [P, T], F32)
    pt = nc.alloc_psum_tensor("pt", [P, T], F32)
    vstage = qcur[:, 1, :]
    vstage_f, rotated = wb[:, 0, :], wb[:, 1, :]
    mean_bank = [po[:, :], pt[:, :], sc[:, 0, :], sc[:, 1, :]]
    b_stat = [qcur[:, 0, :], qcur[:, 1, :], kcur[:, 0, :], kcur[:, 1, :]]
    lev_bank = [sc[:, 0, :], sc[:, 1, :], acc[:, 0, :], acc[:, 1, :]]
    cum_dram = nc.dram_tensor("cum_dram", (2, HEADS, T), F32).ap()

    def par(name, i=0, rows=P):
        first = PARAMS[name][0]
        if isinstance(i, int):
            return params[0:rows, first + i:first + i + 1]
        return params[0:rows, bass.ds(i + first, 1)]

    sems, starts = {}, {}

    def S(name, start=0):
        if name not in sems:
            sems[name] = nc.alloc_semaphore(name)
            if start:
                starts[name] = start
        assert starts.get(name, 0) == start, name
        return sems[name]

    started = S("started")
    passed = S("passed")
    raw_loaded = [S("raw_loaded0"), S("raw_loaded1")]
    x_loaded = [S(f"x_loaded{k}") for k in range(KD)]
    hi_done = S("hi_done")
    lo_done = S("lo_done", 2)
    gemm_done = S("gemm_done", 4)
    acc_free = S("acc_free", 4)

    def high_free(n):
        return n + 1

    def settle(eng):
        eng.sem_inc(passed, 1)

    def halves(ap, h):
        w = ap.rearrange("p (b two h) -> p b two h", two=2, h=h)
        return w[:, :, 0, :], w[:, :, 1, :]

    level_units = [2, 2] + [1] * (len(LEVELS) - 2)
    first_unit = [sum(level_units[:n]) for n in range(len(LEVELS) + 1)]

    def exponent_tile(n):
        return kcur[:, 1, :] if n % 2 else qcur[:, 1, :]

    def each_of_four(eng, body):
        with eng.Fori(0, 3) as i:
            body(i, False)
        body(3, True)

    def panel_done(n):
        return n + 5

    block = nc.Block()
    with block as blk:

        @blk.sync
        def _(sp):
            sp.wait_ge(started, 1)

            def load(src, layer, first, count):
                width = src.shape[-1]

                def one(i, number, slot):
                    sp.wait_ge(lo_done, layer + number + 1)
                    sp.dma_start(raw[:, slot, 0:width], src[i]).then_inc(raw_loaded[slot], 16)

                pairs = count // 2 if count >= 4 else 0
                if pairs:
                    with sp.Fori(0, pairs) as i:
                        for j in range(2):
                            one(i * 2 + j, i * 2 + (first + j), (first + j) % 2)
                for j in range(2 * pairs, count):
                    one(j, first + j, (first + j) % 2)
                return first + count

            n = 0
            for name in SEGMENTS1:
                n = load(dram["w_" + name], 0, n, dram["w_" + name].shape[0])
            assert n == N_MERGE
            with sp.Fori(0, 24) as i:
                sp.wait_ge(lo_done, i * 2 + (N_MERGE + 1))
                sp.dma_start(raw[:, 0, :], dram["w_gate"][i]).then_inc(raw_loaded[0], 16)
                sp.wait_ge(lo_done, i * 2 + (N_MERGE + 2))
                sp.dma_start(raw[:, 1, 0:512], dram["w_branch"][i]).then_inc(raw_loaded[1], 16)
            load(dram["w_rest1"], 0, N_O, 8 + 64)
            with sp.Fori(0, LAYERS) as l:
                n = N_BLOCK1
                for name in SEGMENTS2:
                    src = dram["w_" + name][l]
                    n = load(src, l * PER_LAYER, n, src.shape[0])
                assert n == N_BLOCK1 + PER_LAYER
            load(dram["w_in1"][0:LOOK], 0, N_PANELS, LOOK)
            sp.wait_ge(lo_done, N_PANELS + LOOK + 2)

        @blk.tensor
        def _(pe):
            pe.wait_ge(started, 1)

            def products(dst, w, src, start, stop):
                nc.tensor.matmul(dst, w[0], src[0], start=start, stop=False)
                nc.tensor.matmul(dst, w[0], src[1], start=False, stop=False)
                return nc.tensor.matmul(dst, w[1], src[0], start=False, stop=stop)

            def tile_products(dst, slot, unit, width, k_tiles, src, base=0, ready=None, part=None):
                first = ready[2] if ready and len(ready) == 3 else 0
                for k in part or range(k_tiles):
                    if ready and k >= first:
                        pe.wait_ge(ready[0], ready[1] + (k + 1 - first))
                    cut = slice(unit + k * width, unit + (k + 1) * width)
                    last = products(dst, (w_hi[:, slot, cut], w_lo[:, slot, cut]),
                                    (src[0][:, base + k, :], src[1][:, base + k, :]), k == 0, k == k_tiles - 1)
                return last

            act_in, y_in, merged_in = (act_hi, act_lo), (y_hi, y_lo), (merged_hi, merged_lo)

            def gemm(layer, first, count, k_tiles, src, ready=None):
                def one(n, slot, ready):
                    pe.wait_ge(lo_done, n + 3)
                    pe.wait_ge(acc_free, n + 1)
                    tile_products(acc[:, slot, :], slot, 0, P, k_tiles, src, 0, ready).then_inc(gemm_done, 1)

                fours = count // 4 if count >= 8 else 0
                if fours:
                    with pe.Fori(0, fours) as i:
                        for j in range(4):
                            one(layer + i * 4 + (first + j), (first + j) % 4, ready if j == 0 else None)
                for j in range(4 * fours, count):
                    one(layer + (first + j), (first + j) % 4, ready if j == 0 else None)

            def transpose_values(name, pair, bank, src=vstage):
                for t in range(TT):
                    last = nc.tensor.transpose(bank[:, t * P:(t + 1) * P], src[:, t * P:(t + 1) * P], c["ident"])
                last.then_inc(S(name + "_vt"), 1)

            def norm(r):
                if isinstance(r, int) and r == 0:
                    pe.wait_ge(S("const_loaded"), 32)
                pe.wait_ge(S("norm_total"), r + 1)
                nc.tensor.matmul(sc[:, 0, :], c["ones"], probs[:, 0, :], start=True, stop=True).then_inc(S("norm_sum"), 1)

            def normed_gemm(layer, first, count, r, split):
                gemm(layer, first, 1, KD, act_in, (S("norm_split"), split * 8))
                norm(r)
                gemm(layer, first + 1, count - 1, KD, act_in)

            def softmax_pair(pair, scores_of, values=None, guest=None, staged=None, src=vstage):
                unit0 = pair * 8

                def outputs(u):
                    hh, qt = divmod(u, 4)
                    rows = slice(HD * hh, HD * hh + HD)
                    pe.wait_ge(S("soft_tcopy", 1), unit0 + (u + 2))
                    if u == 0:
                        pe.wait_ge(S("soft_ofree", 1), pair + 1)
                        if values is not None:
                            pe.wait_ge(S("soft_v"), values + 1)
                        else:
                            pe.wait_ge(S("c_v"), staged + 1)
                    for kb in range(qt + 1):
                        last = nc.tensor.matmul(po[rows, qt * P:(qt + 1) * P], vcur[:, kb, rows],
                                                probs_t[:, u % 2, kb * P:(kb + 1) * P], start=kb == 0, stop=kb == qt)
                    last.then_inc(S("soft_pv", 2), 1)

                def transposes(u):
                    pe.wait_ge(S("soft_p"), unit0 + (u + 1))
                    pe.wait_ge(S("soft_tcopy", 1), unit0 + (u + 1))
                    for kb in range(u % 4 + 1):
                        last = nc.tensor.transpose(pt[:, kb * P:(kb + 1) * P], probs[:, u % 2, kb * P:(kb + 1) * P],
                                                   c["ident"])
                    last.then_inc(S("soft_t", 2), 1)

                for u in range(8 + 2):
                    if u < 8:
                        pe.wait_ge(S("soft_exp", 2), unit0 + (u + 1))
                        scores_of(u).then_inc(S("soft_s"), 1)
                    if u < 8 and guest:
                        guest(u)
                    if u == 0 and values is not None:
                        pe.wait_ge(S("soft_ofree", 1), pair + 1)
                        transpose_values("soft", pair, po, src)
                    if 1 <= u <= 8:
                        transposes(u - 1)
                    if u >= 2:
                        outputs(u - 2)

            def guest_panels(n0, slot0):
                def half(u):
                    n, slot = n0 + u // 2, (slot0 + u // 2) % 4
                    if u % 2 == 0:
                        pe.wait_ge(lo_done, n + 3)
                        pe.wait_ge(acc_free, n + 1)
                        tile_products(acc[:, slot, :], slot, 0, P, KD, act_in, part=range(0, 4))
                    else:
                        tile_products(acc[:, slot, :], slot, 0, P, KD, act_in, part=range(4, KD)).then_inc(gemm_done, 1)
                return half

            def head_scores(u, wide):
                hh, qt = divmod(u, 4)
                kw = (qt + 1) * P
                rows, b = (slice(0, wide), hh) if wide else (slice(HD * hh, HD * hh + HD), 0)
                nc.tensor.matmul(sc[:, u % 2, 0:kw], qcur[rows, b, qt * P:kw], kcur[rows, b, 0:kw],
                                 start=True, stop=False)
                return hh, qt, kw

            def add_mask(u, qt, name):
                return nc.tensor.matmul(sc[:, u % 2, qt * P:(qt + 1) * P], c["ident"], c[name], start=False, stop=True)

            def scores_a(u):
                hh, qt, kw = head_scores(u, False)
                nc.tensor.matmul(sc[:, u % 2, 0:kw], c["anti"], tab[:, hh, T - kw:T], start=False, stop=False)
                return add_mask(u, qt, "mask")

            def scores_c(u):
                hh, qt, kw = head_scores(u, QH)
                return add_mask(u, qt, "mask")

            def scores_f(u):
                hh, qt, kw = head_scores(u, HD + 2)
                return add_mask(u, qt, "mask")

            def linear_outputs(name, pair, piece):
                pe.wait_ge(S(name + "_st", 1), pair + 2)
                pe.wait_ge(S(name + "_ofree", 1), pair + 1)
                for hh in range(2):
                    rows = slice(HD * hh, HD * hh + HD)
                    for it in range(TT):
                        for jt in range(it + 1):
                            last = nc.tensor.matmul(po[rows, it * P:(it + 1) * P], vcur[:, jt, rows],
                                                    piece(hh, jt, it), start=jt == 0, stop=jt == it)
                last.then_inc(S(name + "_pv"), 1)

            def head_mean(ready, count, done, p, src):
                pe.wait_ge(S(ready), count)
                nc.tensor.matmul(mean_bank[p], c["head_mean"], src, start=True, stop=True).then_inc(S(done), 1)

            normed_gemm(0, N_A, 12, 0, 0)
            with pe.Fori(0, PAIRS) as p:
                pe.wait_ge(S("soft_stage"), p + 1)
                pe.wait_ge(S("a_bias"), p * 16 + 16)
                softmax_pair(p, scores_a, p, guest_panels(p * 4 + N_B, N_B))
            pe.wait_ge(acc_free, N_C + 4)

            def hgrn_piece(hh, jt, it):
                if jt == it:
                    return s_diag[:, hh, jt, :]
                if it // 2 == jt // 2:
                    return s_128[:, hh, jt // 2, :]
                return s_256[:, hh, jt, (it - 2) * P:(it - 1) * P]

            with pe.Fori(0, PAIRS) as p:
                pe.wait_ge(S("b_stage"), p + 1)
                transpose_values("b", p, pt)
                for v, half in enumerate(LEVELS):
                    if v:
                        pe.wait_ge(S("b_x", 1), p * 9 + (v + 1))
                    for i in range(level_units[v]):
                        unit = first_unit[v] + i
                        bank = lev_bank[unit % 4]
                        pe.wait_ge(S("b_sfree", 4), p * first_unit[-1] + (unit + 1))
                        x_keys, x_q = tab[:, v % 2, :], x_queries[:, v % 2, :]
                        if half == 0:
                            rows = slice(HD * i, HD * i + HD)
                            cuts = [(kcur[rows, 0, t * P:(t + 1) * P], qcur[rows, 0, t * P:(t + 1) * P],
                                     bank[:, t * P:(t + 1) * P]) for t in range(TT)]
                        elif half == 256:
                            cuts = [(x_keys[:, i * P:(i + 1) * P], x_q, bank)]
                        else:
                            n_cuts = min(TT, T // (2 * half))
                            w = T // 2 // n_cuts
                            by_cut = x_q.rearrange("p (hh t i) -> p t hh i", hh=2, i=w)
                            cuts = [(x_keys[:, t * 2 * w:t * 2 * w + P], by_cut[:, t, :, :],
                                     bank[:, t * 2 * w:(t + 1) * 2 * w].rearrange("p (hh i) -> p hh i", i=w))
                                    for t in range(n_cuts)]
                        for keys, queries, dst in cuts:
                            last = nc.tensor.matmul(dst, keys, queries, start=True, stop=True)
                        last.then_inc(S("b_s"), 1)
                linear_outputs("b", p, hgrn_piece)
            pe.wait_ge(S("b_ofree", 1), PAIRS + 1)

            for i in range(4):
                gemm(0, N_C + i, 1, KD, act_in)
            for first, count in ((0, 2), (2, 1)):
                for k in range(first, first + count):
                    pe.wait_ge(S("c_sq"), k + 1)
                    last = nc.tensor.matmul(acc[:, first // 2, :], c["ones"], wa[:, 4 + k, :],
                                            start=k == first, stop=k == first + count - 1)
                last.then_inc(S("c_sum"), 1)
            pe.wait_ge(S("c_rotin"), 1)
            nc.tensor.matmul(acc[:, 3, :], c["rope"], wa[:, 7, :], start=True, stop=True).then_inc(S("c_rot"), 1)
            for p in range(PAIRS):
                head_mean("b_sq", p + 1, "b_mean", p, b_stat[p])
            pe.wait_ge(S("c_ln"), 1)
            pe.wait_ge(S("c_rotfree"), 1)
            for q, tiles in ((0, 4), (1, 2)):
                n, slot = N_UP + q, (N_UP + q) % 4
                pe.wait_ge(lo_done, n + 3)
                pe.wait_ge(acc_free, n + 4)
                for h in range(tiles):
                    last = tile_products(acc[:, h, :], slot, h * 2 * P, P, 2, y_in, 8,
                                         (S("cn_split"), 0) if h + q == 0 else None)
                last.then_inc(gemm_done, 1)
            pe.wait_ge(S("cn_split"), 3)
            n, slot = N_UP + 2, (N_UP + 2) % 4
            pe.wait_ge(lo_done, n + 3)
            pe.wait_ge(acc_free, n + 4)
            for h in range(4):
                last = tile_products(acc[:, h, :], slot, h * P, P, 1, y_in, 10)
            last.then_inc(gemm_done, 1)
            n, slot = N_UP + 3, (N_UP + 3) % 4
            pe.wait_ge(lo_done, n + 3)
            pe.wait_ge(acc_free, n + 4)
            for t in range(TT):
                cut = slice(t * P, (t + 1) * P)
                last = products(acc[:, t, :], (y_hi[:, 10, cut], y_lo[:, 10, cut]),
                                (w_hi[:, slot, 0:512], w_lo[:, slot, 0:512]), True, True)
            last.then_inc(gemm_done, 1)
            pe.wait_ge(S("c_rotin"), 2)
            pe.wait_ge(S("b_rstd"), PAIRS)
            for m, bank in enumerate((po, pt)):
                nc.tensor.matmul(bank[:, :], c["rope"], wv[:, m, :], start=True, stop=True).then_inc(S("c_rot"), 1)
            pe.wait_ge(S("c_rstd"), 2)
            for t in range(TT):
                last = nc.tensor.matmul(sc[:, 0, t:t + 1], probs[0:1, 1, t * P:(t + 1) * P],
                                        consts[0:1, CONSTS.index("ones"), 0:1], start=True, stop=True)
            last.then_inc(S("c_cols"), 1)
            pe.wait_ge(S("c_rotused"), 2)
            pe.wait_ge(S("b_y"), PAIRS)
            with pe.Fori(0, PAIRS) as p:
                def merge_ab(u):
                    n, slot = p * 8 + (N_MERGE + u), (N_MERGE + u) % 4
                    pe.wait_ge(lo_done, n + 3)
                    pe.wait_ge(acc_free, n + 1)
                    if u % 2 == 0:
                        last = tile_products(acc[:, slot, :], slot, 0, P, KD, act_in)
                    else:
                        last = tile_products(acc[:, slot, :], slot, 0, P, 4, y_in, 4 * (u // 2 % 2))
                    last.then_inc(gemm_done, 1)

                pe.wait_ge(S("soft_stage"), p + 5)
                softmax_pair(p + 4, scores_c, guest=merge_ab, staged=p)

            pe.wait_ge(S("soft_y"), 2 * PAIRS)
            with pe.Fori(0, 4) as i:
                for j in range(4):
                    n, slot = i * 4 + (N_MERGE + 32 + j), (N_MERGE + j) % 4
                    pe.wait_ge(lo_done, n + 3)
                    pe.wait_ge(acc_free, n + 1)
                    if j % 2 == 0:
                        last = tile_products(acc[:, slot, :], slot, 0, P, KD, act_in)
                    else:
                        last = tile_products(acc[:, slot, :], slot, 0, P, 4, y_in, 8)
                    last.then_inc(gemm_done, 1)
            gemm(0, N_O, 8, KD, merged_in, (S("m_split"), 0))
            norm(1)
            with pe.Fori(0, 4) as i:
                gemm(i * 16, N_FF, 8, KD, act_in, (S("norm_split"), 8))
                gemm(i * 16, N_FF + 8, 8, KD, y_in, (S("g_split"), i * 8))
            norm(2)
            pe.wait_ge(S("const_loaded"), 48)

            with pe.Fori(0, LAYERS) as l:
                layer = l * PER_LAYER
                normed_gemm(layer, N_BLOCK1 + O_FL, 13, l * 3 + 3, l * 3 + 2)
                with pe.Fori(0, PAIRS) as p:
                    pair = l * 4 + p
                    pe.wait_ge(S("soft_stage"), pair + 9)
                    pe.wait_ge(S("f_aug"), pair * 32 + 32)
                    halves_r = guest_panels(layer + p * 4 + (N_BLOCK1 + O_R), O_R)

                    def guest_r(u):
                        halves_r(u)
                        if u in (4, 6):
                            j = u // 2 - 2
                            pe.wait_ge(S("r_qk"), pair * 2 + (j + 1))
                            nc.tensor.matmul(acc[:, (O_R + j) % 4, :], c["rope"], wa[:, p + 4 * j, :],
                                             start=True, stop=True).then_inc(S("r_rot"), 1)

                    softmax_pair(pair + 8, scores_f, pair + 4, guest_r, src=vstage_f)
                pe.wait_ge(acc_free, layer + (N_BLOCK1 + O_O + 4))
                settle(pe)
                with pe.Fori(0, PAIRS) as p:
                    pair = l * 4 + p
                    pe.wait_ge(S("r_stage"), pair + 1)
                    transpose_values("r", pair, acc[:, 2, :])
                    for u in range(8):
                        hh, jt = divmod(u, 4)
                        rows = slice(HD * hh, HD * hh + HD)
                        pe.wait_ge(S("r_sfree", 4), pair * 8 + (u + 1))
                        nc.tensor.matmul(lev_bank[u % 4][:, 0:T - jt * P], kcur[rows, 0, jt * P:(jt + 1) * P],
                                         qcur[rows, 0, jt * P:T], start=True, stop=True).then_inc(S("r_s"), 1)
                    linear_outputs("r", pair,
                                   lambda hh, jt, it: s_ret[hh][:, s_off[jt] + (it - jt) * P:
                                                                s_off[jt] + (it - jt + 1) * P])
                pe.wait_ge(S("r_ofree", 1), l * 4 + 5)
                settle(pe)
                for p in range(PAIRS):
                    head_mean("r_o", l * 4 + (p + 1), "r_mean", p, wa[:, p, :])
                for p in range(PAIRS):
                    head_mean("r_sq", l * 4 + (p + 1), "r_var", p, wb[:, p, :])
                gemm(layer, N_BLOCK1 + O_O, 8, KD, y_in, (S("r_y"), l * 4, 4))
                done = 0
                for ch, tiles in enumerate(CHUNKS2):
                    first = N_BLOCK1 + O_FFN[ch]
                    if ch == 0:
                        normed_gemm(layer, first, 2 * tiles, l * 3 + 4, l * 3 + 3)
                    else:
                        gemm(layer, first, 2 * tiles, KD, act_in)
                    gemm(layer, first + 2 * tiles, 8, tiles, y_in, (S("h_split"), l * FT2 + done))
                    done += tiles
                normed_gemm(layer, N_BLOCK1 + O_GATE, 8, l * 3 + 5, l * 3 + 4)
                pe.wait_ge(S("e_split"), l * 2 + 2)
                for q in range(3):
                    n, slot = layer + (N_BLOCK1 + O_PLE + q), (O_PLE + q) % 4
                    pe.wait_ge(lo_done, n + 3)
                    pe.wait_ge(acc_free, n + 4)
                    for m in range(3 if q < 2 else 2):
                        last = tile_products(acc[:, m, :], slot, m * 2 * P, P, 2, y_in, 8)
                    last.then_inc(gemm_done, 1)
            norm(9)

        @blk.scalar
        def _(act):
            act.dma_start(params[:, :], dram["params"]).then_inc(S("param_loaded"), 16)
            for k in range(KD):
                act.dma_start(x[:, k, :], dram["x"][:, k, :]).then_inc(x_loaded[k], 16)
            act.dma_start(consts[:, :, :], dram["consts"]).then_inc(S("const_loaded"), 16)
            act.dma_start(masks[:, :, :], dram["masks"]).then_inc(S("const_loaded"), 16)
            act.wait_ge(started, 1)

            def high(half, full, number):
                act.wait_ge(raw_loaded[number % 2], (half + number // 2) * 16 + 16)
                act.wait_ge(gemm_done, high_free(full + number))
                nc.scalar.copy(w_hi[:, number % 4, :], raw[:, number % 2, :]).then_inc(hi_done, 1)

            def split_ahead(half, full, first, count, body=None):
                fours = count // 4 if count >= 8 else 0
                if fours:
                    with act.Fori(0, fours) as i:
                        for j in range(4):
                            high(half + i * 2, full + i * 4, first + LOOK + j)
                            if body:
                                body(i * 4 + j, j % 2)
                for j in range(4 * fours, count):
                    high(half, full, first + LOOK + j)
                    if body:
                        body(j, j % 2)

            def high_of_tile(name, k, dst, src):
                act.wait_ge(S(name + "_h"), k + 1)
                nc.scalar.copy(dst, src).then_inc(S(name + "_hi"), 1)

            def factor(dst, src, scale, eps):
                nc.scalar.activation(dst, src, ACT.Ln, bias=par(eps), scale=scale)
                act.drain()
                return nc.scalar.activation(dst, dst, ACT.Exp, scale=-0.5)

            def norm_tile(r, k, odd, split=None, gains=None, i0=0):
                if isinstance(r, int) and r == 0:
                    act.wait_ge(x_loaded[k], 16)
                else:
                    act.wait_ge(S("norm_x"), (r - 1) * 8 + k + 1)
                    settle(act)
                if split is not None:
                    nc.scalar.activation(act_hi[:, k, :], x[:, k, :], ACT.Copy,
                                         scale=par(gains, i0 + k)).then_inc(S("norm_hi"), 1)
                act.wait_ge(S("norm_added", 2), r * 8 + k + 1)
                settle(act)
                nc.scalar.activation(probs_t[:, odd, :], x[:, k, :], ACT.Square).then_inc(S("norm_sq"), 1)

            def norm_factor(r):
                act.wait_ge(S("norm_sum"), r + 1)
                factor(rstd[:, :], sc[:, 0, :], 1.0 / D, "eps").then_inc(S("norm_rstd"), 1)

            def norm(r, split=None, gains=None, i0=0):
                for k in range(KD):
                    norm_tile(r, k, k % 2, split, gains, i0)
                norm_factor(r)

            def softmax_pair(pair, guest=None, work=None, every=2):
                unit0 = pair * 8

                def expo(u):
                    kw = (u % 4 + 1) * P
                    act.wait_ge(S("soft_max"), unit0 + (u + 1))
                    act.wait_ge(S("soft_t", 2), unit0 + (u + 1))
                    nc.scalar.activation(probs[:, u % 2, 0:kw], sc[:, u % 2, 0:kw], ACT.Exp, bias=neg_max[u % 2],
                                         accum_out=prob_sum[u % 2]).then_inc(S("soft_exp", 2), 1)

                def copy_t(u):
                    kw = (u % 4 + 1) * P
                    act.wait_ge(S("soft_t", 2), unit0 + (u + 3))
                    act.wait_ge(S("soft_pv", 2), unit0 + (u + 1))
                    nc.scalar.copy(probs_t[:, u % 2, 0:kw], pt[:, 0:kw]).then_inc(S("soft_tcopy", 1), 1)

                for u in range(9):
                    if u < 8:
                        expo(u)
                        if guest and u % every == 0:
                            guest(u // every)
                    if u >= 1:
                        copy_t(u - 1)
                    if work:
                        work(u)

            def in_place(func, ready, done, k, tile, **kw):
                act.wait_ge(S(ready), k + 1)
                settle(act)
                nc.scalar.activation(tile, tile, func, **kw).then_inc(S(done), 1)

            high(0, 0, 0)
            high(0, 0, 1)
            act.wait_ge(S("param_loaded"), 16)
            norm(0, 0, "mix_g")
            in_place(ACT.Exp, "b_lb", "b_lbexp", 0, lower)
            split_ahead(0, 0, N_A, 12)
            act.dma_start(tab[:, :, :], dram["bias"][0]).then_inc(S("a_bias"), 16)

            def pair_a(p, last):
                def gates_b(u):
                    tmp = decay_tmp[:, :]
                    if u == 7 and not last:
                        act.dma_start(tab[:, :, :], dram["bias"][p + 1]).then_inc(S("a_bias"), 16)
                    if u == 5:
                        act.wait_ge(S("b_z"), p + 1)
                        settle(act)
                        nc.scalar.activation(wa[:, p + 4, :], wb[:, p, :], ACT.Sigmoid, scale=-1.0).then_inc(S("b_key"), 1)
                        nc.scalar.activation(tmp, tmp, ACT.Exp)
                        act.drain()
                        nc.scalar.activation(tmp, tmp, ACT.Ln, bias=par("one")).then_inc(S("b_softplus"), 1)
                    if u == 8:
                        in_place(ACT.Exp, "b_neglog", "b_inv", p, tmp)
                        in_place(ACT.Ln, "b_mixed", "b_mixedlog", p, tmp)
                        in_place(ACT.Silu, "b_g", "b_gsilu", p, wb[:, p + 4, :])
                        nc.scalar.activation(wa[:, p, :], wa[:, p, :], ACT.Silu).then_inc(S("b_qsilu"), 1)

                softmax_pair(p, lambda j: high(p * 2, p * 4, N_B + LOOK + j), gates_b)

            each_of_four(act, pair_a)

            with act.Fori(0, PAIRS) as p:
                for v in range(1, len(LEVELS)):
                    e = kcur[:, 1, :] if v % 2 else qcur[:, 1, :]
                    in_place(ACT.Exp, "b_d", "b_e", p * 9 + (v - 1), e)

            act.wait_ge(S("b_ofree", 1), PAIRS + 1)
            act.dma_start(positions[:, :], dram["positions"].partition_broadcast(P)).then_inc(S("pos_loaded"), 16)
            for p in range(PAIRS):
                nc.scalar.activation(b_stat[p], wb[:, p, :], ACT.Square).then_inc(S("b_sq"), 1)

            def latent(j, odd):
                if j:
                    k = j - 1
                    act.wait_ge(S("c_raw"), k + 1)
                    nc.scalar.activation(y_hi[:, 8 + k, :], wv[:, k, :], ACT.Copy,
                                         scale=par("q_g", k) if k < 2 else par("kv_g")).then_inc(S("cn_hi"), 1)
                    nc.scalar.activation(wa[:, 4 + k, :], wv[:, k, :], ACT.Square).then_inc(S("c_sq"), 1)

            split_ahead(0, 0, N_C, 4, latent)
            c_stats = [(probs[:, 0, :], acc[:, 0, :], 1.0 / QR), (probs[:, 1, :], acc[:, 1, :], 1.0 / KVR)]
            b_stats = [(b_stat[p], mean_bank[p], 1.0) for p in range(PAIRS)]
            act.wait_ge(S("c_sum"), 2)
            for dst, bank, scale in c_stats:
                last = nc.scalar.activation(dst, bank, ACT.Ln, bias=par("eps"), scale=scale)
            last.then_inc(S("c_ln"), 1)
            act.wait_ge(S("b_mean"), PAIRS)
            for dst, bank, scale in b_stats:
                nc.scalar.activation(dst, bank, ACT.Ln, bias=par("eps"), scale=scale)
            split_ahead(0, 0, N_UP, 2)
            act.drain()
            for i, (dst, _, _) in enumerate(c_stats + b_stats):
                nc.scalar.activation(dst, dst, ACT.Exp, scale=-0.5).then_inc(S("c_rstd" if i < 2 else "b_rstd"), 1)
            for k in range(2):
                in_place(ACT.Sin, "c_angle", "c_sincos", k, tab[:, k, :])
            split_ahead(0, 0, N_UP + 2, 2)
            with act.Fori(0, PAIRS) as p:
                def gate_ab(u):
                    if u % 2:
                        in_place(ACT.Sigmoid, "m_z", "m_gate", p * 4 + u // 2, tab[:, 0, :])

                softmax_pair(p + 4, lambda j: high(p * 4, p * 8, N_MERGE + LOOK + j), gate_ab, 1)

            with act.Fori(0, 4) as i:
                for j in range(4):
                    high(i * 2, i * 4, N_MERGE + 32 + LOOK + j)
                    if j % 2 == 0:
                        in_place(ACT.Sigmoid, "m_z", "m_gate", i * 2 + (16 + j // 2), probs[:, j // 2 % 2, :])
                    else:
                        high_of_tile("m", i * 2 + j // 2, merged_hi[:, i * 2 + j // 2, :], probs_t[:, 1, :])
            split_ahead(0, 0, N_O, 8, lambda k, odd: norm_tile(1, k, odd, 1, "ffn_g"))
            norm_factor(1)

            def hidden_chunk(i, last):
                with act.Fori(0, 2) as ii:
                    for j in range(4):
                        high(i * 8 + ii * 2, i * 16 + ii * 4, N_FF + LOOK + j)
                        high_of_tile("g", i * 8 + ii * 4 + j, y_hi[:, ii * 4 + j, :], probs[:, 0, :])
                split_ahead(i * 8, i * 16, N_FF + 8, 8, lambda k, odd: norm_tile(2, k, odd) if last else None)

            each_of_four(act, hidden_chunk)
            act.dma_start(consts[:, 4:6, :], dram["consts2"]).then_inc(S("const_loaded"), 16)
            norm_factor(2)

            with act.Fori(0, LAYERS) as l:
                half, full = l * (PER_LAYER // 2), l * PER_LAYER
                norm(l * 3 + 3, l * 3 + 2, "attn_w", l * KD)
                split_ahead(half, full, N_BLOCK1 + O_FL, 3)
                fl = wb[0:8, 6, :]
                act.wait_ge(S("f_z"), l + 1)
                nc.scalar.activation(fl, fl, ACT.Exp)
                act.drain()
                nc.scalar.activation(fl, fl, ACT.Ln, bias=par("one", rows=8)).then_inc(S("f_softplus"), 1)
                act.wait_ge(S("f_cum"), l + 1)
                act.dma_start(cum_dram[0], wb[0:8, 6, :]).then_inc(S("cum_stored"), 16)
                act.dma_start(cum_dram[1], wb[0:8, 7, :]).then_inc(S("cum_stored"), 16)
                split_ahead(half, full, N_BLOCK1 + O_F + 2, 10)
                act.dma_start(tab[:, :, :], dram["rotary"]).then_inc(S("rotary_loaded"), 16)
                act.wait_ge(S("cum_stored"), l * 32 + 32)

                def aug_rows(p):
                    act.dma_start(qcur[HD:HD + 1, :, :], cum_dram[0:1, bass.ds(p * 2, 2), :]).then_inc(S("f_aug"), 16)
                    act.dma_start(kcur[HD + 1:HD + 2, :, :], cum_dram[1:2, bass.ds(p * 2, 2), :]).then_inc(S("f_aug"), 16)

                aug_rows(0)

                def pair_f(p, last):
                    pair = l * 4 + p

                    def gates_r(u):
                        if u == 7 and not last:
                            aug_rows(p + 1)
                        if u == 8:
                            in_place(ACT.Silu, "r_g", "r_gsilu", pair, wb[:, p + 4, :])

                    softmax_pair(pair + 8, lambda j: high(half + p * 2, full + p * 4, N_BLOCK1 + O_R + LOOK + j), gates_r)

                each_of_four(act, pair_f)
                act.wait_ge(S("r_rotused"), l * 8 + 8)
                settle(act)
                with act.Fori(0, PAIRS) as p:
                    pair = l * 4 + p
                    act.wait_ge(S("r_st", 1), pair + 1)
                    act.dma_start(tab[:, :, :], dram["decay"][p]).then_inc(S("decay_loaded"), 16)
                for p in range(PAIRS):
                    act.wait_ge(S("r_d"), l * 4 + (p + 1))
                    nc.scalar.activation(wb[:, p, :], wa[:, p, :], ACT.Square).then_inc(S("r_sq"), 1)
                for p in range(PAIRS):
                    act.wait_ge(S("r_var"), l * 4 + (p + 1))
                    factor(wb[:, p, :], mean_bank[p], 1.0, "gn_eps").then_inc(S("r_rstd"), 1)
                split_ahead(half, full, N_BLOCK1 + O_O, 8,
                            lambda k, odd: norm_tile(l * 3 + 4, k, odd, l * 3 + 3, "ffn_w", l * KD))
                norm_factor(l * 3 + 4)
                act.dma_start(wv[:, 0:2, :], dram["p"][l]).then_inc(S("e_loaded"), 16)
                done = 0
                for ch, count in enumerate(CHUNKS2):
                    first = N_BLOCK1 + O_FFN[ch]
                    with act.Fori(0, count // 2) as i:
                        for j in range(4):
                            high(half + i * 2, full + i * 4, first + LOOK + j)
                            if j % 2:
                                act.wait_ge(S("h_conv"), l * FT2 + i * 2 + (done + j // 2 + 1))
                                nc.scalar.activation(probs_t[:, 1, :], probs_t[:, 0, :],
                                                     ACT.Gelu).then_inc(S("h_gelu"), 1)
                                high_of_tile("h", l * FT2 + i * 2 + (done + j // 2), y_hi[:, i * 2 + j // 2, :],
                                             probs[:, 0, :])
                    split_ahead(half, full, first + 2 * count, 8, None if ch < 2 else
                                lambda k, odd: norm_tile(l * 3 + 5, k, odd, l * 3 + 4, "ple_w", l * KD))
                    done += count
                norm_factor(l * 3 + 5)
                act.wait_ge(S("e_loaded"), l * 16 + 16)
                for k in range(2):
                    nc.scalar.copy(y_hi[:, 8 + k, :], wv[:, k, :]).then_inc(S("e_hi"), 1)
                split_ahead(half, full, N_BLOCK1 + O_GATE, 8,
                            lambda j, odd: in_place(ACT.Sigmoid, "e_g", "e_gate", l * 8 + j, wa[:, j, :]))
                split_ahead(half, full, N_BLOCK1 + O_PLE, 3)
            norm(9)
            for k in range(KD):
                act.wait_ge(S("out_ready"), k + 1)
                act.dma_start(out[k * P:(k + 1) * P, :], wb[:, k, :]).then_inc(S("out_stored"), 16)
            act.wait_ge(S("out_stored"), 16 * KD)

        @blk.vector
        def _(dve):
            v = nc.vector
            dve.wait_ge(started, 1)
            dve.wait_ge(S("param_loaded"), 16)

            def each(layer, first, count, body):
                fours = count // 4 if count >= 8 else 0
                if fours:
                    with dve.Fori(0, fours) as i:
                        for j in range(4):
                            body(layer + i * 4 + (first + j), (first + j) % 4, i * 4 + j)
                for j in range(4 * fours, count):
                    body(layer + (first + j), (first + j) % 4, j)

            def evacuate(layer, first, count, dst_of, signal=None):
                def one(n, slot, i):
                    dve.wait_ge(gemm_done, panel_done(n))
                    v.tensor_tensor(dst_of(i), acc[:, slot, :], rstd[:, :], ALU.mult).then_inc(acc_free, 1)
                    if signal:
                        dve.drain().then_inc(S(signal), 1)
                each(layer, first, count, one)

            def add_to_x(layer, first, normed=None):
                def one(n, slot, i):
                    dve.wait_ge(gemm_done, panel_done(n))
                    v.tensor_tensor(x[:, i, :], x[:, i, :], acc[:, slot, :], ALU.add).then_inc(acc_free, 1)
                    if normed:
                        dve.drain().then_inc(S("norm_x"), 1)
                        norm_tile(normed[0], i, slot % 2 ^ first % 2, *normed[1:])
                if normed:
                    norm_start()
                each(layer, first, 8, one)
                if normed:
                    norm_end()

            def low_of_tile(name, k, src, hi, lo):
                dve.wait_ge(S(name + "_hi"), k + 1)
                v.tensor_tensor(lo, src, hi, ALU.subtract).then_inc(S(name + "_split"), 1)
                dve.drain()

            def norm_start():
                v.memset(probs[:, 0, :], 0.0)
                dve.drain()

            def norm_tile(r, k, odd, split=None, gains=None, i0=0):
                if split is not None:
                    dve.wait_ge(S("norm_hi"), split * 8 + k + 1)
                    v.scalar_tensor_tensor(act_lo[:, k, :], x[:, k, :], par(gains, i0 + k), act_hi[:, k, :],
                                           ALU.mult, ALU.subtract).then_inc(S("norm_split"), 1)
                dve.wait_ge(S("norm_sq"), r * 8 + k + 1)
                v.tensor_tensor(probs[:, 0, :], probs[:, 0, :], probs_t[:, odd, :],
                                ALU.add).then_inc(S("norm_added", 2), 1)

            def norm_end():
                dve.drain().then_inc(S("norm_total"), 1)

            def norm(r, split=None, gains=None, i0=0):
                norm_start()
                for k in range(KD):
                    norm_tile(r, k, k % 2, split, gains, i0)
                    dve.drain()
                norm_end()

            def split_here(src, tile, done):
                v.tensor_copy(y_hi[:, tile, :], src)
                dve.drain()
                v.tensor_tensor(y_lo[:, tile, :], src, y_hi[:, tile, :], ALU.subtract).then_inc(S(done), 1)

            def stage(name, p, scale=1.0):
                v.tensor_scalar(qcur[:, 0, :], wa[:, p, :], scale, None, ALU.mult)
                v.tensor_copy(kcur[:, 0, :], wa[:, p + 4, :])
                v.tensor_copy(vstage, wv[:, p, :])
                dve.drain().then_inc(S(name + "_stage"), 1)

            def copy_values(name, pair, bank):
                dve.wait_ge(S(name + "_vt"), pair + 1)
                v.tensor_copy(vcur[:, :, :], bank.rearrange("p (t f) -> p t f", f=P)).then_inc(S(name + "_v"), 1)

            def guest(n, slot, dst, signal=None):
                dve.wait_ge(gemm_done, panel_done(n))
                v.tensor_tensor(dst, acc[:, slot, :], rstd[:, :], ALU.mult).then_inc(acc_free, 1)
                dve.drain()
                if signal:
                    dve.nop().then_inc(S(signal), 1)

            def softmax_pair(pair, tile, values=None, work=None, stage_next=None):
                unit0 = pair * 8

                def row_max(u):
                    kw = (u % 4 + 1) * P
                    dve.wait_ge(S("soft_s"), unit0 + (u + 1))
                    v.tensor_reduce(neg_max[u % 2], sc[:, u % 2, 0:kw], AX.X, ALU.max,
                                    negate=True).then_inc(S("soft_max"), 1)

                def normalise(u):
                    kw = (u % 4 + 1) * P
                    dve.wait_ge(S("soft_exp", 2), unit0 + (u + 3))
                    v.reciprocal(inv_sum[u % 2], prob_sum[u % 2])
                    dve.drain()
                    v.tensor_scalar(probs[:, u % 2, 0:kw], probs[:, u % 2, 0:kw], inv_sum[u % 2], None,
                                    ALU.mult).then_inc(S("soft_p"), 1)

                for u in range(9):
                    if u < 8:
                        row_max(u)
                    if u == 0 and values is not None:
                        copy_values("soft", values, po[:, :])
                    if u:
                        normalise(u - 1)
                    if u == 8 and stage_next:
                        stage_next()
                    if work:
                        work(u)
                dve.wait_ge(S("soft_pv", 2), unit0 + 10)
                v.tensor_copy(y_hi[:, tile, :], po[:, :])
                dve.drain()
                v.tensor_tensor(y_lo[:, tile, :], po[:, :], y_hi[:, tile, :], ALU.subtract)
                dve.drain().then_inc(S("soft_ofree", 1), 1)
                dve.nop().then_inc(S("soft_y"), 1)

            lb = params[:, PARAMS["lb"][0]:PARAMS["lb"][0] + PAIRS]
            v.tensor_tensor(lower, lb, lb, ALU.subtract).then_inc(S("b_lb"), 1)
            norm(0, 0, "mix_g", 0)
            dve.wait_ge(S("b_lbexp"), 1)
            v.reciprocal(rest, lower)
            dve.drain()
            v.tensor_tensor(lower, lower, rest, ALU.mult)
            dve.drain()
            v.tensor_tensor(lower, lower, lower, ALU.subtract)
            dve.drain()
            v.tensor_scalar(rest, lower, -1.0, 1.0, ALU.mult, ALU.add)
            dve.wait_ge(S("norm_rstd"), 1)
            evacuate(0, N_A, 8, lambda i: wa[:, i, :])
            evacuate(0, N_A + 8, 4, lambda i: wv[:, i, :])
            dve.drain()
            stage("soft", 0, HD ** -0.5)

            def pair_a(p, last):
                def gates_b(u):
                    n = p * 4 + N_B
                    z, key, tmp = wb[:, p, :], wa[:, p + 4, :], decay_tmp[:, :]
                    if u == 2:
                        guest(n, N_B % 4, wa[:, p, :])
                    if u == 4:
                        guest(n + 1, (N_B + 1) % 4, z)
                        v.scalar_tensor_tensor(tmp, z, -1.0, z, ALU.mult, ALU.min)
                        dve.drain().then_inc(S("b_z"), 1)
                    if u == 6:
                        guest(n + 2, (N_B + 2) % 4, wv[:, p, :])
                    if u == 7:
                        dve.wait_ge(S("b_softplus"), p + 1)
                        v.scalar_tensor_tensor(z, z, 0.0, tmp, ALU.min, ALU.subtract)
                        v.tensor_scalar(key, key, cols[:, bass.ds(p + 10, 1)], None, ALU.mult)
                        dve.drain()
                        v.tensor_scalar(tmp, z, -1.0, 40.0, ALU.mult, ALU.min).then_inc(S("b_neglog"), 1)
                    if u == 8:
                        dve.wait_ge(S("b_inv"), p + 1)
                        v.tensor_scalar(tmp, tmp, cols[:, bass.ds(p + 4, 1)], cols[:, bass.ds(p + 10, 1)],
                                        ALU.mult, ALU.add).then_inc(S("b_mixed"), 1)
                        guest(n + 3, (N_B + 3) % 4, wb[:, p + 4, :], "b_g")

                softmax_pair(p, p, p, gates_b, None if last else lambda: stage("soft", p + 1, HD ** -0.5))
                dve.wait_ge(S("b_mixedlog"), p + 1)
                v.tensor_tensor(wb[:, p, :], wb[:, p, :], decay_tmp[:, :], ALU.add)
                dve.drain()

            each_of_four(dve, pair_a)

            v.memset(resets[:, :, :], 1.0)
            v.memset(x_queries[0:HD, :, T // 2:T], 0.0)
            v.memset(x_queries[HD:P, :, 0:T // 2], 0.0)
            dve.drain()
            v.memset(resets[:, 0, :].rearrange("p (b h) -> p b h", h=CHUNK)[:, :, 0:1], 0.0)
            dve.wait_ge(S("b_qsilu"), 4)
            dve.drain()

            def stage_b(p):
                stage("b", p)
                v.tensor_tensor_scan(cums[:, 0, :], resets[:, 0, :], wb[:, p, :], 0.0, ALU.mult, ALU.add)
                for i, h in ((1, 128), (2, 256)):
                    for at in range(0, T, h):
                        v.tensor_tensor_scan(cums[:, i, at:at + h], resets[:, 1, at:at + h], wb[:, p, at:at + h],
                                             0.0, ALU.mult, ALU.add)
                dve.drain().then_inc(S("b_cum"), 1)

            def pair_b(p, last):

                def decayed(n):
                    h = LEVELS[n]
                    e = exponent_tile(n)
                    dve.wait_ge(S("b_e"), p * 9 + n)
                    (e0, e1), x0 = halves(e, h), halves(tab[:, n % 2, :], h)[0]
                    k0, q1 = halves(kcur[:, 0, :], h)[0], halves(qcur[:, 0, :], h)[1]
                    v.tensor_tensor(x0, e0, k0, ALU.mult)
                    for hh in range(2):
                        rows = slice(HD * hh, HD * hh + HD)
                        x1 = x_queries[rows, n % 2, hh * (T // 2):(hh + 1) * (T // 2)]
                        v.tensor_tensor(x1.rearrange("p (b h) -> p b h", h=h), e1[rows], q1[rows], ALU.mult)
                    dve.drain().then_inc(S("b_x", 1), 1)

                def collect(n):
                    h = LEVELS[n]
                    for i in range(level_units[n]):
                        unit = first_unit[n] + i
                        bank = lev_bank[unit % 4]
                        dve.wait_ge(S("b_s"), p * first_unit[-1] + (unit + 1))
                        settle(dve)
                        if h == 0:
                            ident = c["ident"].rearrange("p (o i) -> p o i", o=1).broadcast_to([P, TT, P])
                            last = v.tensor_tensor(s_diag[:, i, :, :], bank.rearrange("p (t i) -> p t i", i=P),
                                                   ident, ALU.mult)
                        elif h == 256:
                            last = v.tensor_copy(s_256[:, :, i, :], bank.rearrange("p (hh i) -> p hh i", i=256))
                        elif h == 128:
                            by_tile = bank.rearrange("p (t hh i) -> p t hh i", hh=2, i=P)
                            for hh in range(2):
                                last = v.tensor_copy(s_128[:, hh, :, :], by_tile[:, :, hh, :])
                        else:
                            mask = masks[:, n - 3, :].bitcast(U32).rearrange("p (o b h) -> p o b h", o=1, h=h)
                            by_tile = bank.rearrange("p (t hh b h) -> p t hh b h", t=TT, hh=2, h=h)
                            for hh in range(2):
                                dst = s_diag[:, hh, :, :].rearrange("p t (b two h) -> p t b two h", two=2, h=h)
                                last = v.copy_predicated(dst[:, :, :, 1, :], mask.broadcast_to([P, TT, P // (2 * h), h]),
                                                         by_tile[:, :, hh, :, :])
                        last.then_inc(S("b_sfree", 4), 1)

                copy_values("b", p, pt[:, :])
                for n in range(1, len(LEVELS)):
                    decayed(n)
                    collect(n - 1)
                dve.drain()
                collect(len(LEVELS) - 1)
                dve.drain().then_inc(S("b_st", 1), 1)
                if not last:
                    stage_b(p + 1)
                dve.wait_ge(S("b_pv"), p + 1)
                settle(dve)
                v.tensor_copy(wb[:, p, :], po[:, :])
                dve.drain().then_inc(S("b_ofree", 1), 1)

            stage_b(0)
            each_of_four(dve, pair_b)

            two_pi = 2.0 * np.pi
            c1 = 6.28125
            c2 = float(np.round((two_pi - c1) * 2 ** 22) / 2 ** 22)
            c3 = two_pi - c1 - c2
            magic = 1.5 * 2 ** 23
            ang, turn = probs_t[:, 0, :], probs_t[:, 1, :]
            dve.wait_ge(S("pos_loaded"), 16)
            v.tensor_copy(ang, positions[:, :])
            dve.drain()
            v.tensor_scalar(ang, ang, par("inv_freq"), None, ALU.mult)
            dve.drain()
            v.tensor_scalar(turn, ang, 1.0 / two_pi, magic, ALU.mult, ALU.add)
            dve.drain()
            v.tensor_scalar(turn, turn, magic, None, ALU.subtract)
            dve.drain()
            for part in (c1, c2, c3):
                v.scalar_tensor_tensor(ang, turn, -part, ang, ALU.mult, ALU.add)
                dve.drain()
            pi = 3.1415925
            v.tensor_scalar(tab[:, 0, :], ang, pi, -pi, ALU.min, ALU.max).then_inc(S("c_angle"), 1)
            v.tensor_scalar(ang, ang, 0.5 * np.pi, None, ALU.add)
            dve.drain()
            v.tensor_scalar(turn, ang, np.pi, -two_pi, ALU.is_gt, ALU.mult)
            dve.drain()
            v.tensor_tensor(ang, ang, turn, ALU.add)
            dve.drain()
            v.tensor_scalar(tab[:, 1, :], ang, pi, -pi, ALU.min, ALU.max).then_inc(S("c_angle"), 1)
            sin, cos = tab[:, 0, :], tab[:, 1, :]
            for k in range(4):
                if k < 3:
                    evacuate(0, N_C + k, 1, lambda i: wv[:, k, :], "c_raw")
                else:
                    evacuate(0, N_C + 3, 1, lambda i: wa[:, 7, :], "c_rotin")
                if k:
                    dve.wait_ge(S("cn_hi"), k)
                    v.scalar_tensor_tensor(y_lo[:, 7 + k, :], wv[:, k - 1, :], par("q_g", k - 1) if k < 3 else par("kv_g"),
                                           y_hi[:, 7 + k, :], ALU.mult, ALU.subtract).then_inc(S("cn_split"), 1)
            dve.wait_ge(S("c_rot"), 1)
            v.tensor_copy(wv[:, 3, :], acc[:, 3, :]).then_inc(S("c_rotfree"), 1)

            def head_norms_b(pairs):
                for p in pairs:
                    dve.wait_ge(S("b_rstd"), p + 1)
                    t = wb[:, p, :]
                    v.scalar_tensor_tensor(t, t, par("hgrn_g"), b_stat[p], ALU.mult, ALU.mult)
                    dve.drain()
                    v.tensor_tensor(t, t, wb[:, p + 4, :], ALU.mult)
                    dve.drain()
                    split_here(t, p + 4, "b_y")
                    dve.drain()

            def by_head(dst, k):
                factor = probs[:, k:k + 1, :].broadcast_to([P, 4, T])
                heads = dst[0:HD, :, :].rearrange("p (h two) t -> p h two t", two=2)
                v.tensor_tensor(heads[:, :, 0, :], acc[0:HD, :, :], factor[0:HD], ALU.mult)
                v.tensor_tensor(heads[:, :, 1, :], acc[HD:P, :, :], factor[HD:P], ALU.mult).then_inc(acc_free, 1)

            dve.wait_ge(gemm_done, panel_done(N_UP))
            dve.wait_ge(S("c_rstd"), 2)
            by_head(wa, 0)
            head_norms_b((0,))
            dve.wait_ge(gemm_done, panel_done(N_UP + 1))
            v.tensor_tensor(wv[:, 0:2, :], acc[:, 0:2, :], probs[:, 0:1, :].broadcast_to([P, 2, T]),
                            ALU.mult).then_inc(acc_free, 1)
            dve.drain().then_inc(S("c_rotin"), 1)
            head_norms_b((1, 2, 3))
            dve.wait_ge(gemm_done, panel_done(N_UP + 2))
            by_head(wb, 1)
            dve.wait_ge(S("c_sincos"), 2)
            key = slice(NOPE, QH)
            v.tensor_tensor(wv[key, 3, :], wv[key, 3, :], sin[key], ALU.mult)
            v.tensor_tensor(wa[key, 7, :], wa[key, 7, :], cos[key], ALU.mult)
            dve.drain()
            for b in range(2):
                v.tensor_tensor(kcur[key, b, :], wa[key, 7, :], wv[key, 3, :], ALU.add)
            dve.drain()
            for m, rot in enumerate((po, pt)):
                dve.wait_ge(S("c_rot"), 2 + m)
                v.tensor_tensor(probs_t[:, m, :], rot[:, :], sin, ALU.mult).then_inc(S("c_rotused"), 1)
                v.tensor_tensor(wv[:, m, :], wv[:, m, :], cos, ALU.mult)
                dve.drain()
                v.tensor_tensor(wv[:, m, :], wv[:, m, :], probs_t[:, m, :], ALU.add)
            dve.drain()
            for h in range(HEADS):
                v.tensor_copy(wa[key, h, :], wv[ROPE * (h % 4):ROPE * (h % 4 + 1), h // 4, :])
            dve.drain()
            dve.wait_ge(S("c_cols"), 1)
            v.tensor_copy(cols[:, 10:14], sc[:, 0, 0:TT])
            dve.drain()
            dve.wait_ge(gemm_done, panel_done(N_UP + 3))
            for t in range(TT):
                last = v.tensor_scalar(wv[:, t, :], acc[:, t, :], cols[:, 10 + t:11 + t], None, ALU.mult)
            last.then_inc(acc_free, 1)
            dve.drain()

            def stage_c(p):
                for b in range(2):
                    v.tensor_scalar(qcur[0:QH, b, :], wa[0:QH, p * 2 + b, :], QH ** -0.5, None, ALU.mult)
                    v.tensor_copy(kcur[0:NOPE, b, :], wb[0:NOPE, p * 2 + b, :])
                dve.drain().then_inc(S("soft_stage"), 1)

            def pair_c(p, last):
                v.tensor_copy(vcur[:, :, :], wv[:, :, bass.ds(p * P, P)]).then_inc(S("c_v"), 1)

                def merge_ab(u):
                    if not u:
                        return
                    j = u - 1
                    n, slot = p * 8 + (N_MERGE + j), (N_MERGE + j) % 4
                    gate, term, total = tab[:, 0, :], tab[:, 1, :], wa[:, p * 2 + j // 4, :]
                    if j % 2 == 0:
                        guest(n, slot, gate, "m_z")
                        return
                    dve.wait_ge(S("m_gate"), p * 4 + (j // 2 + 1))
                    dve.wait_ge(gemm_done, panel_done(n))
                    v.tensor_tensor(total if j % 4 == 1 else term, acc[:, slot, :], gate, ALU.mult).then_inc(acc_free, 1)
                    dve.drain()
                    if j % 4 == 3:
                        v.tensor_tensor(total, total, term, ALU.add)
                        dve.drain()

                softmax_pair(p + 4, p + 8, work=merge_ab, stage_next=None if last else lambda: stage_c(p + 1))

            stage_c(0)
            each_of_four(dve, pair_c)

            with dve.Fori(0, 4) as i:
                for b in range(2):
                    m = i * 2 + b
                    n = i * 4 + (N_MERGE + 32 + 2 * b)
                    gate = probs[:, b, :]
                    guest(n, (N_MERGE + 2 * b) % 4, gate, "m_z")
                    dve.wait_ge(S("m_gate"), m + 17)
                    dve.wait_ge(gemm_done, panel_done(n + 1))
                    total, term = probs_t[:, 1, :], probs_t[:, 0, :]
                    v.tensor_tensor(term, acc[:, (N_MERGE + 2 * b + 1) % 4, :], gate, ALU.mult).then_inc(acc_free, 1)
                    dve.drain()
                    v.tensor_tensor(total, wa[:, m, :], term, ALU.add)
                    dve.drain().then_inc(S("m_h"), 1)
                    low_of_tile("m", m, total, merged_hi[:, m, :], merged_lo[:, m, :])
            add_to_x(0, N_O, (1, 1, "ffn_g", 0))
            dve.wait_ge(S("norm_rstd"), 2)

            def hidden_chunk(i, last):
                def relu_squared(n, slot, j):
                    dve.wait_ge(gemm_done, panel_done(n))
                    v.scalar_tensor_tensor(probs[:, 1, :], acc[:, slot, :], 0.0, rstd[:, :],
                                           ALU.max, ALU.mult).then_inc(acc_free, 1)
                    dve.drain()
                    v.tensor_tensor(probs[:, 0, :], probs[:, 1, :], probs[:, 1, :], ALU.mult).then_inc(S("g_h"), 1)
                    low_of_tile("g", i * 8 + j, probs[:, 0, :], y_hi[:, j, :], y_lo[:, j, :])
                each(i * 16, N_FF, 8, relu_squared)
                add_to_x(i * 16, N_FF + 8, (2,) if last else None)

            each_of_four(dve, hidden_chunk)

            dve.wait_ge(S("norm_rstd"), 3)
            for k in range(KD):
                v.scalar_tensor_tensor(x[:, k, :], x[:, k, :], par("mid_g", k), rstd[:, :], ALU.mult,
                                       ALU.mult).then_inc(S("norm_x"), 1)
            dve.drain()

            with dve.Fori(0, LAYERS) as l:
                layer = l * PER_LAYER
                norm(l * 3 + 3, l * 3 + 2, "attn_w", l * KD)
                dve.wait_ge(S("norm_rstd"), l * 3 + 4)
                dve.wait_ge(gemm_done, panel_done(layer + (N_BLOCK1 + O_FL)))
                fz, ft, fneg, fone = (wb[0:8, i, :] for i in (5, 6, 7, 4))
                v.tensor_tensor(fz, acc[0:8, O_FL % 4, :], rstd[0:8, :], ALU.mult).then_inc(acc_free, 1)
                v.memset(wb[0:8, 4, :], 1.0)
                v.memset(qcur[aug, :, :], 1.0)
                v.memset(kcur[aug, :, :], 1.0)
                dve.drain()
                v.tensor_scalar(fz, fz, par("f_bias", l, 8), None, ALU.add)
                dve.drain()
                v.scalar_tensor_tensor(ft, fz, -1.0, fz, ALU.mult, ALU.min).then_inc(S("f_z"), 1)
                dve.wait_ge(S("f_softplus"), l + 1)
                v.scalar_tensor_tensor(fz, fz, 0.0, ft, ALU.min, ALU.subtract)
                dve.drain()
                v.tensor_tensor_scan(ft, fone, fz, 0.0, ALU.mult, ALU.add)
                dve.drain()
                v.tensor_scalar(fneg, ft, -1.0, None, ALU.mult).then_inc(S("f_cum"), 1)
                evacuate(layer, N_BLOCK1 + O_F, 8, lambda i: wa[:, i, :])
                evacuate(layer, N_BLOCK1 + O_F + 8, 4, lambda i: wv[:, i, :])
                dve.wait_ge(S("rotary_loaded"), l * 16 + 16)
                settle(dve)
                dve.drain()
                def stage_f(p):
                    for b in range(2):
                        head = slice(HD * b, HD * b + HD)
                        v.tensor_scalar(qcur[0:HD, b, :], wa[head, p, :], HD ** -0.5, None, ALU.mult)
                        v.tensor_copy(kcur[0:HD, b, :], wa[head, p + 4, :])
                    v.tensor_copy(vstage_f, wv[:, p, :])
                    dve.drain().then_inc(S("soft_stage"), 1)

                stage_f(0)

                def pair_f(p, last):
                    def projections_r(u):
                        n = layer + p * 4 + (N_BLOCK1 + O_R)
                        dst = (wa[:, p, :], wa[:, p + 4, :], wv[:, p, :], wb[:, p + 4, :])
                        if u in (2, 4):
                            j = u // 2 - 1
                            dve.wait_ge(gemm_done, panel_done(n + j))
                            v.tensor_tensor(dst[j], acc[:, (O_R + j) % 4, :], rstd[:, :], ALU.mult)
                            dve.drain().then_inc(S("r_qk"), 1)
                        if u in (5, 7):
                            j = u // 2 - 2
                            t, tmp = dst[j], rotated
                            v.tensor_tensor(t, t, tab[:, 1, :], ALU.mult)
                            dve.wait_ge(S("r_rot"), pair * 2 + (j + 1))
                            v.tensor_tensor(tmp, acc[:, (O_R + j) % 4, :], tab[:, 0, :], ALU.mult).then_inc(acc_free, 1)
                            dve.drain()
                            v.tensor_tensor(t, t, tmp, ALU.add).then_inc(S("r_rotused"), 1)
                            dve.drain()
                        if u in (6, 8):
                            j = u // 2 - 1
                            guest(n + j, (O_R + j) % 4, dst[j], "r_g" if j == 3 else None)

                    pair = l * 4 + p
                    softmax_pair(pair + 8, p, pair + 4, projections_r,
                                 None if last else lambda: stage_f(p + 1))

                each_of_four(dve, pair_f)

                dve.wait_ge(S("r_gsilu"), l * 4 + 4)
                settle(dve)
                dve.drain()
                stage("r", 0)

                def pair_r(p, last):
                    pair = l * 4 + p
                    copy_values("r", pair, acc[:, 2, :])
                    dve.wait_ge(S("decay_loaded"), pair * 16 + 16)
                    for u in range(8):
                        hh, jt = divmod(u, 4)
                        w = T - jt * P
                        dve.wait_ge(S("r_s"), pair * 8 + (u + 1))
                        v.tensor_tensor(s_ret[hh][:, s_off[jt]:s_off[jt] + w], lev_bank[u % 4][:, 0:w],
                                        tab[:, hh, 0:w], ALU.mult).then_inc(S("r_sfree", 4), 1)
                    dve.drain().then_inc(S("r_st", 1), 1)
                    if not last:
                        stage("r", p + 1)
                    dve.wait_ge(S("r_pv"), pair + 1)
                    settle(dve)
                    v.tensor_copy(wa[:, p, :], po[:, :])
                    dve.drain().then_inc(S("r_ofree", 1), 1)
                    dve.nop().then_inc(S("r_o"), 1)

                each_of_four(dve, pair_r)
                for p in range(PAIRS):
                    dve.wait_ge(S("r_mean"), l * 4 + (p + 1))
                    v.tensor_tensor(wa[:, p, :], wa[:, p, :], mean_bank[p], ALU.subtract).then_inc(S("r_d"), 1)
                for p in range(PAIRS):
                    o = wa[:, p, :]
                    dve.wait_ge(S("r_rstd"), l * 4 + (p + 1))
                    v.tensor_tensor(o, o, wb[:, p, :], ALU.mult)
                    dve.drain()
                    v.tensor_tensor(o, o, wb[:, p + 4, :], ALU.mult)
                    dve.drain()
                    split_here(o, p + 4, "r_y")
                    dve.drain()
                add_to_x(layer, N_BLOCK1 + O_O, (l * 3 + 4, l * 3 + 3, "ffn_w", l * KD))
                dve.wait_ge(S("norm_rstd"), l * 3 + 5)
                settle(dve)

                v.memset(padded[:, 0:2], 0.0)
                done = 0
                for ch, tiles in enumerate(CHUNKS2):
                    first = N_BLOCK1 + O_FFN[ch]
                    with dve.Fori(0, tiles // 2) as i:
                        for j in range(2):
                            n = layer + i * 4 + (first + 2 * j)
                            slot = (first + 2 * j) % 4
                            tile = l * FT2 + i * 2 + (done + j)
                            y_tile = i * 2 + j
                            conv = probs_t[:, 0, :]
                            dve.wait_ge(gemm_done, panel_done(n))
                            v.tensor_tensor(padded[:, 2:T + 2], acc[:, slot, :], rstd[:, :], ALU.mult).then_inc(acc_free, 1)
                            dve.drain()
                            v.tensor_scalar(conv, padded[:, 0:T], par("conv_w", tile * 3), par("conv_b", tile),
                                            ALU.mult, ALU.add)
                            dve.drain()
                            v.scalar_tensor_tensor(conv, padded[:, 1:T + 1], par("conv_w", tile * 3 + 1), conv,
                                                   ALU.mult, ALU.add)
                            dve.drain()
                            v.scalar_tensor_tensor(conv, padded[:, 2:T + 2], par("conv_w", tile * 3 + 2), conv,
                                                   ALU.mult, ALU.add).then_inc(S("h_conv"), 1)
                            dve.wait_ge(S("h_gelu"), tile + 1)
                            v.tensor_tensor(probs_t[:, 1, :], probs_t[:, 1, :], rstd[:, :], ALU.mult)
                            dve.drain()
                            dve.wait_ge(gemm_done, panel_done(n + 1))
                            v.tensor_tensor(probs[:, 0, :], acc[:, (slot + 1) % 4, :], probs_t[:, 1, :],
                                            ALU.mult).then_inc(acc_free, 1)
                            dve.drain().then_inc(S("h_h"), 1)
                            low_of_tile("h", tile, probs[:, 0, :], y_hi[:, y_tile, :], y_lo[:, y_tile, :])
                    add_to_x(layer, first + 2 * tiles, (l * 3 + 5, l * 3 + 4, "ple_w", l * KD) if ch == 2 else None)
                    done += tiles
                for k in range(2):
                    dve.wait_ge(S("e_hi"), l * 2 + (k + 1))
                    v.tensor_tensor(y_lo[:, 8 + k, :], wv[:, k, :], y_hi[:, 8 + k, :],
                                    ALU.subtract).then_inc(S("e_split"), 1)
                dve.wait_ge(S("norm_rstd"), l * 3 + 6)
                settle(dve)
                evacuate(layer, N_BLOCK1 + O_GATE, 8, lambda i: wa[:, i, :], "e_g")
                dve.wait_ge(S("e_gate"), l * 8 + 8)
                for q in range(3):
                    dve.wait_ge(gemm_done, panel_done(layer + (N_BLOCK1 + O_PLE + q)))
                    w = 3 if q < 2 else 2
                    gate = wa[:, 3 * q:3 * q + w, :]
                    v.tensor_tensor(gate, gate, acc[:, 0:w, :], ALU.mult).then_inc(acc_free, 1)
                    dve.drain()
                    v.tensor_tensor(x[:, 3 * q:3 * q + w, :], x[:, 3 * q:3 * q + w, :], gate, ALU.add)
                dve.drain().then_inc(S("norm_x"), 8)
            norm(9)
            dve.wait_ge(S("norm_rstd"), 10)
            for k in range(KD):
                v.scalar_tensor_tensor(wb[:, k, :], x[:, k, :], par("final_g", k), rstd[:, :],
                                       ALU.mult, ALU.mult).then_inc(S("out_ready"), 1)

        @blk.gpsimd
        def _(pool):
            for name, start in starts.items():
                pool.sem_inc(sems[name], start)
            pool.sem_inc(started, 1)

            def low(n, slot):
                pool.wait_ge(hi_done, n + 1)
                nc.gpsimd.tensor_tensor(w_lo[:, slot, :], raw[:, slot % 2, :], w_hi[:, slot, :],
                                        ALU.subtract).then_inc(lo_done, 1)

            first = N_C + LOOK
            with pool.Fori(0, first // 4) as i:
                for j in range(4):
                    low(i * 4 + j, j)
            for n in range(first // 4 * 4, first):
                low(n, n % 4)

            with pool.Fori(0, PAIRS) as p:
                pool.wait_ge(S("b_cum"), p + 1)
                pool.wait_ge(S("b_vt"), p + 1)
                settle(pool)
                for n in range(1, len(LEVELS)):
                    h = LEVELS[n]
                    cum = cums[:, {256: 2, 128: 1}.get(h, 0), :]
                    (e0, e1), (c0, c1) = halves(exponent_tile(n), h), halves(cum, h)
                    mid = c0[:, :, h - 1:h].broadcast_to([P, T // (2 * h), h])
                    pool.wait_ge(S("b_x", 1), p * 9 + (max(n - 2, 0) + 1))
                    settle(pool)
                    nc.gpsimd.tensor_tensor(e0, mid, c0, ALU.subtract)
                    if h >= 64:
                        nc.gpsimd.tensor_copy(e1, c1)
                    else:
                        nc.gpsimd.tensor_tensor(e1, c1, mid, ALU.subtract)
                    pool.drain().then_inc(S("b_d"), 1)

            with pool.Fori(0, (N_PANELS + LOOK - first) // 4) as i:
                for j in range(4):
                    low(i * 4 + (first + j), (first + j) % 4)
            for n in range(N_PANELS + LOOK - (N_PANELS + LOOK - first) % 4, N_PANELS + LOOK):
                low(n, n % 4)


def constant_arrays():
    i = np.arange(P)
    k, q = i[:, None], i[None, :]
    table = {"ident": k == q, "anti": k + q == P - 1, "ones": np.ones((P, P)), "head_mean": (k // HD == q // HD) / HD}
    mask1 = np.where(q // CHUNK <= k // CHUNK, 0.0, MASKED)
    mask2 = np.where(q <= k, 0.0, MASKED)
    rope_c = np.zeros((P, P))
    for h in range(0, P, ROPE):
        for r in range(ROPE // 2):
            rope_c[h + ROPE // 2 + r, h + r] = -1.0
            rope_c[h + r, h + ROPE // 2 + r] = 1.0
    rope_r = np.zeros((P, P))
    for h in (0, HD):
        for r in range(HD // 2):
            rope_r[h + HD // 2 + r, h + r] = -1.0
            rope_r[h + r, h + HD // 2 + r] = 1.0
    table["mask"], table["rope"] = mask1, rope_c
    consts = np.stack([np.asarray(table[n], np.float32) for n in CONSTS], 1)
    consts2 = np.stack([mask2, rope_r], 1).astype(np.float32)
    masks = np.stack([(k // (2 * h) == q // (2 * h)) & (k % (2 * h) < h) & (q % (2 * h) >= h)
                      for h in LEVELS[3:]], 1).astype(np.float32)
    masks = np.stack([masks[:, n].reshape(P, -1, 2, h)[:, :, 1].reshape(P, -1) for n, h in enumerate(LEVELS[3:])], 1)
    freq = np.float32(10000.0) ** (-np.arange(0, HD, 2, dtype=np.float32) / np.float32(HD))
    ang = np.arange(T, dtype=np.float32)[None, :] * freq.astype(np.float32)[i % (HD // 2)][:, None]
    rotary = np.stack([np.sin(ang.astype(np.float64)), np.cos(ang.astype(np.float64))], 1).astype(np.float32)
    log_gamma = np.log1p(-(2.0 ** (-5.0 - np.arange(HEADS))))
    rel = np.arange(T)[None, :] - k
    decay = np.where(rel >= 0, HD ** -0.5 * np.exp(log_gamma[:, None, None] * np.maximum(rel, 0)), 0.0)
    decay = decay.reshape(PAIRS, 2, P, T).transpose(0, 2, 1, 3).astype(np.float32)
    inv_freq = np.tile(np.float32(10000.0) ** (-np.arange(0, ROPE, 2, dtype=np.float32) / np.float32(ROPE)),
                       2 * P // ROPE)[:, None]
    return {"consts": consts, "consts2": consts2, "masks": masks, "rotary": rotary, "decay": decay}, inv_freq


def columns(a, rows=P):
    return np.moveaxis(a.reshape(*a.shape[:-1], -1, rows), -1, 0).reshape(rows, -1)


def feature_panels(w, width=P):
    k, m = w.shape[0] // P, w.shape[1] // width
    return w.reshape(k, P, m, width).transpose(2, 1, 0, 3).reshape(m, P, k * width)


def in_turns(*parts):
    return np.stack(parts, 1).reshape(-1, *parts[0].shape[1:])


def padded_columns(w, first):
    out = np.zeros((w.shape[0], P), w.dtype)
    out[:, first:first + w.shape[1]] = w
    return out


def lay_out(a):
    arrays, inv_freq = constant_arrays()
    f = lambda v: np.asarray(v)
    w = f(a["w_in"])[0]
    s = np.cumsum([0, 512, 512, 512, 512, 512, 512, 512, QR, KVR, ROPE, 3 * D])
    aq, ak, av, bq, bf, bi, bg, cq, ckv, ckr, gates = (w[:, s[i]:s[i + 1]] for i in range(11))
    cat = np.concatenate
    fp = feature_panels
    arrays["w_in1"] = cat([fp(aq), fp(ak), fp(av), in_turns(fp(bq), fp(bf), fp(bi), fp(bg)), fp(cq), fp(ckv),
                           fp(padded_columns(ckr, NOPE))])
    uq = f(a["mla_w_uq"])[0].reshape(QR, HEADS, QH)
    arrays["w_c_qn"] = fp(uq[:, :, :NOPE].reshape(QR, 512)).transpose(1, 0, 2).reshape(1, P, 1024)
    arrays["w_c_qr"] = fp(uq[:, :, NOPE:].reshape(QR, 256)).transpose(1, 0, 2).reshape(1, P, 512)
    ukv = f(a["mla_w_ukv"])[0].reshape(KVR, HEADS, 2, HD)
    arrays["w_c_kv"] = np.stack([ukv[:, :, 0].reshape(P, 512), ukv[:, :, 1].reshape(P, 512)])
    gate = fp(gates).reshape(3, KD, P, 1024)
    branch = [fp(f(a["w_branch"])[0, b]) for b in range(3)]
    arrays["w_gate"], arrays["w_branch"] = (cat([in_turns(w[0], w[1]), w[2]]) for w in (gate, branch))
    ff1 = feature_panels(f(a["w_ff1"])[0]).reshape(4, 8, P, 1024)
    ff2 = np.stack([feature_panels(part) for part in f(a["w_ff2"])[0].reshape(4, D, D)])
    arrays["w_rest1"] = cat([feature_panels(f(a["w_out"])[0]), cat([ff1, ff2], 1).reshape(64, P, 1024)])
    layers = {n: [] for n in SEGMENTS2}
    for l in range(LAYERS):
        w = f(a["w_in_2"])[l]
        s = np.cumsum([0, 512, 512, 512, HEADS, 512, 512, 512, 512])
        fq, fk, fv, fl, rq, rk, rv, rg = (w[:, s[i]:s[i + 1]] for i in range(8))
        up, down = f(a["w_up_2"])[l], f(a["w_down_2"])[l]
        both = np.stack([feature_panels(up[:, :FF2]), feature_panels(up[:, FF2:])], 1)
        wide, narrow, at = [], [], 0
        for tiles in CHUNKS2:
            part = [both[at:at + tiles].reshape(-1, P, 1024), feature_panels(down[at * P:(at + tiles) * P])]
            if tiles == 8:
                wide += part
            else:
                wide.append(part[0])
                narrow.append(part[1])
            at += tiles
        layers["in2"].append(cat([fp(padded_columns(fl, 0)), fp(fq), fp(fk), fp(fv),
                                  in_turns(fp(rq), fp(rk), fp(rv), fp(rg)), fp(f(a["w_out_2"])[l])]))
        layers["ffn_wide"].append(cat(wide))
        layers["ffn_narrow"].append(cat(narrow))
        layers["ple_gate"].append(feature_panels(f(a["w_ple_gate_2"])[l]))
        proj = feature_panels(f(a["w_ple_proj_2"])[l])
        layers["ple_a"].append(proj[0:6].reshape(2, 3, P, 256).transpose(0, 2, 1, 3).reshape(2, P, 768))
        layers["ple_b"].append(proj[6:8].transpose(1, 0, 2).reshape(1, P, 512))
    for n, parts in layers.items():
        arrays["w_" + n] = np.stack(parts)
    r = f(a["rel_bias"])[0][:, ::-1]
    ext = r[:, np.clip(np.arange(640) - (T - 1) + A_REL, 0, 2 * A_REL)]
    arrays["bias"] = ext
    arrays["x"] = f(a["x"])[0].T.reshape(KD, P, T).transpose(1, 0, 2)
    arrays["p"] = f(a["p_2"])[:, 0].transpose(0, 2, 1).reshape(LAYERS, 2, P, T).transpose(0, 2, 1, 3)
    arrays["positions"] = f(a["positions"])[0]
    one = np.ones((P, 1), np.float32)
    bias8 = np.zeros((P, LAYERS), np.float32)
    bias8[:HEADS] = f(a["forget_bias_2"]).T
    conv_w = f(a["conv_w_2"]).reshape(LAYERS, 3, FT2, P).transpose(3, 0, 2, 1).reshape(P, -1)
    parts = {"one": one, "eps": one * np.float32(EPS), "gn_eps": one * np.float32(GN_EPS), "inv_freq": inv_freq,
             "mix_g": columns(f(a["norm_mix_g"])), "ffn_g": columns(f(a["norm_ffn_g"])),
             "q_g": columns(f(a["mla_q_norm_g"])), "kv_g": columns(f(a["mla_kv_norm_g"])),
             "hgrn_g": cat([f(a["hgrn_norm_g"])[0]] * 2)[:, None], "lb": columns(f(a["hgrn_lb_logits"])),
             "mid_g": columns(f(a["final_norm_g"])), "final_g": columns(f(a["final_norm_w_2"])), "attn_w": columns(f(a["attn_norm_w_2"])),
             "ffn_w": columns(f(a["ffn_norm_w_2"])), "ple_w": columns(f(a["ple_norm_w_2"])), "f_bias": bias8,
             "conv_b": columns(f(a["conv_b_2"])), "conv_w": conv_w}
    arrays["params"] = cat([parts[n] for n in PARAMS], 1)
    return {n: np.ascontiguousarray(v) for n, v in arrays.items()}


def program(nc, arrays):
    dram = {}
    for n, v in arrays.items():
        dram[n] = nc.dram_tensor("in_" + n, v.shape, mybir.dt.from_np(v.dtype), kind="ExternalInput").ap()
    ext = dram["bias"]
    dram["bias"] = BiasWindows(ext)
    out = nc.dram_tensor("out", (D, T), F32, kind="ExternalOutput").ap()
    build(nc, dram, out)


class BiasWindows:

    def __init__(self, ext):
        self.ext = ext

    def __getitem__(self, pair):
        rows = self.ext[bass.ds(pair * 2, 2), 0:T]
        return bass.AP(rows.tensor, rows.offset, [[1, P], [640, 2], [1, T]])


def kernel(**inputs):
    import concourse.bacc as bacc
    from concourse.bass_utils import run_bass_kernel_spmd

    arrays = lay_out(inputs)
    nc = bacc.Bacc("TRN2", target_bir_lowering=False, num_devices=1)
    program(nc, arrays)
    r = run_bass_kernel_spmd(nc, [{"in_" + n: v for n, v in arrays.items()}], core_ids=[0])
    return r.results[0]["out"].T.reshape(1, T, D)
```
